# Optimizing a Trainium2 kernel written in Bass

```python
import jax, jax.numpy as jnp
from jax import lax
import numpy as np

D_MODEL = 2048
BATCH = 1
SEQ = 512
DEPTH = 1
DEC_BATCH = 1
DEC_SEQ = 64
PAST_LEN = 256

CHUNK = 64
RMS_EPS = 1e-6
ROPE_BASE = 10000.0
MIX_WIDTH = D_MODEL
RET_WIDTH = MIX_WIDTH // 2
RET_HEADS = 8
RET_DV = RET_WIDTH // RET_HEADS
RET_DK = RET_DV
MLSTM_WIDTH = MIX_WIDTH - RET_WIDTH
MLSTM_HEADS = 4
MLSTM_DV = MLSTM_WIDTH // MLSTM_HEADS
MLSTM_DK = MLSTM_DV // 2
IN_SIZES = (RET_HEADS * RET_DK, RET_HEADS * RET_DK, RET_WIDTH, RET_WIDTH,
            MLSTM_HEADS * MLSTM_DK, MLSTM_HEADS * MLSTM_DK, MLSTM_WIDTH, MLSTM_WIDTH,
            MLSTM_HEADS, MLSTM_HEADS)
IN_COLS = sum(IN_SIZES)
PEER_HEADS = 8
PEER_QDIM = 256
N_KEYS = 128
N_EXPERTS = N_KEYS * N_KEYS
PEER_TOPK = 16
EXPERT_BLOCK = 128
PLE_DIM = 256

kernel_name = 'hymba_retention_mlstm_peer_stream_step'

def _rmsnorm(x, g):
    x32 = x.astype(jnp.float32)
    y = x32 * lax.rsqrt(jnp.mean(x32 * x32, axis=-1, keepdims=True) + RMS_EPS)
    return (y * g.astype(jnp.float32)).astype(x.dtype)

def _head_norm(o, g):
    n_heads, d = o.shape[1], o.shape[3]
    y = o * lax.rsqrt(jnp.mean(o * o, axis=-1, keepdims=True) + RMS_EPS)
    return y * g.astype(jnp.float32).reshape(1, n_heads, 1, d)

def _rope(x, pos):
    half = x.shape[-1] // 2
    inv = ROPE_BASE ** (-jnp.arange(half, dtype=jnp.float32) / half)
    ang = pos[:, None] * inv[None, :]
    cos, sin = jnp.cos(ang), jnp.sin(ang)
    x1, x2 = x[..., :half], x[..., half:]
    return jnp.concatenate([x1 * cos - x2 * sin, x1 * sin + x2 * cos], axis=-1)

def _split_heads(t, n_heads):
    b, l, _ = t.shape
    return t.reshape(b, l, n_heads, -1).transpose(0, 2, 1, 3)

def _to_chunks(t, cl):
    b, h, l = t.shape[:3]
    t = t.reshape((b, h, l // cl, cl) + t.shape[3:])
    return jnp.moveaxis(t, 2, 0)

def _from_chunks(t):
    nc, b, h, cl = t.shape[:4]
    t = jnp.moveaxis(t, 0, 2)
    return t.reshape((b, h, nc * cl) + t.shape[4:])

def _in_offsets():
    return [int(o) for o in np.cumsum(np.array(IN_SIZES))[:-1]]

def _retention_chunk(S, q, k, v, log_gamma):
    L = q.shape[2]
    pos = jnp.arange(L, dtype=jnp.float32)
    diff = pos[:, None] - pos[None, :]
    causal = diff >= 0
    decay = jnp.where(causal[None], jnp.exp(jnp.where(causal, diff, 0.0)[None] * log_gamma[:, None, None]), 0.0)
    scores = jnp.einsum('bhld,bhmd->bhlm', q, k) * decay[None]
    q_dec = q * jnp.exp((pos[None, :] + 1.0) * log_gamma[:, None])[None, :, :, None]
    k_dec = k * jnp.exp((L - 1.0 - pos[None, :]) * log_gamma[:, None])[None, :, :, None]
    o = jnp.einsum('bhlm,bhmv->bhlv', scores, v) + jnp.einsum('bhld,bhdv->bhlv', q_dec, S)
    S_new = jnp.exp(L * log_gamma)[None, :, None, None] * S + jnp.einsum('bhmd,bhmv->bhdv', k_dec, v)
    return o, S_new

def _mlstm_chunk(C, n, m, q, k, v, ig, fg):
    L = q.shape[2]
    b = jnp.cumsum(jax.nn.log_sigmoid(fg), axis=-1)
    causal = jnp.tril(jnp.ones((L, L), dtype=bool))
    dlog = jnp.where(causal, b[..., :, None] - b[..., None, :] + ig[..., None, :], -jnp.inf)
    inter_log = b + m[..., None]
    m_t = jnp.maximum(inter_log, jnp.max(dlog, axis=-1))
    dw = jnp.exp(dlog - m_t[..., None])
    inter_w = jnp.exp(inter_log - m_t)
    sm = jnp.einsum('bhld,bhsd->bhls', q, k) * dw
    num = jnp.einsum('bhls,bhsv->bhlv', sm, v) + inter_w[..., None] * jnp.einsum('bhld,bhdv->bhlv', q, C)
    den = jnp.sum(sm, axis=-1) + inter_w * jnp.einsum('bhld,bhd->bhl', q, n)
    h = num / jnp.maximum(jnp.abs(den), jnp.exp(-m_t))[..., None]
    m_new = m_t[..., -1]
    ws = jnp.exp(b[..., -1:] - b + ig - m_new[..., None])
    carry_decay = jnp.exp(b[..., -1] + m - m_new)
    C_new = carry_decay[..., None, None] * C + jnp.einsum('bhs,bhsd,bhsv->bhdv', ws, k, v)
    n_new = carry_decay[..., None] * n + jnp.einsum('bhs,bhsd->bhd', ws, k)
    return h, C_new, n_new, m_new

def _token_mixers(a, pos, S0, C0, n0, m0, w_in, b_gates, g_ret, g_ml, w_out):
    f32 = jnp.float32
    B, L, _ = a.shape
    z = a @ w_in
    rq, rk, rv, rg, mq, mk, mv, mo, mi, mf = jnp.split(z, _in_offsets(), axis=-1)
    rq = _rope(_split_heads(rq, RET_HEADS).astype(f32), pos)
    rk = _rope(_split_heads(rk, RET_HEADS).astype(f32), pos) * (RET_DK ** -0.5)
    rv = _split_heads(rv, RET_HEADS).astype(f32)
    mq = _split_heads(mq, MLSTM_HEADS).astype(f32)
    mk = _split_heads(mk, MLSTM_HEADS).astype(f32) * (MLSTM_DK ** -0.5)
    mv = _split_heads(mv, MLSTM_HEADS).astype(f32)
    gates = (jnp.concatenate([mi, mf], axis=-1).astype(f32) + b_gates.astype(f32)).transpose(0, 2, 1)
    ig, fg = gates[:, :MLSTM_HEADS], gates[:, MLSTM_HEADS:]
    cl = min(CHUNK, L)
    xs = tuple(_to_chunks(t, cl) for t in (rq, rk, rv, mq, mk, mv, ig, fg))
    log_gamma = jnp.log(1.0 - jnp.power(2.0, -5.0 - jnp.arange(RET_HEADS, dtype=f32)))

    def body(carry, xc):
        S, C, n, m = carry
        qr, kr, vr, qm, km, vm, igc, fgc = xc
        o_r, S = _retention_chunk(S, qr, kr, vr, log_gamma)
        o_m, C, n, m = _mlstm_chunk(C, n, m, qm, km, vm, igc, fgc)
        return (S, C, n, m), (o_r, o_m)

    carry0 = (S0.astype(f32), C0.astype(f32), n0.astype(f32), m0.astype(f32))
    (S, C, n, m), (o_r, o_m) = lax.scan(body, carry0, xs)
    o_r = _from_chunks(o_r)
    o_m = _from_chunks(o_m)
    ret = _head_norm(o_r, g_ret).transpose(0, 2, 1, 3).reshape(B, L, RET_WIDTH) * jax.nn.silu(rg.astype(f32))
    mls = _head_norm(o_m, g_ml).transpose(0, 2, 1, 3).reshape(B, L, MLSTM_WIDTH) * jax.nn.sigmoid(mo.astype(f32))
    mix = jnp.concatenate([ret, mls], axis=-1).astype(a.dtype) @ w_out
    return mix, S, C, n, m

def _peer(c, w_q, keys1, keys2, u, v):
    f32 = jnp.float32
    B, L, D = c.shape
    T = B * L
    ct = c.reshape(T, D)
    q = (ct @ w_q).reshape(T, PEER_HEADS, PEER_QDIM).astype(f32)
    half = PEER_QDIM // 2
    s1 = jnp.einsum('thd,kd->thk', q[..., :half], keys1.astype(f32))
    s2 = jnp.einsum('thd,kd->thk', q[..., half:], keys2.astype(f32))
    t1, i1 = lax.top_k(s1, PEER_TOPK)
    t2, i2 = lax.top_k(s2, PEER_TOPK)
    cand = (t1[..., :, None] + t2[..., None, :]).reshape(T, PEER_HEADS, PEER_TOPK * PEER_TOPK)
    cidx = (i1[..., :, None] * N_KEYS + i2[..., None, :]).reshape(T, PEER_HEADS, PEER_TOPK * PEER_TOPK)
    sc, sel = lax.top_k(cand, PEER_TOPK)
    eidx = jnp.take_along_axis(cidx, sel, axis=-1).reshape(T, PEER_HEADS * PEER_TOPK)
    gate = jax.nn.softmax(sc, axis=-1).reshape(T, PEER_HEADS * PEER_TOPK).astype(c.dtype)
    n_blk = -(-T // EXPERT_BLOCK)
    pad = n_blk * EXPERT_BLOCK - T
    cb = jnp.pad(ct, ((0, pad), (0, 0))).reshape(n_blk, EXPERT_BLOCK, D)
    ib = jnp.pad(eidx, ((0, pad), (0, 0))).reshape(n_blk, EXPERT_BLOCK, PEER_HEADS * PEER_TOPK)
    gb = jnp.pad(gate, ((0, pad), (0, 0))).reshape(n_blk, EXPERT_BLOCK, PEER_HEADS * PEER_TOPK)

    def expert_block(args):
        xb, idx, g = args
        act = jax.nn.gelu(jnp.einsum('td,tkd->tk', xb, u[idx]), approximate=False)
        return jnp.einsum('tk,tkd->td', g * act, v[idx])

    out = lax.map(expert_block, (cb, ib, gb)).reshape(n_blk * EXPERT_BLOCK, D)[:T]
    return out.reshape(B, L, D)

def _trunk(x, p, pos, st_ret, st_C, st_n, st_m, g_mix, w_in, b_gates, g_ret, g_mlstm, w_out, g_ffn,
           w_peer_q, peer_keys1, peer_keys2, peer_u, peer_v, g_ple, w_ple_gate, w_ple_proj, g_final):
    h = x
    Ss, Cs, ns, ms = [], [], [], []
    for i in range(DEPTH):
        mix, S, C, n, m = _token_mixers(_rmsnorm(h, g_mix[i]), pos, st_ret[i], st_C[i], st_n[i], st_m[i],
                                        w_in[i], b_gates[i], g_ret[i], g_mlstm[i], w_out[i])
        h = h + mix
        h = h + _peer(_rmsnorm(h, g_ffn[i]), w_peer_q[i], peer_keys1[i], peer_keys2[i], peer_u[i], peer_v[i])
        e = _rmsnorm(h, g_ple[i])
        h = h + jax.nn.sigmoid(e @ w_ple_gate[i]) * (p[i].astype(h.dtype) @ w_ple_proj[i])
        Ss.append(S)
        Cs.append(C)
        ns.append(n)
        ms.append(m)
    y = _rmsnorm(h, g_final)
    return y, jnp.stack(Ss), jnp.stack(Cs), jnp.stack(ns), jnp.stack(ms)

def setup_inputs(seed: int = 0) -> dict:
    key = jax.random.key(seed)
    ks = jax.random.split(key, 32)

    def nrm(k, shape, scale):
        return scale * jax.random.normal(k, shape, jnp.float32)

    b_gates = jnp.concatenate([
        nrm(ks[10], (DEPTH, MLSTM_HEADS), 0.1),
        jnp.linspace(3.0, 6.0, MLSTM_HEADS, dtype=jnp.float32)[None, :] + nrm(ks[11], (DEPTH, MLSTM_HEADS), 0.1)],
        axis=-1)
    return {
        'x_prompt': nrm(ks[0], (BATCH, SEQ, D_MODEL), 1.0),
        'x_sample': nrm(ks[1], (DEC_BATCH, DEC_SEQ, D_MODEL), 1.0),
        'p_prompt': nrm(ks[2], (DEPTH, BATCH, SEQ, PLE_DIM), 1.0),
        'p_sample': nrm(ks[3], (DEPTH, DEC_BATCH, DEC_SEQ, PLE_DIM), 1.0),
        'state_ret': nrm(ks[4], (DEPTH, DEC_BATCH, RET_HEADS, RET_DK, RET_DV), 1.0),
        'state_mlstm_C': nrm(ks[5], (DEPTH, DEC_BATCH, MLSTM_HEADS, MLSTM_DK, MLSTM_DV), 0.5),
        'state_mlstm_n': nrm(ks[6], (DEPTH, DEC_BATCH, MLSTM_HEADS, MLSTM_DK), 0.5),
        'state_mlstm_m': nrm(ks[7], (DEPTH, DEC_BATCH, MLSTM_HEADS), 1.0),
        'g_mix': 1.0 + nrm(ks[8], (DEPTH, D_MODEL), 0.05),
        'w_in': nrm(ks[9], (DEPTH, D_MODEL, IN_COLS), D_MODEL ** -0.5),
        'b_gates': b_gates,
        'g_ret': 1.0 + nrm(ks[12], (DEPTH, RET_WIDTH), 0.05),
        'g_mlstm': 1.0 + nrm(ks[13], (DEPTH, MLSTM_WIDTH), 0.05),
        'w_out': nrm(ks[14], (DEPTH, MIX_WIDTH, D_MODEL), MIX_WIDTH ** -0.5),
        'g_ffn': 1.0 + nrm(ks[15], (DEPTH, D_MODEL), 0.05),
        'w_peer_q': nrm(ks[16], (DEPTH, D_MODEL, PEER_HEADS * PEER_QDIM), D_MODEL ** -0.5),
        'peer_keys1': nrm(ks[17], (DEPTH, N_KEYS, PEER_QDIM // 2), (PEER_QDIM // 2) ** -0.5),
        'peer_keys2': nrm(ks[18], (DEPTH, N_KEYS, PEER_QDIM // 2), (PEER_QDIM // 2) ** -0.5),
        'peer_u': nrm(ks[19], (DEPTH, N_EXPERTS, D_MODEL), D_MODEL ** -0.5),
        'peer_v': nrm(ks[20], (DEPTH, N_EXPERTS, D_MODEL), 0.5),
        'g_ple': 1.0 + nrm(ks[21], (DEPTH, D_MODEL), 0.05),
        'w_ple_gate': nrm(ks[22], (DEPTH, D_MODEL, D_MODEL), D_MODEL ** -0.5),
        'w_ple_proj': nrm(ks[23], (DEPTH, PLE_DIM, D_MODEL), PLE_DIM ** -0.5),
        'g_final': 1.0 + nrm(ks[24], (D_MODEL,), 0.05),
    }

def reference(x_prompt, x_sample, p_prompt, p_sample, state_ret, state_mlstm_C, state_mlstm_n, state_mlstm_m,
              g_mix, w_in, b_gates, g_ret, g_mlstm, w_out, g_ffn, w_peer_q, peer_keys1, peer_keys2,
              peer_u, peer_v, g_ple, w_ple_gate, w_ple_proj, g_final):
    f32 = jnp.float32
    bp = x_prompt.shape[0]
    z_ret = jnp.zeros((DEPTH, bp, RET_HEADS, RET_DK, RET_DV), f32)
    z_C = jnp.zeros((DEPTH, bp, MLSTM_HEADS, MLSTM_DK, MLSTM_DV), f32)
    z_n = jnp.zeros((DEPTH, bp, MLSTM_HEADS, MLSTM_DK), f32)
    z_m = jnp.zeros((DEPTH, bp, MLSTM_HEADS), f32)
    pos_prompt = jnp.arange(x_prompt.shape[1], dtype=f32)
    pos_sample = PAST_LEN + jnp.arange(x_sample.shape[1], dtype=f32)
    y_prompt, ret_p, C_p, n_p, m_p = _trunk(
        x_prompt, p_prompt, pos_prompt, z_ret, z_C, z_n, z_m, g_mix, w_in, b_gates, g_ret, g_mlstm, w_out,
        g_ffn, w_peer_q, peer_keys1, peer_keys2, peer_u, peer_v, g_ple, w_ple_gate, w_ple_proj, g_final)
    y_sample, ret_s, C_s, n_s, m_s = _trunk(
        x_sample, p_sample, pos_sample, state_ret, state_mlstm_C, state_mlstm_n, state_mlstm_m, g_mix, w_in,
        b_gates, g_ret, g_mlstm, w_out, g_ffn, w_peer_q, peer_keys1, peer_keys2, peer_u, peer_v, g_ple,
        w_ple_gate, w_ple_proj, g_final)
    return (y_prompt, y_sample, ret_p, C_p, n_p, m_p, ret_s, C_s, n_s, m_s)


_drawn_inputs = setup_inputs


def setup_inputs(seed=0):
    import zlib

    import numpy as np

    out = dict(_drawn_inputs(seed))
    spreads = {}
    factors = {'g_ple': 6.676}
    for name, (base, spread) in spreads.items():
        noise = np.random.default_rng([zlib.crc32(name.encode()), seed]).standard_normal(out[name].shape)
        drawn = base * np.exp(spread * noise) if base else spread * noise
        out[name] = __import__('jax').numpy.asarray(drawn.astype(out[name].dtype))
    for name, factor in factors.items():
        out[name] = (out[name] * factor).astype(out[name].dtype)
    return out
```

```python
from contextlib import ExitStack

import numpy as np

import concourse.bass as bass
from concourse import mybir

F32 = mybir.dt.float32
U32 = mybir.dt.uint32
ALU = mybir.AluOpType
ACT = mybir.ActivationFunctionType
AX_X = mybir.AxisListType.X

P = 128
D = 2048
KT = D // P
PROMPT, SAMPLE = 512, 64
NB = PROMPT // P + 1
SB = NB - 1
T = NB * P
PAST = 256
EPS = 1e-6
RH, RD = 8, 128
MH, MK, MV = 4, 128, 256
RW, MW = RH * RD, MH * MV
ZC = 4 * RW + 2 * MH * MK + 2 * MW
Z_RQ, Z_RK, Z_RV, Z_RG = 0, RW, 2 * RW, 3 * RW
Z_MQ = 4 * RW
Z_MK = Z_MQ + MH * MK
Z_MV = Z_MK + MH * MK
Z_MO = Z_MV + MW
CG = 512
ZG = ZC // CG
DG = D // CG
EH, EQ, NKEY, TOPK = 8, 256, 128, 16
HH = 2 * EH
NE = NKEY * NKEY
NPICK = EH * TOPK
PLE = 256
GRP = 8
PAIR_ROWS = [(0, 1, 16), (1, 1, 8), (2, 1, 5), (3, 1, 4), (4, 1, 3), (5, 3, 2), (8, 8, 1)]
NC = sum(n * w for _, n, w in PAIR_ROWS)
LOWEST = -3.0e38
FAR = 1.0e30


def constants():
    half = RD // 2
    inv = np.float32(10000.0) ** (-np.arange(half, dtype=np.float32) / np.float32(half))
    pos = np.concatenate([np.arange(PROMPT), PAST + np.arange(SAMPLE), PAST + np.arange(SAMPLE)]).astype(np.float32)
    ang = (pos[:, None] * inv[None, :]).astype(np.float32)
    rope = np.stack([np.cos(ang), np.sin(ang)], 1).astype(np.float32)
    rope = rope.reshape(NB, P, 2 * half).transpose(1, 0, 2).reshape(P, NB * 2 * half)
    lg = np.log(1.0 - 2.0 ** (-5.0 - np.arange(RH)))
    scale = RD ** -0.5
    i = np.arange(P)
    tabs = []
    for n in (P, SAMPLE):
        diff = i[None, :] - i[:, None]
        keep = (diff >= 0) & (i[:, None] < n)
        dec = np.where(keep[:, None, :], np.exp(np.where(keep, diff, 0)[:, None, :] * lg[None, :, None]), 0) * scale
        kd = np.where(i[:, None] < n, np.exp((n - 1.0 - np.minimum(i, n - 1))[:, None] * lg[None, :]), 0) * scale
        gl = np.broadcast_to(np.exp(n * lg)[None, :], (P, RH))
        tabs.append(np.concatenate([dec.reshape(P, RH * P), kd, gl], 1))
    qd = np.exp((i[None, :] + 1.0) * lg[:, None]).reshape(1, RH * P)
    far = np.where(i[:, None] <= i[None, :], 0.0, FAR)
    ident = np.eye(P)
    fold = (i[:, None] % SAMPLE == i[None, :] % SAMPLE)
    sel = np.zeros((P, MH, P))
    for h in range(MH):
        sel[h, h] = 1.0
    row = np.concatenate([far, ident, fold.astype(float), sel.reshape(P, MH * P), np.broadcast_to(np.arange(NC), (P, NC))], 1)
    return {
        "c_rope": rope,
        "c_decay": np.stack(tabs).astype(np.float32),
        "c_qdecay": np.broadcast_to(qd, (P, RH * P)).astype(np.float32).copy(),
        "c_misc": row.astype(np.float32),
    }


class Gate:

    def __init__(self, nc, eng, name):
        self.eng, self.sem = eng, nc.alloc_semaphore(name)

    def close(self):
        self.eng.sem_inc(self.sem, 1)


class Chain:

    def __init__(self, eng, sem):
        self.eng, self.sem, self.n, self.off = eng, sem, 0, 0

    def then_wait(self, ins):
        self.n += 1
        ins.then_inc(self.sem, 1)
        self.eng.wait_ge(self.sem, self.off + self.n)


def build(nc, a, out):
    with ExitStack() as ctx:
        def sb(name, shape, dt=F32):
            return ctx.enter_context(nc.sbuf_tensor(name, shape, dt))

        actT = sb("actT", [P, KT, T])
        hbuf = sb("hbuf", [P, NB * D])
        wbuf = sb("wbuf", [P, 2 * KT * CG])
        gain = sb("gain", [P, D])
        xn = sb("xn", [P, 2, D])
        stage = sb("stage", [P, NB * CG])
        misc = sb("misc", [P, 3 * P + MH * P + NC])
        stat = sb("stat", [P, 80])
        cols = sb("cols", [P, NB, 4, MH])
        cdbc = sb("cdbc", [P, NB, MH])
        mrows = sb("mrows", [MH, T])
        psum = ctx.enter_context(nc.psum_tensor("psum", [P, 8, 512], F32))

        h = hbuf[:, :].rearrange("p (b d) -> p b d", b=NB)
        W = wbuf[:, :].rearrange("p (s k c) -> p s k c", s=2, k=KT)
        far = misc[:, 0:P]
        ident = misc[:, P:2 * P]
        fold = misc[:, 2 * P:3 * P]
        sel = misc[:, 3 * P:3 * P + MH * P].rearrange("p (h q) -> p h q", h=MH)
        iota = misc[:, 3 * P + MH * P:]

        zd = nc.dram_tensor("z_scratch", (NB, P, ZC), F32, kind="Internal").ap()

        def bank(n, width=512, banks=1):
            v = psum[:, n:n + banks, :].rearrange("p b c -> p (b c)")
            return v[:, 0:width]

        def row_bcast(ap1d):
            return ap1d.rearrange("(o d) -> o d", o=1).to_broadcast([P, ap1d.shape[0]])

        def load_x(eng, sem):
            for b in range(SB):
                eng.dma_start(h[:, b, :], a["x_prompt"][0, b * P:(b + 1) * P, :]).then_inc(sem, 16)
            for c in range(2):
                eng.dma_start(h[c * SAMPLE:(c + 1) * SAMPLE, SB, :], a["x_sample"][0]).then_inc(sem, 16)

        norm_transpose = make_norm_transpose(nc, h, gain, xn, stage, stat, ident, actT, bank)

        x_in, misc_in = nc.alloc_semaphore("x_in"), nc.alloc_semaphore("misc_in")
        with nc.Block() as block:
            def loads(sp, gin):
                sp.dma_start(misc[:, :], a["c_misc"]).then_inc(misc_in, 16)
                sp.dma_start(gain[:, :], row_bcast(a["g_mix"][0])).then_inc(gin, 16)
                load_x(sp, x_in)
            norm_transpose(block, 0, loads, x_in, misc_in)

        project(nc, a, out, actT, W, stage, misc, sel, ident, cols, cdbc, mrows, gain, xn, bank, zd)
        mixers(nc, a, out, actT, hbuf, wbuf, gain, xn, stage, stat, far, ident, sel, cols, cdbc, mrows, bank, zd)

        with ExitStack() as s:
            sem = lambda name: nc.alloc_semaphore(name)
            w_in = [sem("o_w0"), sem("o_w1")]
            mm, added = sem("o_mm"), sem("o_added")
            with nc.Block() as block:
                @block.sync
                def _(sp):
                    load_x(sp, x_in)
                    weight_groups(sp, W, a["w_out"][0], DG, w_in, mm)

                @block.tensor
                def _(pe):
                    product_groups(pe, actT, W, bank, DG, w_in, mm, added)

                @block.vector
                def _(dve):
                    dve.wait_ge(x_in, 32 * (NB + 1))
                    with dve.Fori(0, DG) as g:
                        for b in range(NB):
                            dve.wait_ge(mm, g * NB + (b + 1))
                            hc = h[:, b, bass.ds(g * CG, CG)]
                            dve.tensor_tensor(hc, bank(b), hc, ALU.add).then_inc(added, 1)

        with nc.Block() as block:
            def loads(sp, gin):
                sp.dma_start(gain[:, :], row_bcast(a["g_ffn"][0])).then_inc(gin, 16)
            norm_transpose(block, 1, loads)

        experts(nc, a, h, actT, wbuf, W, gain, xn, stage, stat, ident, fold, iota, bank)

        with nc.Block() as block:
            def loads(sp, gin):
                sp.dma_start(gain[:, :], row_bcast(a["g_ple"][0])).then_inc(gin, 16)
            norm_transpose(block, 2, loads)

        embeddings(nc, a, out, h, actT, W, gain, xn, stage, stat, ident, bank, row_bcast)


def make_norm_transpose(nc, h, gain, xn, stage, stat, ident, actT, bank):
    squared, mean, rooted, normed, turned, copied_a, copied_v, chain, gin = (
        nc.alloc_semaphore("n_" + x) for x in
        ("squared", "mean", "rooted", "normed", "turned", "copied_a", "copied_v", "dve", "gain"))
    ssq, ms, rt, rs = (stat[:, 2 * i:2 * i + 2] for i in range(4))
    junk = stage[:, 0:D]

    def blk(b):
        return h[:, b, :] if isinstance(b, int) else h[:, bass.ds(b, 1), :].rearrange("p o d -> p (o d)")

    def blocks(eng, body):
        body(0, 0, True)
        with eng.Fori(0, (NB - 1) // 2) as i:
            for r in (1, 0):
                body(2 * i + (2 - r), r, False)

    def run(block, use, loads, inputs=None, cin=None):
        u = NB * use

        @block.sync
        def _(sp):
            loads(sp, gin)

        @block.scalar
        def _(act):
            def body(b, r, first):
                if inputs is not None:
                    act.wait_ge(inputs, 16 * (NB + 1))
                if not (first and use == 0):
                    act.wait_ge(squared, b + u)
                    act.wait_ge(mean, b + u)
                act.activation(junk, blk(b), ACT.Square, accum_out=ssq[:, r:r + 1]).then_inc(squared, 1)
                act.wait_ge(mean, b + (u + 1))
                act.activation(rt[:, r:r + 1], ms[:, r:r + 1], ACT.Sqrt).then_inc(rooted, 1)
                for q in range(2):
                    act.wait_ge(turned, 4 * b + (4 * u + q + 1))
                    act.copy(actT[:, 4 * q:4 * q + 4, bass.ds(b * P, P)], bank(4 * r + q)).then_inc(copied_a, 1)
            blocks(act, body)

        @block.vector
        def _(dve):
            ch = Chain(dve, chain)
            dve.wait_ge(gin, 16 * (use + 1))

            def body(b, r, first):
                ch.n, ch.off = 0, b + u
                dve.wait_ge(squared, b + (u + 1))
                dve.tensor_scalar(ms[:, r:r + 1], ssq[:, r:r + 1], 1.0 / D, EPS, ALU.mult, ALU.add).then_inc(mean, 1)
                dve.wait_ge(rooted, b + (u + 1))
                ch.then_wait(dve.reciprocal(rs[:, r:r + 1], rt[:, r:r + 1]))
                if not first:
                    dve.wait_ge(turned, 4 * b + 4 * (u - 1))
                dve.scalar_tensor_tensor(out=xn[:, r, :], in0=blk(b), scalar=rs[:, r:r + 1],
                                         in1=gain[:, :], op0=ALU.mult, op1=ALU.mult).then_inc(normed, 1)
                for q in range(2, 4):
                    dve.wait_ge(turned, 4 * b + (4 * u + q + 1))
                    dve.tensor_copy(actT[:, 4 * q:4 * q + 4, bass.ds(b * P, P)], bank(4 * r + q)).then_inc(copied_v, 1)
            blocks(dve, body)

        @block.tensor
        def _(pe):
            if cin is not None:
                pe.wait_ge(cin, 16)

            def body(b, r, first):
                pe.wait_ge(normed, b + (u + 1))
                if not first:
                    pe.wait_ge(copied_a, 2 * b + 2 * (u - 1))
                    pe.wait_ge(copied_v, 2 * b + 2 * (u - 1))
                for q in range(4):
                    for j in range(4):
                        k = 4 * q + j
                        t = pe.transpose(bank(4 * r + q)[:, j * P:(j + 1) * P], xn[:, r, k * P:(k + 1) * P], ident)
                    t.then_inc(turned, 1)
            blocks(pe, body)
    return run


def weight_groups(eng, W, w, groups, w_in, mm, c0=0):
    wv = w.rearrange("(k p) c -> p k c", p=P)

    def load(g, s):
        eng.dma_start(W[:, s, :, :], wv[:, :, bass.ds(g * CG + c0, CG)]).then_inc(w_in[s], 16)
    load(0, 0)
    load(1, 1)
    with eng.Fori(1, groups // 2) as i:
        for s in range(2):
            eng.wait_ge(mm, (2 * i + (s - 1)) * NB)
            load(2 * i + s, s)


def product_groups(pe, actT, W, bank, groups, w_in, mm, taken):
    def pair(i, first):
        for s in range(2):
            pe.wait_ge(w_in[s], 16 * i + 16)
            for b in range(NB):
                if not (first and s == 0):
                    pe.wait_ge(taken, (2 * i + (s - 1)) * NB + (b + 1))
                for k in range(KT):
                    m = pe.matmul(bank(b), actT[:, k, b * P:(b + 1) * P], W[:, s, k, :],
                                  start=(k == 0), stop=(k == KT - 1))
                m.then_inc(mm, 1)
    pair(0, True)
    with pe.Fori(1, groups // 2) as i:
        pair(i, False)


def project(nc, a, out, actT, W, stage, misc, sel, ident, cols, cdbc, mrows, gain, xn, bank, zd):
    with ExitStack() as s:
        sem = lambda name: nc.alloc_semaphore("p_" + name)
        sb = lambda name, shape: s.enter_context(nc.sbuf_tensor("p_" + name, shape, F32))
        w_in = [sem("w0"), sem("w1")]
        wg_in, mm, taken = sem("wgate"), sem("mm"), sem("taken")
        stored = [sem(f"stored{b}") for b in range(NB)]
        g_mm, g_act, g_dve, bias_in = sem("gate_mm"), sem("gate_act"), sem("gate_dve"), sem("bias")
        cc_mm, cc_done, m_out = sem("cols_mm"), sem("cols_done"), sem("m_out")
        rows_ready, row_act = sem("rows_ready"), sem("row_act")
        rows_ready_a, chain = sem("rows_ready_act"), sem("dve")
        wg = sb("wg", [P, KT, 2 * MH])
        onesrow = sb("onesrow", [MH, P])
        xrow = xn[0:MH, :, :].rearrange("p a d -> p (a d)")
        ig, fg, bs, am, tmp = (xrow[:, i * T:(i + 1) * T] for i in range(5))
        mx = mrows[:, :]
        grow = gain[0:MH, :]
        ex = grow[:, 0:3 * T]
        mprev = grow[:, 3 * T:3 * T + 8]
        cde = grow[:, 3 * T + 8:3 * T + 8 + NB]
        cdd = grow[:, 3 * T + 16:3 * T + 16 + NB * MH].rearrange("p (b h) -> p b h", b=NB)
        bias = grow[:, 3 * T + 40:3 * T + 42]
        v3 = lambda ap: ap.rearrange("p (b l) -> p b l", b=NB)
        order = [SB] + list(range(SB))
        with nc.Block() as block:
            @block.sync
            def _(sp):
                sp.dma_start(wg[:, :, :], a["w_in"][0].rearrange("(k p) c -> p k c", p=P)[:, :, ZC:ZC + 2 * MH]
                             ).then_inc(wg_in, 16)
                s.enter_context(nc.allow_non_contiguous_dma(reason="a few gate parameters"))
                sp.dma_start(bias, a["b_gates"][0].rearrange("(g h) -> h g", h=MH)).then_inc(bias_in, 16)
                sp.dma_start(mprev[:, SB:SB + 1], a["state_mlstm_m"][0].rearrange("o h -> h o")).then_inc(bias_in, 16)
                weight_groups(sp, W, a["w_in"][0], ZG, w_in, mm)
                sp.wait_ge(rows_ready, 1)
                sp.dma_start(out["m_prompt"][0].rearrange("o h -> h o"), mprev[:, SB + 1:SB + 2]).then_inc(m_out, 16)
                sp.dma_start(out["m_sample"][0].rearrange("o h -> h o"), mprev[:, SB + 2:SB + 3]).then_inc(m_out, 16)
                sp.wait_ge(m_out, 32)

            @block.tensor
            def _(pe):
                pe.wait_ge(wg_in, 16)
                for g in range(2):
                    for k in range(KT):
                        pe.matmul(bank(5 + g)[0:MH, :], wg[:, k, g * MH:(g + 1) * MH], actT[:, k, 0:PROMPT],
                                  start=(k == 0), stop=(k == KT - 1))
                    for k in range(KT):
                        m = pe.matmul(bank(7 - 7 * g)[0:MH, 0:P], wg[:, k, g * MH:(g + 1) * MH],
                                      actT[:, k, PROMPT:T], start=(k == 0), stop=(k == KT - 1))
                    m.then_inc(g_mm, 1)
                pe.wait_ge(g_dve, 4)
                product_groups(pe, actT, W, bank, ZG, w_in, mm, taken)
                pe.wait_ge(rows_ready, 1)
                srcs = (am, ex[:, 0:T], ex[:, T:2 * T], ex[:, 2 * T:3 * T])
                for b in range(NB):
                    for q in range(4):
                        c = (b * 4 + q) * MH
                        pe.transpose(bank(5)[:, c:c + MH], srcs[q][:, b * P:(b + 1) * P], ident[0:MH, 0:MH])
                pe.matmul(bank(6)[:, 0:NB * MH], onesrow[:, :], cdd, start=True, stop=True).then_inc(cc_mm, 1)

            @block.scalar
            def _(act):
                act.wait_ge(rows_ready_a, 1)
                act.activation(tmp, tmp, ACT.Exp).then_inc(row_act, 1)
                act.wait_ge(row_act, 1)
                act.activation(tmp, tmp, ACT.Ln, bias=1.0).then_inc(row_act, 1)
                act.wait_ge(rows_ready_a, 2)
                act.activation(ex, ex, ACT.Exp).then_inc(row_act, 1)
                act.activation(cde, cde, ACT.Exp).then_inc(row_act, 1)

                def group(g, first):
                    for b in range(NB):
                        act.wait_ge(mm, g * NB + (b + 1))
                        if not first:
                            act.wait_ge(stored[b], g * 16)
                        act.copy(stage[:, b * CG:(b + 1) * CG], bank(b)).then_inc(taken, 1)
                        act.wait_ge(taken, g * NB + (b + 1))
                        act.dma_start(zd[b, :, bass.ds(g * CG, CG)], stage[:, b * CG:(b + 1) * CG]
                                      ).then_inc(stored[b], 16)
                group(0, True)
                with act.Fori(1, ZG) as g:
                    group(g, False)
                for b in range(NB):
                    act.wait_ge(stored[b], 16 * ZG)

            @block.vector
            def _(dve):
                ch = Chain(dve, chain)
                do = ch.then_wait
                do(dve.memset(onesrow[:, :], 1.0))
                do(dve.memset(mprev[:, 0:1], 0.0))
                dve.wait_ge(bias_in, 32)
                for g, dst in ((0, ig), (1, fg)):
                    dve.wait_ge(g_mm, g + 1)
                    for ap, src in ((dst[:, 0:PROMPT], bank(5 + g)[0:MH, :]), (dst[:, PROMPT:T], bank(7 - 7 * g)[0:MH, 0:P])):
                        dve.tensor_scalar(ap, src, bias[:, g:g + 1], None, ALU.add).then_inc(g_dve, 1)
                dve.wait_ge(g_dve, 4)
                dve.scalar_tensor_tensor(out=tmp, in0=fg, scalar=-1.0, in1=fg, op0=ALU.mult,
                                         op1=ALU.min).then_inc(rows_ready_a, 1)
                do(dve.tensor_scalar(fg, fg, 0.0, None, ALU.min))
                dve.wait_ge(row_act, 2)
                do(dve.tensor_tensor(fg, fg, tmp, ALU.subtract))
                do(dve.memset(fg[:, PROMPT + SAMPLE:T], 0.0))
                for b in range(NB):
                    do(dve.tensor_tensor_scan(bs[:, b * P:(b + 1) * P], fg[:, b * P:(b + 1) * P],
                                              fg[:, b * P:(b + 1) * P], 0.0, ALU.add, ALU.bypass))
                do(dve.tensor_tensor(am, ig, bs, ALU.subtract))
                do(dve.memset(am[:, PROMPT + SAMPLE:T], -FAR))
                for b in order:
                    am_b, mx_b = am[:, b * P:(b + 1) * P], mx[:, b * P:(b + 1) * P]
                    do(dve.tensor_tensor_scan(mx_b, am_b, am_b, mprev[:, b:b + 1], ALU.max, ALU.bypass))
                    nxt = {SB: SB + 2, SB - 1: SB + 1}.get(b, b + 1)
                    do(dve.tensor_tensor(mprev[:, nxt:nxt + 1], bs[:, (b + 1) * P - 1:(b + 1) * P],
                                         mx[:, (b + 1) * P - 1:(b + 1) * P], ALU.add))
                last = v3(mx)[:, :, P - 1:P]
                prev = mprev[:, 0:NB].rearrange("p (b o) -> p b o", o=1)
                do(dve.tensor_tensor(v3(ex[:, 0:T]), prev.to_broadcast([MH, NB, P]), v3(mx), ALU.subtract))
                do(dve.scalar_tensor_tensor(out=ex[:, T:2 * T], in0=bs, scalar=-1.0, in1=mx, op0=ALU.mult, op1=ALU.subtract))
                do(dve.tensor_tensor(v3(ex[:, 2 * T:3 * T]), v3(am), last.to_broadcast([MH, NB, P]), ALU.subtract))
                do(dve.tensor_tensor(cde.rearrange("p (b o) -> p b o", o=1), prev, last, ALU.subtract))
                dve.sem_inc(rows_ready_a, 1)
                dve.wait_ge(row_act, 4)
                for hh in range(MH):
                    do(dve.tensor_scalar(cdd[:, :, hh], cde, sel[0:MH, hh, 0:1], None, ALU.mult))
                dve.sem_inc(rows_ready, 1)
                dve.wait_ge(cc_mm, 1)
                cv = cols[:, :, :, :].rearrange("p b q h -> p (b q h)")
                dve.tensor_copy(cv, bank(5)[:, 0:NB * 4 * MH]).then_inc(cc_done, 1)
                dve.wait_ge(cc_done, 1)
                dve.tensor_scalar(cols[:, :, 3, :], cols[:, :, 3, :], MK ** -0.5, None, ALU.mult).then_inc(cc_done, 1)
                dve.tensor_copy(cdbc[:, :, :].rearrange("p b h -> p (b h)"), bank(6)[:, 0:NB * MH]).then_inc(cc_done, 1)


def mixers(nc, a, out, actT, hbuf, wbuf, gain, xn, stage, stat, far, ident, sel, cols, cdbc, mrows, bank, zd):
    with ExitStack() as s:
        sem = lambda name: nc.alloc_semaphore("m_" + name)
        sb = lambda name, shape: s.enter_context(nc.sbuf_tensor("m_" + name, shape, F32))
        at = [0]

        def carve(n, *dims):
            v = hbuf[:, at[0]:at[0] + n]
            at[0] += n
            if len(dims) == 2:
                v = v.rearrange("p (a b) -> p a b", a=dims[0])
            return v
        zb = [wbuf[:, i * ZC:(i + 1) * ZC] for i in range(2)]
        qkT = carve(24 * P, 24, P)
        rk = carve(2 * RW)
        tv = carve(2 * RW)
        qdT = rk[:, 0:RW].rearrange("p (h l) -> p h l", h=RH)
        sT = carve(RW, RH, P)
        kdec = xn[:, 0, 0:RW].rearrange("p (h d) -> p h d", h=RH)
        dw = xn[:, 0, RW:RW + 512]
        smT = xn[:, 0, RW + 512:2 * RW].rearrange("p (h l) -> p h l", h=MH)
        obuf = xn[:, 1, :]
        gateb = stage[:, 0:2 * RW]
        wk = stage[:, 2 * RW:2 * RW + 512].rearrange("p (h d) -> p h d", h=MH)
        tv2 = wbuf[:, 2 * ZC:2 * ZC + 2 * RW]
        vext = sb("vext", [P, MH, MV + 1])
        S = sb("S", [P, RH, RD])
        Sd = carve(RW, RH, RD)
        Cx = sb("Cx", [P, MH, MV + 1])
        Cd = sb("Cd", [P, MH, MV + 1])
        dec = sb("dec", [P, RH * P + 2 * RH])
        qdt = carve(RH * P)
        rope = sb("rope", [P, NB, RD])
        st = stat
        half = RD // 2

        const_in, st_in, z_in = sem("const"), sem("state_in"), [sem("z0"), sem("z1")]
        rot_v, rot_p, tq, te = sem("rot_v"), sem("rot_p"), sem("turned"), sem("turned_copied")
        qd_done, kd_done, wk_done, vx_done = sem("qdec"), sem("kdec"), sem("wkey"), sem("vext")
        pmb, mb_read, dwx, dwe = sem("maxima"), sem("maxima_read"), sem("dw_exponents"), sem("dw")
        ps_r, ps_m, s_r, s_m = sem("ps_ret"), sem("ps_ml"), sem("scores_ret"), sem("scores_ml")
        pu_r, pu_m, sd, cd = sem("upd_ret"), sem("upd_ml"), sem("s_decayed"), sem("c_decayed")
        su, cu = sem("s_updated"), sem("c_updated")
        po_r, po_m, po_i = sem("out_ret"), sem("out_ml"), sem("out_inter")
        ne, nr, ni = sem("inter_scaled"), sem("ret_read"), sem("num_read")
        sg, gg = sem("gates_sig"), sem("gates_gain")
        sq, rts, msr, mixd = sem("squares"), sem("roots"), sem("means"), sem("mixed")
        pt, ptc = sem("mix_turned"), sem("mix_copied")
        st_out, reset = sem("state_out"), sem("state_reset")
        ch_v, ch_p = sem("dve"), sem("pool")
        dec_in = sem("dec_in")
        qk16 = lambda z: z[:, 0:2 * RW].rearrange("p (h t e) -> p h t e", h=2 * RH, t=2)

        def cur(t, n=1):
            return t * n

        def blocks(eng, body):
            body(0, SB, 0, True)
            with eng.Fori(0, SB // 2) as i:
                for r in range(2):
                    body(2 * i + (r + 1), 2 * i + r, (r + 1) % 2, False)

        def cs(b, t):
            v = rope[:, b:b + 1, :] if isinstance(b, int) else rope[:, bass.ds(b, 1), :]
            return v[:, :, t * half:(t + 1) * half].to_broadcast([P, 2 * RH, half])

        def colap(b, q):
            return (cols[:, b, q, :] if isinstance(b, int) else
                    cols[:, bass.ds(b, 1), q, :].rearrange("p b h -> p (b h)"))

        vx_one, ptv = sem("vext_one"), sem("mix_copied_v")

        def mix_copy(copy, q, b, sample, done):
            src = bank(2 + q)
            if sample:
                s64 = src.rearrange("p (j l) -> p j l", j=4)[:, :, 0:SAMPLE]
                copy(actT[:, 4 * q:4 * q + 4, PROMPT:PROMPT + SAMPLE], s64)
                copy(actT[:, 4 * q:4 * q + 4, PROMPT + SAMPLE:T], s64).then_inc(done, 1)
            else:
                copy(actT[:, 4 * q:4 * q + 4, bass.ds(b * P, P)], src).then_inc(done, 1)

        with nc.Block() as block:
            @block.sync
            def _(sp):
                sp.dma_start(rope[:, :, :].rearrange("p b r -> p (b r)"), a["c_rope"]).then_inc(const_in, 16)
                sp.dma_start(qdt[:, :], a["c_qdecay"]).then_inc(const_in, 16)
                sp.dma_start(gain[:, 0:RW], a["g_ret"][0:1, :].to_broadcast([P, RW])).then_inc(const_in, 16)
                sp.dma_start(gain[:, RW:], a["g_mlstm"][0:1, :].to_broadcast([P, MW])).then_inc(const_in, 16)
                sp.dma_start(dec[:, :], a["c_decay"][1]).then_inc(dec_in, 16)
                sp.dma_start(S[:, :, :], a["state_ret"][0, 0].rearrange("h k v -> k h v")).then_inc(st_in, 16)
                sp.dma_start(Cx[:, :, 0:MV], a["state_mlstm_C"][0, 0].rearrange("h k v -> k h v")).then_inc(st_in, 16)
                with nc.allow_non_contiguous_dma(reason="one normaliser column"):
                    sp.dma_start(Cx[:, :, MV], a["state_mlstm_n"][0, 0].rearrange("h k -> k h")).then_inc(st_in, 16)

                def body(t, b, r, sample):
                    if not (sample or (isinstance(t, int))):
                        pass
                    zsrc = zd[b] if isinstance(b, int) else zd[bass.ds(b, 1)].rearrange("b p c -> p (b c)")
                    if not sample and r == 0:
                        sp.wait_ge(pt, 4 * t - 4)
                    elif not sample:
                        sp.wait_ge(pt, 4 * t - 4)
                    sp.dma_start(zb[r], zsrc).then_inc(z_in[r], 16)
                body(0, SB, 0, True)
                sp.dma_start(zb[1], zd[0]).then_inc(z_in[1], 16)

                def states(tag):
                    sp.dma_start(out["ret_" + tag][0, 0].rearrange("h k v -> k h v"), S[:, :, :]).then_inc(st_out, 16)
                    sp.dma_start(out["C_" + tag][0, 0].rearrange("h k v -> k h v"), Cx[:, :, 0:MV]).then_inc(st_out, 16)
                    with nc.allow_non_contiguous_dma(reason="one normaliser column"):
                        sp.dma_start(out["n_" + tag][0, 0].rearrange("h k -> k h"), Cx[:, :, MV]).then_inc(st_out, 16)
                sp.wait_ge(su, 1)
                sp.wait_ge(cu, 1)
                states("sample")
                sp.wait_ge(s_r, 1)
                sp.wait_ge(kd_done, 1)
                sp.wait_ge(sd, 1)
                sp.dma_start(dec[:, :], a["c_decay"][0]).then_inc(dec_in, 16)
                sp.wait_ge(pt, 4)
                sp.dma_start(zb[0], zd[1]).then_inc(z_in[0], 16)
                for t in (3, 4):
                    sp.wait_ge(pt, 4 * (t - 1))
                    sp.dma_start(zb[t % 2], zd[t - 1]).then_inc(z_in[t % 2], 16)
                sp.wait_ge(su, NB)
                sp.wait_ge(cu, NB)
                states("prompt")
                sp.wait_ge(st_out, 6 * 16)

            def z_wait(eng, t, r, sample):
                if sample:
                    eng.wait_ge(z_in[0], 16)
                else:
                    eng.wait_ge(z_in[r], 8 * t + (8 if r else 16))

            @block.gpsimd
            def _(pool):
                ch = Chain(pool, ch_p)
                pool.wait_ge(const_in, 64)
                n_ops = 7

                def body(t, b, r, sample):
                    ch.n, ch.off = 0, cur(t, n_ops)
                    do = ch.then_wait
                    z_wait(pool, t, r, sample)
                    x = qk16(zb[r])
                    if not sample:
                        pool.wait_ge(po_r, t)
                        pool.wait_ge(msr, t)
                        pool.wait_ge(kd_done, t)
                    t1 = tv2[:, 0:RW].rearrange("p (h e) -> p h e", e=half)
                    t2 = tv2[:, RW:].rearrange("p (h e) -> p h e", e=half)
                    do(pool.tensor_tensor(t1, x[:, :, 0, :], cs(b, 1), ALU.mult))
                    do(pool.tensor_tensor(t2, x[:, :, 1, :], cs(b, 0), ALU.mult))
                    pool.tensor_tensor(qk16(rk)[:, :, 1, :], t1, t2, ALU.add).then_inc(rot_p, 1)
                    pool.wait_ge(rot_p, t + 1)
                    pool.wait_ge(rot_v, t + 1)
                    pool.wait_ge(dec_in, 16 if sample else 32)
                    if not sample:
                        pool.wait_ge(pu_r, t)
                        pool.wait_ge(pu_m, t)
                    kd = dec[:, RH * P:RH * P + RH].rearrange("p (h o) -> p h o", o=1)
                    pool.tensor_tensor(kdec, rk[:, RW:].rearrange("p (h d) -> p h d", h=RH),
                                       kd.to_broadcast([P, RH, RD]), ALU.mult).then_inc(kd_done, 1)
                    wc = colap(b, 3).rearrange("p (h o) -> p h o", o=1)
                    pool.tensor_tensor(wk, zb[r][:, Z_MK:Z_MV].rearrange("p (h d) -> p h d", h=MH),
                                       wc.to_broadcast([P, MH, MK]), ALU.mult).then_inc(wk_done, 1)
                    if sample:
                        pool.wait_ge(st_in, 48)
                    else:
                        pool.wait_ge(reset, 2)
                        pool.wait_ge(su, t)
                        pool.wait_ge(cu, t)
                    gl = dec[:, RH * P + RH:].rearrange("p (h o) -> p h o", o=1)
                    pool.tensor_tensor(Sd[:, :, :], S[:, :, :], gl.to_broadcast([P, RH, RD]), ALU.mult).then_inc(sd, 1)
                    cb = (cdbc[:, b, :] if isinstance(b, int) else
                          cdbc[:, bass.ds(b, 1), :].rearrange("p b h -> p (b h)")).rearrange("p (h o) -> p h o", o=1)
                    pool.tensor_tensor(Cd[:, :, :], Cx[:, :, :], cb.to_broadcast([P, MH, MV + 1]), ALU.mult).then_inc(cd, 1)
                    pool.wait_ge(sg, t + 1)
                    do(pool.tensor_tensor(gateb[:, 0:RW], gateb[:, 0:RW], zb[r][:, Z_RG:Z_RG + RW], ALU.mult))
                    pool.tensor_tensor(gateb, gateb, gain[:, :], ALU.mult).then_inc(gg, 1)
                    assert ch.n <= n_ops
                    while ch.n < n_ops:
                        pool.sem_inc(ch_p, 1)
                        ch.n += 1
                blocks(pool, body)

            @block.scalar
            def _(act):
                def body(t, b, r, sample):
                    z_wait(act, t, r, sample)
                    if not sample:
                        act.wait_ge(mixd, 2 * t)
                    act.activation(gateb[:, 0:RW], zb[r][:, Z_RG:Z_RG + RW], ACT.Sigmoid)
                    act.activation(gateb[:, RW:], zb[r][:, Z_MO:Z_MO + MW], ACT.Sigmoid).then_inc(sg, 1)
                    if not sample:
                        act.wait_ge(po_m, t)
                    else:
                        act.wait_ge(vx_one, 1)
                    act.copy(vext[:, :, 0:MV], zb[r][:, Z_MV:Z_MO].rearrange("p (h v) -> p h v", h=MH)).then_inc(vx_done, 1)
                    if not sample:
                        act.wait_ge(po_i, t)
                        act.wait_ge(qd_done, t)
                    for j in range(6):
                        act.wait_ge(tq, 6 * t + (j + 1))
                        act.copy(qkT[:, 4 * j:4 * j + 4, :], bank(j)).then_inc(te, 1)
                    act.wait_ge(dwx, t + 1)
                    act.activation(dw, dw, ACT.Exp, scale=-1.0).then_inc(dwe, 1)
                    act.wait_ge(po_i, t + 1)
                    for hh in range(MH):
                        m = act.activation(tv[:, hh * MV:(hh + 1) * MV], bank(0, 1024, 2)[:, hh * MV:(hh + 1) * MV],
                                           ACT.Identity, scale=colap(b, 1)[:, hh:hh + 1])
                    m.then_inc(ne, 1)
                    act.wait_ge(rot_p, t + 1)
                    for q in range(2):
                        act.wait_ge(nr if q == 0 else ni, t + 1)
                        act.activation(tv2[:, q * RW:(q + 1) * RW], obuf[:, q * RW:(q + 1) * RW], ACT.Square).then_inc(sq, 1)
                    act.wait_ge(msr, t + 1)
                    act.activation(st[:, 12:24], st[:, 0:12], ACT.Sqrt).then_inc(rts, 1)
                    for q in range(2):
                        act.wait_ge(pt, 4 * t + (q + 1))
                        mix_copy(act.copy, q, b, sample, ptc)
                blocks(act, body)

            @block.tensor
            def _(pe):
                def body(t, b, r, sample):
                    z = zb[r]
                    z_wait(pe, t, r, sample)
                    pe.wait_ge(rot_v, t + 1)
                    pe.wait_ge(rot_p, t + 1)
                    if not sample:
                        pe.wait_ge(ptc, 2 * t)
                        pe.wait_ge(ptv, 2 * t)
                    for j in range(6):
                        for i in range(4):
                            n = 4 * j + i
                            src = rk[:, n * P:(n + 1) * P] if n < 2 * RH else z[:, Z_MQ + (n - 2 * RH) * P:Z_MQ + (n - 2 * RH + 1) * P]
                            m = pe.transpose(bank(j)[:, i * P:(i + 1) * P], src, ident)
                        m.then_inc(tq, 1)
                    if not sample:
                        pe.wait_ge(cu, t)
                        pe.wait_ge(ni, t)
                    for hh in range(MH):
                        m = pe.matmul(bank(6)[:, hh * P:(hh + 1) * P], sel[0:MH, hh, :], mrows[:, bass.ds(b * P, P)],
                                      start=True, stop=True)
                    m.then_inc(pmb, 1)
                    pe.wait_ge(te, 6 * t + 4)
                    for hh in range(RH):
                        m = pe.matmul(bank(0, 1024, 2)[:, hh * P:(hh + 1) * P], qkT[:, RH + hh, :], qkT[:, hh, :],
                                      start=True, stop=True)
                    m.then_inc(ps_r, 1)
                    pe.wait_ge(te, 6 * t + 6)
                    for hh in range(MH):
                        m = pe.matmul(bank(2)[:, hh * P:(hh + 1) * P], qkT[:, 20 + hh, :], qkT[:, 16 + hh, :],
                                      start=True, stop=True)
                    m.then_inc(ps_m, 1)
                    pe.wait_ge(kd_done, t + 1)
                    for hh in range(RH):
                        m = pe.matmul(bank(3, 1024, 2)[:, hh * RD:(hh + 1) * RD], kdec[:, hh, :],
                                      z[:, Z_RV + hh * RD:Z_RV + (hh + 1) * RD], start=True, stop=True)
                    m.then_inc(pu_r, 1)
                    pe.wait_ge(wk_done, t + 1)
                    pe.wait_ge(vx_done, t + 1)
                    pe.wait_ge(mb_read, t + 1)
                    for hh in range(MH):
                        pe.matmul(bank(5, 1024, 2)[:, hh * MV:(hh + 1) * MV], wk[:, hh, :], vext[:, hh, 0:MV],
                                  start=True, stop=True)
                        m = pe.matmul(bank(7)[:, 8 + hh:9 + hh], wk[:, hh, :], vext[:, hh, MV:MV + 1],
                                      start=True, stop=True)
                    m.then_inc(pu_m, 1)
                    pe.wait_ge(s_r, t + 1)
                    pe.wait_ge(qd_done, t + 1)
                    if sample:
                        pe.wait_ge(st_in, 48)
                    else:
                        pe.wait_ge(reset, 2)
                        pe.wait_ge(su, t)
                    for hh in range(RH):
                        o = bank(0, 1024, 2)[:, hh * RD:(hh + 1) * RD]
                        pe.matmul(o, sT[:, hh, :], z[:, Z_RV + hh * RD:Z_RV + (hh + 1) * RD], start=True, stop=False)
                        m = pe.matmul(o, qdT[:, hh, :], S[:, hh, :], start=False, stop=True)
                    m.then_inc(po_r, 1)
                    pe.wait_ge(s_m, t + 1)
                    pe.wait_ge(su, t + 1)
                    for hh in range(MH):
                        pe.matmul(bank(2, 1024, 2)[:, hh * MV:(hh + 1) * MV], smT[:, hh, :], vext[:, hh, 0:MV],
                                  start=True, stop=True)
                        m = pe.matmul(bank(7)[:, hh:hh + 1], smT[:, hh, :], vext[:, hh, MV:MV + 1], start=True, stop=True)
                    m.then_inc(po_m, 1)
                    pe.wait_ge(nr, t + 1)
                    for hh in range(MH):
                        pe.matmul(bank(0, 1024, 2)[:, hh * MV:(hh + 1) * MV], qkT[:, 16 + hh, :], Cx[:, hh, 0:MV],
                                  start=True, stop=True)
                        m = pe.matmul(bank(7)[:, 4 + hh:5 + hh], qkT[:, 16 + hh, :], Cx[:, hh, MV:MV + 1],
                                      start=True, stop=True)
                    m.then_inc(po_i, 1)
                    pe.wait_ge(ni, t + 1)
                    pe.wait_ge(cu, t + 1)
                    for q in range(4):
                        pe.wait_ge(mixd, 2 * t + (1 if q < 2 else 2))
                        for j in range(4):
                            n = 4 * q + j
                            m = pe.transpose(bank(2 + q)[:, j * P:(j + 1) * P], obuf[:, n * P:(n + 1) * P], ident)
                        m.then_inc(pt, 1)
                blocks(pe, body)

            @block.vector
            def _(dve):
                ch = Chain(dve, ch_v)
                n_ops = 24
                dve.memset(vext[:, :, MV:MV + 1], 1.0).then_inc(vx_one, 1)
                dve.wait_ge(const_in, 64)

                def body(t, b, r, sample):
                    ch.n, ch.off = 0, cur(t, n_ops)
                    do = ch.then_wait
                    z_wait(dve, t, r, sample)
                    x = qk16(zb[r])
                    t1 = tv[:, 0:RW].rearrange("p (h e) -> p h e", e=half)
                    t2 = tv[:, RW:].rearrange("p (h e) -> p h e", e=half)
                    do(dve.tensor_tensor(t1, x[:, :, 0, :], cs(b, 0), ALU.mult))
                    do(dve.tensor_tensor(t2, x[:, :, 1, :], cs(b, 1), ALU.mult))
                    if not sample:
                        dve.wait_ge(po_r, t)
                        dve.wait_ge(kd_done, t)
                    dve.tensor_tensor(qk16(rk)[:, :, 0, :], t1, t2, ALU.subtract).then_inc(rot_v, 1)
                    dve.wait_ge(pmb, t + 1)
                    if not sample:
                        dve.wait_ge(s_m, t)
                    for hh in range(MH):
                        m = dve.scalar_tensor_tensor(out=dw[:, hh * P:(hh + 1) * P], in0=bank(6)[:, hh * P:(hh + 1) * P],
                                                     scalar=colap(b, 0)[:, hh:hh + 1], in1=far,
                                                     op0=ALU.subtract, op1=ALU.max)
                        if hh < MH - 1:
                            do(m)
                    m.then_inc(dwx, 1)
                    dve.wait_ge(dwx, t + 1)
                    dve.sem_inc(mb_read, 1)
                    dve.wait_ge(ps_r, t + 1)
                    dve.wait_ge(dec_in, 16 if sample else 32)
                    dve.tensor_tensor(sT.rearrange("p h l -> p (h l)"), bank(0, 1024, 2), dec[:, 0:RH * P], ALU.mult).then_inc(s_r, 1)
                    dve.tensor_tensor(qdT.rearrange("p h l -> p (h l)"), qkT[:, 0:RH, :].rearrange("p h l -> p (h l)"),
                                      qdt[:, :], ALU.mult).then_inc(qd_done, 1)
                    dve.wait_ge(ps_m, t + 1)
                    dve.wait_ge(dwe, t + 1)
                    dve.scalar_tensor_tensor(out=smT.rearrange("p h l -> p (h l)"), in0=bank(2), scalar=MK ** -0.5, in1=dw,
                                             op0=ALU.mult, op1=ALU.mult).then_inc(s_m, 1)
                    dve.wait_ge(po_r, t + 1)
                    dve.wait_ge(sd, t + 1)
                    dve.wait_ge(pu_r, t + 1)
                    dve.tensor_tensor(S[:, :, :].rearrange("p h v -> p (h v)"), Sd[:, :, :].rearrange("p h v -> p (h v)"),
                                      bank(3, 1024, 2), ALU.add).then_inc(su, 1)
                    dve.tensor_copy(obuf[:, 0:RW], bank(0, 1024, 2)).then_inc(nr, 1)
                    dve.wait_ge(po_i, t + 1)
                    dve.wait_ge(po_m, t + 1)
                    do(dve.tensor_tensor(st[:, 24:28], bank(7)[:, 4:8], colap(b, 1), ALU.mult))
                    do(dve.tensor_tensor(st[:, 28:32], bank(7)[:, 0:4], st[:, 24:28], ALU.add))
                    do(dve.scalar_tensor_tensor(out=st[:, 32:36], in0=st[:, 28:32], scalar=-1.0, in1=st[:, 28:32],
                                                op0=ALU.mult, op1=ALU.max))
                    do(dve.tensor_tensor(st[:, 36:40], st[:, 32:36], colap(b, 2), ALU.max))
                    do(dve.reciprocal(st[:, 40:44], st[:, 36:40]))
                    dve.wait_ge(ne, t + 1)
                    do(dve.tensor_tensor(tv[:, RW:], bank(2, 1024, 2), tv[:, 0:RW], ALU.add))
                    rd = st[:, 40:44].rearrange("p (h o) -> p h o", o=1)
                    dve.tensor_tensor(obuf[:, RW:].rearrange("p (h v) -> p h v", h=MH),
                                      tv[:, RW:].rearrange("p (h v) -> p h v", h=MH),
                                      rd.to_broadcast([P, MH, MV]), ALU.mult).then_inc(ni, 1)
                    dve.wait_ge(cd, t + 1)
                    do(dve.tensor_tensor(Cx[:, :, 0:MV], Cd[:, :, 0:MV],
                                         bank(5, 1024, 2).rearrange("p (h v) -> p h v", h=MH), ALU.add))
                    dve.tensor_tensor(Cx[:, :, MV], Cd[:, :, MV], bank(7)[:, 8:12], ALU.add).then_inc(cu, 1)
                    dve.wait_ge(sq, 2 * t + 2)
                    do(dve.tensor_reduce(st[:, 44:52], tv2[:, 0:RW].rearrange("p (h v) -> p h v", h=RH), AX_X, ALU.add))
                    do(dve.tensor_reduce(st[:, 52:56], tv2[:, RW:].rearrange("p (h v) -> p h v", h=MH), AX_X, ALU.add))
                    do(dve.tensor_scalar(st[:, 0:8], st[:, 44:52], 1.0 / RD, EPS, ALU.mult, ALU.add))
                    dve.tensor_scalar(st[:, 8:12], st[:, 52:56], 1.0 / MV, EPS, ALU.mult, ALU.add).then_inc(msr, 1)
                    dve.wait_ge(rts, t + 1)
                    do(dve.reciprocal(st[:, 56:68], st[:, 12:24]))
                    dve.wait_ge(gg, t + 1)
                    do(dve.tensor_tensor(obuf[:, 0:RW].rearrange("p (h v) -> p h v", h=RH),
                                         obuf[:, 0:RW].rearrange("p (h v) -> p h v", h=RH),
                                         st[:, 56:64].rearrange("p (h o) -> p h o", o=1).to_broadcast([P, RH, RD]), ALU.mult))
                    dve.tensor_tensor(obuf[:, 0:RW], obuf[:, 0:RW], gateb[:, 0:RW], ALU.mult).then_inc(mixd, 1)
                    do(dve.tensor_tensor(obuf[:, RW:].rearrange("p (h v) -> p h v", h=MH),
                                         obuf[:, RW:].rearrange("p (h v) -> p h v", h=MH),
                                         st[:, 64:68].rearrange("p (h o) -> p h o", o=1).to_broadcast([P, MH, MV]), ALU.mult))
                    dve.tensor_tensor(obuf[:, RW:], obuf[:, RW:], gateb[:, RW:], ALU.mult).then_inc(mixd, 1)
                    for q in range(2, 4):
                        dve.wait_ge(pt, 4 * t + (q + 1))
                        mix_copy(dve.tensor_copy, q, b, sample, ptv)
                    if sample:
                        dve.wait_ge(st_out, 48)
                        dve.memset(S[:, :, :], 0.0).then_inc(reset, 1)
                        dve.memset(Cx[:, :, :], 0.0).then_inc(reset, 1)
                    assert ch.n <= n_ops, ch.n
                    dve.sem_inc(ch_v, n_ops - ch.n)
                blocks(dve, body)


def experts(nc, a, h, actT, wbuf, W, gain, xn, stage, stat, ident, fold, iota, bank):
    with ExitStack() as s:
        sb = lambda name, shape, dt=F32: s.enter_context(nc.sbuf_tensor("e_" + name, shape, dt))
        eidx = sb("eidx", [P, NB, NPICK], U32)
        gate = sb("gate", [P, NB, NPICK])
        route(nc, a, actT, wbuf, W, xn, stage, stat, ident, iota, bank, eidx, gate)
        gather(nc, a, h, wbuf, gain, xn, stage, stat, fold, bank, eidx, gate)


def route(nc, a, actT, wbuf, W, xn, stage, stat, ident, iota, bank, eidx, gate):
    with ExitStack() as s:
        sem = lambda name: nc.alloc_semaphore("r_" + name)
        sb = lambda name, shape, dt=F32: s.enter_context(nc.sbuf_tensor("r_" + name, shape, dt))
        keys = sb("keys", [P, 2, NKEY])
        keysT = sb("keysT", [P, 2, NKEY])
        qT = xn[:, 0, 0:2 * T].rearrange("p (r t) -> p r t", r=2)
        sc = xn[:, 0, 2 * T:3 * T]
        sc2 = xn[:, 0, 3 * T:3 * T + NKEY]
        top = sb("top", [P, NB, HH, TOPK])
        topi = sb("topi", [P, NB, HH, TOPK], U32)
        cand = stage[:, 0:EH * NC].rearrange("p (h c) -> p h c", h=EH)
        cidx = stage[:, EH * NC:2 * EH * NC].rearrange("p (h c) -> p h c", h=EH)
        cand2 = stage[:, 2 * EH * NC:3 * EH * NC].rearrange("p (h c) -> p h c", h=EH)
        ti = sb("ti", [P, HH, TOPK])
        tv = sb("tv", [P, NB, TOPK])
        tx = sb("tx", [P, NB, TOPK], U32)
        best = sb("best", [P, EH, TOPK])
        besti = sb("besti", [P, EH, TOPK], U32)
        bestf = sb("bestf", [P, EH, TOPK])
        sm = sb("sm", [P, EH, TOPK])
        sums = sb("sums", [P, 2 * EH])
        ef = sb("ef", [P, EH, TOPK])
        hot = wbuf[:, 0:NPICK * NC].rearrange("p (k c) -> p k c", c=NC)
        k_in, k_t, k_c = sem("keys"), sem("keys_turned"), sem("keys_copied")
        w_in = [sem("w0"), sem("w1")]
        qmm, qcp, smm, scp = sem("q_mm"), sem("q_copied"), sem("s_mm"), sem("s_copied")
        chain, exd, exq, found = sem("dve"), sem("exp_done"), sem("exp_ready"), sem("found")
        per_hh = 1 + 5 * NB
        with nc.Block() as block:
            @block.sync
            def _(sp):
                sp.dma_start(keys[:, 0, :], a["peer_keys1"][0]).then_inc(k_in, 16)
                sp.dma_start(keys[:, 1, :], a["peer_keys2"][0]).then_inc(k_in, 16)
                wv = a["w_peer_q"][0].rearrange("(k p) c -> p k c", p=P)
                for g in range(2):
                    sp.dma_start(W[:, g, :, :], wv[:, :, g * CG:(g + 1) * CG]).then_inc(w_in[g], 16)
                for g in range(2, DG):
                    sp.wait_ge(qmm, 4 * (g - 1))
                    sp.dma_start(W[:, g % 2, :, :], wv[:, :, g * CG:(g + 1) * CG]).then_inc(w_in[g % 2], 16)

            @block.tensor
            def _(pe):
                pe.wait_ge(k_in, 32)
                for i in range(2):
                    m = pe.transpose(bank(4)[:, i * P:(i + 1) * P], keys[:, i, :], ident)
                m.then_inc(k_t, 1)

                def queries(x, r, g, c, first):
                    if c == 0:
                        pe.wait_ge(w_in[g], 16 * first + 16 if isinstance(first, int) else first)
                    if not isinstance(x, int) or x >= 2:
                        pe.wait_ge(qcp, 2 * x - 2)
                    for k in range(KT):
                        pe.matmul(bank(2 * r), W[:, g, k, c * P:(c + 1) * P], actT[:, k, 0:PROMPT],
                                  start=(k == 0), stop=(k == KT - 1))
                    for k in range(KT):
                        m = pe.matmul(bank(2 * r + 1)[:, 0:SAMPLE], W[:, g, k, c * P:(c + 1) * P],
                                      actT[:, k, PROMPT:PROMPT + SAMPLE], start=(k == 0), stop=(k == KT - 1))
                    m.then_inc(qmm, 1)

                def scores(x, r):
                    pe.wait_ge(qcp, 2 * x + 2)
                    if not isinstance(x, int) or x >= 2:
                        pe.wait_ge(scp, x - 1)
                    elif x == 0:
                        pe.wait_ge(k_c, 1)
                    for b in range(NB):
                        o = bank(4 + 2 * r, 1024, 2)[:, b * P:(b + 1) * P]
                        m = pe.matmul(o, qT[:, r, b * P:(b + 1) * P], keysT[:, r, :], start=True, stop=True)
                    m.then_inc(smm, 1)

                def eight(i, first):
                    for c8 in range(8):
                        x, r, g, c = 8 * i + c8, c8 % 2, c8 // 4, c8 % 4
                        queries(x, r, g, c, i if isinstance(i, int) else 16 * i + 16)
                        if c8 == 0 and first:
                            continue
                        scores(x - 1, (c8 + 1) % 2)
                for i in range(HH // 8):
                    eight(i, i == 0)
                scores(HH - 1, 1)

            @block.scalar
            def _(act):
                act.wait_ge(k_t, 1)
                act.copy(keysT[:, :, :].rearrange("p a k -> p (a k)"), bank(4)[:, 0:2 * P]).then_inc(k_c, 1)

                def body(x, r, early):
                    act.wait_ge(qmm, x + 1)
                    if not early:
                        act.wait_ge(smm, x - 1)
                    act.copy(qT[:, r, 0:PROMPT], bank(2 * r)).then_inc(qcp, 1)
                    act.copy(qT[:, r, PROMPT:PROMPT + SAMPLE], bank(2 * r + 1)[:, 0:SAMPLE])
                    act.copy(qT[:, r, PROMPT + SAMPLE:T], bank(2 * r + 1)[:, 0:SAMPLE]).then_inc(qcp, 1)
                for x in range(2):
                    body(x, x, True)
                with act.Fori(1, HH // 2) as i:
                    for r in range(2):
                        body(2 * i + r, r, False)
                for b in range(NB):
                    act.wait_ge(exq, b + 1)
                    act.activation(sm[:, :, :], sm[:, :, :], ACT.Exp).then_inc(exd, 1)

            @block.vector
            def _(dve):
                ch = Chain(dve, chain)
                passed = Gate(nc, dve, "r_passed")

                def sixteen(vals, idx, src, spare):
                    def do(ins):
                        ch.then_wait(ins)
                        passed.close()
                    do(dve.max(vals[:, 0:8], src))
                    do(dve.max_index(idx[:, 0:8], vals[:, 0:8], src))
                    do(dve.match_replace(spare, vals[:, 0:8], src, LOWEST))
                    do(dve.max(vals[:, 8:16], spare))
                    do(dve.max_index(idx[:, 8:16], vals[:, 8:16], spare))

                with dve.Fori(0, EH) as i:
                    for r in range(2):
                        if r == 0:
                            ch.n, ch.off = 0, i * (10 * NB + 4)
                        dve.wait_ge(smm, 2 * i + (r + 1))
                        dve.tensor_copy(sc[:, :], bank(4 + 2 * r, T, 2)).then_inc(scp, 1)
                        dve.wait_ge(scp, 2 * i + (r + 1))
                        passed.close()
                        for b in range(NB):
                            sixteen(tv[:, b, :], tx[:, b, :], sc[:, b * P:(b + 1) * P], sc2[:, :])
                        x = bass.ds(2 * i + r, 1)
                        ch.then_wait(dve.tensor_copy(top[:, :, x, :].rearrange("p b o k -> p b (o k)"), tv[:, :, :]))
                        ch.then_wait(dve.tensor_copy(topi[:, :, x, :].rearrange("p b o k -> p b (o k)"), tx[:, :, :]))
                base = EH * (10 * NB + 4)
                n_blk = 150
                with dve.Fori(0, NB) as b:
                    ch.n, ch.off = 0, b * n_blk + base
                    do = ch.then_wait
                    tb = top[:, bass.ds(b, 1), :, :].rearrange("p o h k -> p (o h) k").rearrange("p (h t) k -> p h t k", t=2)
                    do(dve.tensor_copy(ti[:, :, :], topi[:, bass.ds(b, 1), :, :].rearrange("p o h k -> p (o h) k")))
                    ib = ti[:, :, :].rearrange("p (h t) k -> p h t k", t=2)
                    do(dve.tensor_scalar(ib[:, :, 0, :], ib[:, :, 0, :], float(NKEY), None, ALU.mult))
                    c0 = 0
                    for j, n, w in PAIR_ROWS:
                        for src, dst in ((tb, cand), (ib, cidx)):
                            if n == 1:
                                o = dst[:, :, c0:c0 + w]
                                x1 = src[:, :, 0, j:j + 1].to_broadcast([P, EH, w])
                                x2 = src[:, :, 1, 0:w]
                            else:
                                o = dst[:, :, c0:c0 + n * w].rearrange("p h (n w) -> p h n w", n=n)
                                x1 = src[:, :, 0, j:j + n].rearrange("p h (n o) -> p h n o", o=1).to_broadcast([P, EH, n, w])
                                x2 = src[:, :, 1, 0:w].rearrange("p h (o w) -> p h o w", o=1).to_broadcast([P, EH, n, w])
                            do(dve.tensor_tensor(o, x1, x2, ALU.add))
                        c0 += n * w
                    passed.close()
                    for e in range(EH):
                        sixteen(best[:, e, :], besti[:, e, :], cand[:, e, :], cand2[:, e, :])
                    do(dve.tensor_tensor(sm[:, :, :], best[:, :, :], best[:, :, 0:1].to_broadcast([P, EH, TOPK]), ALU.subtract))
                    dve.sem_inc(exq, 1)
                    do(dve.tensor_copy(bestf[:, :, :], besti[:, :, :]))
                    bf = bestf[:, :, :].rearrange("p h (k o) -> p (h k) o", o=1)
                    io = iota.rearrange("p (o c) -> p o c", o=1)
                    do(dve.tensor_tensor(hot, bf.to_broadcast([P, NPICK, NC]), io.to_broadcast([P, NPICK, NC]), ALU.is_equal))
                    for e in range(EH):
                        he = hot[:, e * TOPK:(e + 1) * TOPK, :]
                        do(dve.tensor_tensor(he, he, cidx[:, e:e + 1, :].to_broadcast([P, TOPK, NC]), ALU.mult))
                    do(dve.tensor_reduce(ef[:, :, :].rearrange("p h k -> p (h k)"), hot, AX_X, ALU.add))
                    do(dve.tensor_copy(eidx[:, bass.ds(b, 1), :].rearrange("p o k -> p (o k)"),
                                       ef[:, :, :].rearrange("p h k -> p (h k)")))
                    dve.wait_ge(exd, b + 1)
                    do(dve.tensor_reduce(sums[:, 0:EH], sm[:, :, :], AX_X, ALU.add))
                    do(dve.reciprocal(sums[:, EH:], sums[:, 0:EH]))
                    do(dve.tensor_tensor(gate[:, bass.ds(b, 1), :].rearrange("p o (h k) -> p (o h) k", k=TOPK), sm[:, :, :],
                                         sums[:, EH:].rearrange("p (h o) -> p h o", o=1).to_broadcast([P, EH, TOPK]), ALU.mult))
                    assert ch.n <= n_blk, ch.n
                    dve.sem_inc(chain, n_blk - ch.n)
                for v in (eidx, gate):
                    dve.tensor_copy(v[SAMPLE:P, SB, 0:NPICK // 2], v[SAMPLE:P, SB, NPICK // 2:]).then_inc(found, 1)


def gather(nc, a, h, wbuf, gain, xn, stage, stat, fold, bank, eidx, gate):
    with ExitStack() as s:
        sem = lambda name: nc.alloc_semaphore("g_" + name)
        sb = lambda name, shape, dt=F32: s.enter_context(nc.sbuf_tensor("g_" + name, shape, dt))
        ring = wbuf[:, :].rearrange("p (s d) -> p s d", s=8)
        u_in = [sem(f"u{i}") for i in range(4)]
        v_in = [sem(f"v{i}") for i in range(4)]
        uix = sb("uix", [P, 2, GRP], U32)
        vix = sb("vix", [P, 2, GRP], U32)
        dots = sb("dots", [P, 2, GRP])
        gel = sb("gel", [P, 2, GRP])
        wts = sb("wts", [P, 2, GRP])
        cx = xn[:, 0, :]
        junk = xn[:, 1, :]
        junk_a = stage[:, 0:D]
        u_idx, v_idx, u_used, v_used = sem("u_idx"), sem("v_idx"), sem("u_used"), sem("v_used")
        gelud, weighted, c_ready, zeroed, folded = sem("gelu"), sem("weights"), sem("c"), sem("zeroed"), sem("folded")
        squared, rooted, mean, chain, fmm = sem("squared"), sem("rooted"), sem("mean"), sem("dve"), sem("fold_mm")
        NG = NPICK // GRP
        u_tab, v_tab = a["peer_u"][0], a["peer_v"][0]
        off = bass.IndirectOffsetOnAxis
        with nc.Block() as block:
            @block.gpsimd
            def _(pool):
                passed = Gate(nc, pool, "g_passed")

                def u_group(n, r, b, g, first):
                    if not first:
                        for i in range(4):
                            pool.wait_ge(u_in[i], 32 * n - 32)
                    passed.close()
                    pool.tensor_copy(uix[:, r, :], eidx[:, bass.ds(b, 1), bass.ds(g * GRP, GRP)].rearrange("p o k -> p (o k)")
                                     if not isinstance(b, int) else eidx[:, b, bass.ds(g * GRP, GRP)]).then_inc(u_idx, 1)
                    pool.wait_ge(u_idx, n + 1)
                    passed.close()

                def v_group(n, r, b, g, first):
                    if not first:
                        for i in range(4):
                            pool.wait_ge(v_in[i], 32 * n - 32)
                    passed.close()
                    pool.tensor_copy(vix[:, r, :], eidx[:, bass.ds(b, 1), bass.ds(g * GRP, GRP)].rearrange("p o k -> p (o k)")
                                     if not isinstance(b, int) else eidx[:, b, bass.ds(g * GRP, GRP)]).then_inc(v_idx, 1)
                    pool.wait_ge(v_idx, n + 1)
                    passed.close()

                def u_row(n, r, j, first):
                    if not (first and j < 4):
                        pool.wait_ge(u_used, GRP * n + (j - 3))
                    passed.close()
                    pool.indirect_dma_start(ring[:, j % 4, :], None, u_tab, off(uix[:, r, j:j + 1], 0)
                                            ).then_inc(u_in[j % 4], 16)

                def v_row(n, r, j, first):
                    if not (first and j < 4):
                        pool.wait_ge(v_used, GRP * n + (j - 3))
                    passed.close()
                    pool.indirect_dma_start(ring[:, 4 + j % 4, :], None, v_tab, off(vix[:, r, j:j + 1], 0)
                                            ).then_inc(v_in[j % 4], 16)

                def block_of(b, groups, very_first):
                    n0 = b * NG
                    u_group(n0, 0, b, 0, very_first)
                    for j in range(GRP):
                        u_row(n0, 0, j, very_first)

                    def both(g, ru, rv, fu, fv):
                        u_group(n0 + g, ru, b, g, fu)
                        v_group(n0 + g - 1, rv, b, g - 1, fv)
                        for j in range(GRP):
                            u_row(n0 + g, ru, j, False)
                            v_row(n0 + g - 1, rv, j, fv)
                    both(1, 1, 0, very_first, very_first)
                    with pool.Fori(1, groups // 2) as i:
                        both(2 * i, 0, 1, False, False)
                        both(2 * i + 1, 1, 0, False, False)
                    v_group(n0 + groups - 1, 1, b, groups - 1, False)
                    for j in range(GRP):
                        v_row(n0 + groups - 1, 1, j, False)
                block_of(0, NG, True)
                with pool.Fori(1, SB) as b:
                    block_of(b, NG, False)
                block_of(SB, NG // 2, False)

            @block.scalar
            def _(act):
                def start(b, first):
                    hb = h[:, b, :] if isinstance(b, int) else h[:, bass.ds(b, 1), :]
                    if not first:
                        act.wait_ge(u_used, NG * GRP * b)
                    act.activation(junk_a, hb, ACT.Square, accum_out=stat[:, 0:1]).then_inc(squared, 1)
                    act.wait_ge(mean, b + 1)
                    act.activation(stat[:, 2:3], stat[:, 1:2], ACT.Sqrt).then_inc(rooted, 1)

                def gelus(n, r, first):
                    act.wait_ge(u_used, GRP * n + GRP)
                    if not first:
                        act.wait_ge(weighted, n - 1)
                    act.activation(gel[:, r, :], dots[:, r, :], ACT.Gelu).then_inc(gelud, 1)

                def block_of(b, groups, first):
                    start(b, first)
                    n0 = b * NG
                    for r in range(2):
                        gelus(n0 + r, r, first)
                    with act.Fori(1, groups // 2) as i:
                        for r in range(2):
                            gelus(n0 + 2 * i + r, r, False)
                block_of(0, NG, True)
                with act.Fori(1, SB) as b:
                    block_of(b, NG, False)
                block_of(SB, NG // 2, False)

            @block.vector
            def _(dve):
                ch = Chain(dve, chain)

                def hblk(b):
                    return h[:, b, :] if isinstance(b, int) else h[:, bass.ds(b, 1), :].rearrange("p o d -> p (o d)")

                def start(b):
                    dve.wait_ge(squared, b + 1)
                    dve.tensor_scalar(stat[:, 1:2], stat[:, 0:1], 1.0 / D, EPS, ALU.mult, ALU.add).then_inc(mean, 1)
                    dve.wait_ge(rooted, b + 1)
                    ch.n, ch.off = 0, b
                    ch.then_wait(dve.reciprocal(stat[:, 3:4], stat[:, 2:3]))
                    dve.scalar_tensor_tensor(out=cx, in0=hblk(b), scalar=stat[:, 3:4], in1=gain[:, :],
                                             op0=ALU.mult, op1=ALU.mult).then_inc(c_ready, 1)
                    dve.wait_ge(c_ready, b + 1)

                def dot(n, r, j):
                    dve.wait_ge(u_in[j % 4], 32 * n + (16 if j < 4 else 32))
                    if not (isinstance(n, int) and n == 0 and j == 0):
                        dve.wait_ge(u_used, GRP * n + j)
                    dve.tensor_tensor_reduce(junk, ring[:, j % 4, :], cx, 1.0, 0.0, ALU.mult, ALU.add,
                                             dots[:, r, j:j + 1]).then_inc(u_used, 1)

                def weigh(n, r, b, g):
                    dve.wait_ge(gelud, n + 1)
                    gv = (gate[:, b, bass.ds(g * GRP, GRP)] if isinstance(b, int) else
                          gate[:, bass.ds(b, 1), bass.ds(g * GRP, GRP)].rearrange("p o k -> p (o k)"))
                    dve.tensor_tensor(wts[:, r, :], gel[:, r, :], gv, ALU.mult).then_inc(weighted, 1)
                    dve.wait_ge(weighted, n + 1)

                def add(n, r, j, b):
                    dve.wait_ge(v_in[j % 4], 32 * n + (16 if j < 4 else 32))
                    if not (isinstance(n, int) and n == 0 and j == 0):
                        dve.wait_ge(v_used, GRP * n + j)
                    dve.scalar_tensor_tensor(out=hblk(b), in0=ring[:, 4 + j % 4, :], scalar=wts[:, r, j:j + 1],
                                             in1=hblk(b), op0=ALU.mult, op1=ALU.add).then_inc(v_used, 1)

                def block_of(b, groups):
                    start(b)
                    if b is SB:
                        dve.memset(h[SAMPLE:P, SB, :], 0.0).then_inc(zeroed, 1)
                        dve.wait_ge(zeroed, 1)
                    n0 = b * NG

                    def first_dots(n, r):
                        for j in range(GRP):
                            dot(n, r, j)
                    first_dots(n0, 0)

                    def both(g, ru, rv):
                        dot(n0 + g, ru, 0)
                        weigh(n0 + g - 1, rv, b, g - 1)
                        for j in range(GRP):
                            if j:
                                dot(n0 + g, ru, j)
                            add(n0 + g - 1, rv, j, b)
                    both(1, 1, 0)
                    with dve.Fori(1, groups // 2) as i:
                        both(2 * i, 0, 1)
                        both(2 * i + 1, 1, 0)
                    weigh(n0 + groups - 1, 1, b, groups - 1)
                    for j in range(GRP):
                        add(n0 + groups - 1, 1, j, b)
                block_of(0, NG)
                with dve.Fori(1, SB) as b:
                    block_of(b, NG)
                block_of(SB, NG // 2)
                dve.wait_ge(fmm, 1)
                dve.tensor_copy(h[:, SB, :], bank(0, D, 4)).then_inc(folded, 1)

            @block.tensor
            def _(pe):
                pe.wait_ge(v_used, GRP * (NG * SB + NG // 2))
                for q in range(4):
                    m = pe.matmul(bank(q), fold, h[:, SB, q * 512:(q + 1) * 512], start=True, stop=True)
                m.then_inc(fmm, 1)


def embeddings(nc, a, out, h, actT, W, gain, xn, stage, stat, ident, bank, row_bcast):
    PK = PLE // P
    with ExitStack() as s:
        sem = lambda name: nc.alloc_semaphore("x_" + name)
        sb = lambda name, shape: s.enter_context(nc.sbuf_tensor("x_" + name, shape, F32))
        p_sb = sb("p", [P, NB, PLE])
        pT = sb("pT", [P, PK, T])
        wp = xn
        p_in, wp_in, w_in = sem("p_in"), sem("wp_in"), [sem("w0"), sem("w1")]
        pt, ptc, mm, taken, sg = sem("p_turned"), sem("p_copied"), sem("mm"), sem("taken"), sem("sigmoid")
        pj, added, chain = sem("proj"), sem("added"), sem("dve")
        g_in, squared, mean, rooted, y_ready = sem("gain"), sem("squared"), sem("mean"), sem("rooted"), sem("y")
        y_out = [sem("y_out0"), sem("y_out1")]
        sig = stage[:, 0:2 * CG].rearrange("p (r c) -> p r c", r=2)
        junk = stage[:, 0:D]
        with nc.Block() as block:
            @block.sync
            def _(sp):
                for b in range(SB):
                    sp.dma_start(p_sb[:, b, :], a["p_prompt"][0, 0, b * P:(b + 1) * P, :]).then_inc(p_in, 16)
                for c in range(2):
                    sp.dma_start(p_sb[c * SAMPLE:(c + 1) * SAMPLE, SB, :], a["p_sample"][0, 0]).then_inc(p_in, 16)
                sp.dma_start(wp[:, :, :], a["w_ple_proj"][0].rearrange("(k p) c -> p k c", p=P)).then_inc(wp_in, 16)
                sp.dma_start(gain[:, :], row_bcast(a["g_final"])).then_inc(g_in, 16)
                weight_groups(sp, W, a["w_ple_gate"][0], DG, w_in, mm)
                for b in range(NB):
                    sp.wait_ge(y_ready, b + 1)
                    if b < SB:
                        sp.dma_start(out["y_prompt"][0, b * P:(b + 1) * P, :], xn[:, b % 2, :]).then_inc(y_out[b % 2], 16)
                    else:
                        sp.dma_start(out["y_sample"][0], xn[0:SAMPLE, b % 2, :]).then_inc(y_out[b % 2], 16)
                sp.wait_ge(y_out[0], 48)
                sp.wait_ge(y_out[1], 32)

            @block.tensor
            def _(pe):
                pe.wait_ge(p_in, 96)
                for b in range(NB):
                    for k in range(PK):
                        m = pe.transpose(bank(2 * (b // 2) + k)[:, (b % 2) * P:(b % 2 + 1) * P],
                                         p_sb[:, b, k * P:(k + 1) * P], ident)
                m.then_inc(pt, 1)
                pe.wait_ge(ptc, NB)
                pe.wait_ge(wp_in, 16)

                def pair(i, first):
                    for sl in range(2):
                        pe.wait_ge(w_in[sl], 16 * i + 16)
                        for b in range(NB):
                            n = (2 * i + sl) * NB + b
                            q = (sl * NB + b) % 2
                            if not (first and sl == 0):
                                pe.wait_ge(taken, n - (NB - 1))
                            for k in range(KT):
                                m = pe.matmul(bank(b), actT[:, k, b * P:(b + 1) * P], W[:, sl, k, :],
                                              start=(k == 0), stop=(k == KT - 1))
                            m.then_inc(mm, 1)
                            if not (first and sl == 0 and b < 2):
                                pe.wait_ge(added, n - 1)
                            for k in range(PK):
                                m = pe.matmul(bank(5 + q), pT[:, k, b * P:(b + 1) * P],
                                              wp[:, k, bass.ds((2 * i + sl) * CG, CG)], start=(k == 0), stop=(k == PK - 1))
                            m.then_inc(pj, 1)
                pair(0, True)
                with pe.Fori(1, DG // 2) as i:
                    pair(i, False)

            @block.scalar
            def _(act):
                def pair(i, first):
                    for sl in range(2):
                        for b in range(NB):
                            n = (2 * i + sl) * NB + b
                            q = (sl * NB + b) % 2
                            act.wait_ge(mm, n + 1)
                            if not (first and sl == 0 and b < 2):
                                act.wait_ge(added, n - 1)
                            act.activation(sig[:, q, :], bank(b), ACT.Sigmoid).then_inc(taken, 1)
                pair(0, True)
                with act.Fori(1, DG // 2) as i:
                    pair(i, False)
                for b in range(NB):
                    act.wait_ge(added, DG * NB)
                    if b:
                        act.wait_ge(mean, b)
                        act.wait_ge(squared, b)
                    act.activation(junk, h[:, b, :], ACT.Square, accum_out=stat[:, 0:1]).then_inc(squared, 1)
                    act.wait_ge(mean, b + 1)
                    if b:
                        act.wait_ge(chain, 2 * DG * NB + b)
                    act.activation(stat[:, 2:3], stat[:, 1:2], ACT.Sqrt).then_inc(rooted, 1)

            @block.vector
            def _(dve):
                ch = Chain(dve, chain)
                dve.wait_ge(pt, 1)
                for b in range(NB):
                    src = bank(2 * (b // 2), 1024, 2).rearrange("p (k c) -> p k c", k=PK)[:, :, (b % 2) * P:(b % 2 + 1) * P]
                    dve.tensor_copy(pT[:, :, b * P:(b + 1) * P], src).then_inc(ptc, 1)

                def pair(i):
                    ch.n, ch.off = 0, i * (2 * NB)
                    for sl in range(2):
                        for b in range(NB):
                            n = (2 * i + sl) * NB + b
                            q = (sl * NB + b) % 2
                            dve.wait_ge(taken, n + 1)
                            dve.wait_ge(pj, n + 1)
                            ch.then_wait(dve.tensor_tensor(sig[:, q, :], bank(5 + q), sig[:, q, :], ALU.mult))
                            hc = h[:, b, bass.ds((2 * i + sl) * CG, CG)]
                            dve.tensor_tensor(hc, hc, sig[:, q, :], ALU.add).then_inc(added, 1)
                with dve.Fori(0, DG // 2) as i:
                    pair(i)
                ch.n, ch.off = DG * NB, 0
                dve.sem_inc(chain, DG * NB)
                ch.n += DG * NB
                dve.wait_ge(g_in, 16)
                for b in range(NB):
                    dve.wait_ge(squared, b + 1)
                    if b:
                        dve.wait_ge(rooted, b)
                    dve.tensor_scalar(stat[:, 1:2], stat[:, 0:1], 1.0 / D, EPS, ALU.mult, ALU.add).then_inc(mean, 1)
                    dve.wait_ge(rooted, b + 1)
                    ch.then_wait(dve.reciprocal(stat[:, 3:4], stat[:, 2:3]))
                    if b >= 2:
                        dve.wait_ge(y_out[b % 2], 16 * (b // 2))
                    dve.scalar_tensor_tensor(out=xn[:, b % 2, :], in0=h[:, b, :], scalar=stat[:, 3:4],
                                             in1=gain[:, :], op0=ALU.mult, op1=ALU.mult).then_inc(y_ready, 1)


_INS = ["x_prompt", "x_sample", "p_prompt", "p_sample", "state_ret", "state_mlstm_C", "state_mlstm_n", "state_mlstm_m",
        "g_mix", "w_in", "b_gates", "g_ret", "g_mlstm", "w_out", "g_ffn", "w_peer_q", "peer_keys1", "peer_keys2",
        "peer_u", "peer_v", "g_ple", "w_ple_gate", "w_ple_proj", "g_final"]
_OUTS = [("y_prompt", (1, PROMPT, D)), ("y_sample", (1, SAMPLE, D)),
         ("ret_prompt", (1, 1, RH, RD, RD)), ("C_prompt", (1, 1, MH, MK, MV)), ("n_prompt", (1, 1, MH, MK)), ("m_prompt", (1, 1, MH)),
         ("ret_sample", (1, 1, RH, RD, RD)), ("C_sample", (1, 1, MH, MK, MV)), ("n_sample", (1, 1, MH, MK)), ("m_sample", (1, 1, MH))]


def kernel(**inputs):
    import concourse.bacc as bacc
    from concourse.bass_utils import run_bass_kernel_spmd

    nc = bacc.Bacc("TRN2", target_bir_lowering=False, num_devices=1)
    arrays, a, out = {}, {}, {}
    for name, value in [(n, inputs[n]) for n in _INS] + list(constants().items()):
        v = np.ascontiguousarray(value)
        arrays[f"in_{name}"] = v
        a[name] = nc.dram_tensor(f"in_{name}", v.shape, mybir.dt.from_np(v.dtype), kind="ExternalInput").ap()
    for name, shape in _OUTS:
        out[name] = nc.dram_tensor(f"out_{name}", shape, F32, kind="ExternalOutput").ap()
    build(nc, a, out)
    r = run_bass_kernel_spmd(nc, [arrays], core_ids=[0])
    return tuple(r.results[0][f"out_{name}"] for name, _ in _OUTS)
```

```python
from contextlib import ExitStack

import numpy as np

import concourse.bass as bass
from concourse import mybir

F32 = mybir.dt.float32
U32 = mybir.dt.uint32
ALU = mybir.AluOpType
ACT = mybir.ActivationFunctionType
AX_X = mybir.AxisListType.X

P = 128
D = 2048
KT = D // P
PROMPT, SAMPLE = 512, 64
NB = PROMPT // P + 1
SB = NB - 1
T = NB * P
PAST = 256
EPS = 1e-6
RH, RD = 8, 128
MH, MK, MV = 4, 128, 256
RW, MW = RH * RD, MH * MV
ZC = 4 * RW + 2 * MH * MK + 2 * MW
Z_RQ, Z_RK, Z_RV, Z_RG = 0, RW, 2 * RW, 3 * RW
Z_MQ = 4 * RW
Z_MK = Z_MQ + MH * MK
Z_MV = Z_MK + MH * MK
Z_MO = Z_MV + MW
GROUPS = [[0, 1], [2, 3, SB]]
MAXB = 3
TG = MAXB * P
WQ = 4
KQ = KT // WQ
CG = 512
ZG = ZC // CG
DG = D // CG
EH, EQ, NKEY, TOPK = 8, 256, 128, 16
HH = 2 * EH
NE = NKEY * NKEY
NPICK = EH * TOPK
PLE = 256
GRP = 8
PAIR_ROWS = [(0, 1, 16), (1, 1, 8), (2, 1, 5), (3, 1, 4), (4, 1, 3), (5, 3, 2), (8, 8, 1)]
NC = sum(n * w for _, n, w in PAIR_ROWS)
LOWEST = -3.0e38
FAR = 1.0e30


def constants():
    half = RD // 2
    inv = np.float32(10000.0) ** (-np.arange(half, dtype=np.float32) / np.float32(half))
    pos = np.concatenate([np.arange(PROMPT), PAST + np.arange(SAMPLE), PAST + np.arange(SAMPLE)]).astype(np.float32)
    ang = (pos[:, None] * inv[None, :]).astype(np.float32)
    rope = np.stack([np.cos(ang), np.sin(ang)], 1).astype(np.float32)
    rope = rope.reshape(NB, P, 2 * half).transpose(1, 0, 2).reshape(P, NB * 2 * half)
    lg = np.log(1.0 - 2.0 ** (-5.0 - np.arange(RH)))
    scale = RD ** -0.5
    i = np.arange(P)
    tabs = []
    for n in (P, SAMPLE):
        diff = i[None, :] - i[:, None]
        keep = (diff >= 0) & (i[:, None] < n)
        dec = np.where(keep[:, None, :], np.exp(np.where(keep, diff, 0)[:, None, :] * lg[None, :, None]), 0) * scale
        kd = np.where(i[:, None] < n, np.exp((n - 1.0 - np.minimum(i, n - 1))[:, None] * lg[None, :]), 0) * scale
        gl = np.broadcast_to(np.exp(n * lg)[None, :], (P, RH))
        qd = np.exp((i[:, None] + 1.0) * lg[None, :])
        tabs.append(np.concatenate([dec.reshape(P, RH * P), kd, gl, qd], 1))
    far = np.where(i[:, None] <= i[None, :], 0.0, FAR)
    ident = np.eye(P)
    fold = (i[:, None] % SAMPLE == i[None, :] % SAMPLE)
    row = np.concatenate([far, ident, fold.astype(float), np.broadcast_to(np.arange(NC), (P, NC))], 1)
    return {
        "c_rope": rope,
        "c_decay": np.stack(tabs).astype(np.float32),
        "c_misc": row.astype(np.float32),
    }


class Machine:
    pass


class Gate:

    def __init__(self, nc, eng, name):
        self.eng, self.sem = eng, nc.alloc_semaphore(name)

    def close(self):
        self.eng.sem_inc(self.sem, 1)


class Chain:

    def __init__(self, eng, sem):
        self.eng, self.sem, self.n, self.off = eng, sem, 0, 0

    def then_wait(self, ins):
        self.n += 1
        ins.then_inc(self.sem, 1)
        self.eng.wait_ge(self.sem, self.off + self.n)


def build(nc, a, out):
    with ExitStack() as ctx:
        def sb(name, shape, dt=F32):
            return ctx.enter_context(nc.sbuf_tensor(name, shape, dt))

        actT = sb("actT", [P, KT * TG])
        h1 = sb("h1", [P, len(GROUPS[0]), D])
        h2 = sb("h2", [P, MAXB, D])
        ring = sb("ring", [P, 8 * D])
        W = sb("W", [P, KT, CG])
        gain = sb("gain", [P, D])
        xn = sb("xn", [P, 2, D])
        stage = sb("stage", [P, NB * CG])
        misc = sb("misc", [P, 3 * P + NC])
        stat = sb("stat", [P, 80])
        eidx = sb("eidx", [P, MAXB, NPICK], U32)
        gate = sb("gate", [P, MAXB, NPICK])
        cols = sb("cols", [P, MAXB, 4, MH])
        cdbc = sb("cdbc", [P, MAXB, MH])
        mrows = sb("mrows", [MH, TG])
        Cx = sb("Cx", [P, MH, MV + 1])
        tv = sb("tv", [P, MAXB, TOPK])
        tx = sb("tx", [P, MAXB, TOPK], U32)
        besti = sb("besti", [P, EH, TOPK], U32)
        uix = sb("uix", [P, 2, GRP], U32)
        vix = sb("vix", [P, 2, GRP], U32)
        dots = sb("dots", [P, 2, GRP])
        gel = sb("gel", [P, 2, GRP])
        wts = sb("wts", [P, 2, GRP])
        psum = ctx.enter_context(nc.psum_tensor("psum", [P, 8, 512], F32))

        far = misc[:, 0:P]
        ident = misc[:, P:2 * P]
        fold = misc[:, 2 * P:3 * P]
        iota = misc[:, 3 * P:]
        aT = actT[:, :].rearrange("p (k t) -> p k t", k=KT)
        zd = nc.dram_tensor("z_scratch", (NB, P, ZC), F32, kind="Internal").ap()
        s_keep = nc.dram_tensor("s_scratch", (P, RW), F32, kind="Internal").ap()
        c_keep = nc.dram_tensor("c_scratch", (P, MH * (MV + 1)), F32, kind="Internal").ap()

        def bank(n, width=512, banks=1):
            v = psum[:, n:n + banks, :].rearrange("p b c -> p (b c)")
            return v[:, 0:width]

        def row_bcast(ap1d):
            return ap1d.rearrange("(o d) -> o d", o=1).to_broadcast([P, ap1d.shape[0]])

        hs = (h1, h2)
        x_in, misc_in = nc.alloc_semaphore("x_in"), nc.alloc_semaphore("misc_in")
        x_loads = [0]

        def load_x(eng, grp):
            for j, b in enumerate(GROUPS[grp]):
                if b < SB:
                    eng.dma_start(hs[grp][:, j, :], a["x_prompt"][0, b * P:(b + 1) * P, :]).then_inc(x_in, 16)
                    x_loads[0] += 1
                else:
                    for c in range(2):
                        eng.dma_start(hs[grp][c * SAMPLE:(c + 1) * SAMPLE, j, :], a["x_sample"][0]).then_inc(x_in, 16)
                        x_loads[0] += 1

        m = Machine()
        m.nc, m.a, m.out, m.aT, m.h, m.ring = nc, a, out, aT, hs, ring
        m.W, m.gain, m.xn, m.stage, m.stat, m.eidx = W, gain, xn, stage, stat, eidx
        m.gate, m.cols, m.cdbc, m.mrows, m.far, m.ident = gate, cols, cdbc, mrows, far, ident
        m.fold, m.iota, m.zd, m.s_keep, m.c_keep, m.bank = fold, iota, zd, s_keep, c_keep, bank
        m.row_bcast, m.Cx, m.tv, m.tx, m.besti, m.uix = row_bcast, Cx, tv, tx, besti, uix
        m.vix, m.dots, m.gel, m.wts = vix, dots, gel, wts
        norm = make_norm_transpose(m)
        weights = Weights(nc, W)
        project = Project(m, weights)
        rows = make_rows(m)
        mixers = make_mixers(m)
        route = make_route(m, weights)
        gather = make_gather(m)
        embed = Embeddings(m, weights)

        def norm_stage(grp, g, from_x=False):
            with nc.Block() as block:
                def loads(sp, gin):
                    if from_x and grp == 0:
                        sp.dma_start(misc[:, :], a["c_misc"]).then_inc(misc_in, 16)
                    sp.dma_start(gain[:, :], row_bcast(a[g][0])).then_inc(gin, 16)
                    if from_x:
                        load_x(sp, grp)
                norm(block, grp, loads, (lambda eng: eng.wait_ge(x_in, 16 * x_loads[0])) if from_x else None, misc_in)

        o_mm, o_added = nc.alloc_semaphore("o_mm"), nc.alloc_semaphore("o_added")

        def project_out(grp):
            n = len(GROUPS[grp])
            base = grp * DG * len(GROUPS[0])
            with nc.Block() as block:
                @block.sync
                def _(sp):
                    load_x(sp, grp)
                    weights.load(sp, a["w_out"][0], DG)

                @block.tensor
                def _(pe):
                    product_groups(pe, aT, weights, bank, n, DG, o_mm, o_added, base)

                @block.vector
                def _(dve):
                    dve.wait_ge(x_in, 16 * x_loads[0])
                    with dve.Fori(0, DG // 2) as i:
                        for s in range(2):
                            for j in range(n):
                                k = (2 * i + s) * n + (base + j + 1)
                                dve.wait_ge(o_mm, k)
                                hc = hs[grp][:, j, bass.ds((2 * i + s) * CG, CG)]
                                dve.tensor_tensor(hc, bank(3 * s + j), hc, ALU.add).then_inc(o_added, 1)
            weights.done(DG)

        norm_stage(0, "g_mix", True)
        project.alone(0)
        rows(0)
        mixers(0)
        project_out(0)
        norm_stage(0, "g_ffn")
        route(0)
        norm_stage(1, "g_mix", True)
        with nc.Block() as block:
            gather(block, 0, [0], project.beside(1))
        rows(1)
        mixers(1)
        with nc.Block() as block:
            gather(block, 0, [1])
        project_out(1)
        norm_stage(1, "g_ffn")
        route(1)
        norm_stage(0, "g_ple")
        with nc.Block() as block:
            gather(block, 1, [0, 1, 2], embed.beside(0))
        norm_stage(1, "g_ple")
        embed.alone(1)


def make_norm_transpose(m):
    nc, xn, gain, stat, bank, aT = m.nc, m.xn, m.gain, m.stat, m.bank, m.aT
    squared, mean, rooted, normed, turned, copied_a, copied_v, chain, gin = (
        nc.alloc_semaphore("n_" + x) for x in
        ("squared", "mean", "rooted", "normed", "turned", "copied_a", "copied_v", "dve", "gain"))
    ssq, ms, rt, rs = (stat[:, 2 * i:2 * i + 2] for i in range(4))
    junk = m.stage[:, 0:D]
    used = {"uses": 0, "blocks": 0}

    def run(block, grp, loads, inputs, misc_in):
        h, t0, use = m.h[grp], used["blocks"], used["uses"]
        todo = [(j, t0 + j, (t0 + j) % 2) for j in range(len(GROUPS[grp]))]
        used["blocks"] += len(todo)
        used["uses"] += 1

        @block.sync
        def _(sp):
            loads(sp, gin)

        @block.scalar
        def _(act):
            if inputs is not None:
                inputs(act)
            for j, t, r in todo:
                if t:
                    act.wait_ge(squared, t)
                    act.wait_ge(mean, t)
                act.activation(junk, h[:, j, :], ACT.Square, accum_out=ssq[:, r:r + 1]).then_inc(squared, 1)
                act.wait_ge(mean, t + 1)
                act.activation(rt[:, r:r + 1], ms[:, r:r + 1], ACT.Sqrt).then_inc(rooted, 1)
                for q in range(2):
                    act.wait_ge(turned, 4 * t + q + 1)
                    act.copy(aT[:, 4 * q:4 * q + 4, j * P:(j + 1) * P],
                             bank(4 * r + q).rearrange("p (k l) -> p k l", k=4)).then_inc(copied_a, 1)

        @block.vector
        def _(dve):
            dve.wait_ge(gin, 16 * (use + 1))
            for j, t, r in todo:
                dve.wait_ge(squared, t + 1)
                dve.tensor_scalar(ms[:, r:r + 1], ssq[:, r:r + 1], 1.0 / D, EPS, ALU.mult, ALU.add).then_inc(mean, 1)
                dve.wait_ge(rooted, t + 1)
                dve.reciprocal(rs[:, r:r + 1], rt[:, r:r + 1]).then_inc(chain, 1)
                dve.wait_ge(chain, t + 1)
                if t >= 2:
                    dve.wait_ge(turned, 4 * (t - 1))
                dve.scalar_tensor_tensor(out=xn[:, r, :], in0=h[:, j, :], scalar=rs[:, r:r + 1],
                                         in1=gain[:, :], op0=ALU.mult, op1=ALU.mult).then_inc(normed, 1)
                for q in range(2, 4):
                    dve.wait_ge(turned, 4 * t + q + 1)
                    dve.tensor_copy(aT[:, 4 * q:4 * q + 4, j * P:(j + 1) * P],
                                    bank(4 * r + q).rearrange("p (k l) -> p k l", k=4)).then_inc(copied_v, 1)

        @block.tensor
        def _(pe):
            pe.wait_ge(misc_in, 16)
            for j, t, r in todo:
                pe.wait_ge(normed, t + 1)
                if t >= 2:
                    pe.wait_ge(copied_a, 2 * (t - 1))
                    pe.wait_ge(copied_v, 2 * (t - 1))
                for q in range(4):
                    for i in range(4):
                        k = 4 * q + i
                        ins = pe.transpose(bank(4 * r + q)[:, i * P:(i + 1) * P], xn[:, r, k * P:(k + 1) * P], m.ident)
                    ins.then_inc(turned, 1)
    return run


class Weights:

    def __init__(self, nc, W):
        self.W, self.g0 = W, 0
        self.landed = [nc.alloc_semaphore(f"w_landed{q}") for q in range(WQ)]
        self.used = nc.alloc_semaphore("w_used")

    def load(self, eng, w, groups):
        wv = w.rearrange("(k p) c -> p k c", p=P)

        def part(g, q):
            ks = slice(q * KQ, (q + 1) * KQ)
            eng.dma_start(self.W[:, ks, :], wv[:, ks, bass.ds(g * CG, CG)]).then_inc(self.landed[q], 16)
        for q in range(WQ):
            part(0, q)
        with eng.Fori(1, groups) as g:
            for q in range(WQ):
                eng.wait_ge(self.used, WQ * g + (WQ * (self.g0 - 1) + q + 1))
                part(g, q)

    def wait(self, pe, g, q):
        pe.wait_ge(self.landed[q], 16 * g + 16 * (self.g0 + 1))

    def done(self, groups):
        self.g0 += groups


def product_groups(pe, aT, weights, bank, n, groups, mm, taken, base, after=None):
    def pair(i, first):
        for s in range(2):
            for q in range(WQ):
                weights.wait(pe, 2 * i + s, q)
                for j in range(n):
                    if q == 0 and not first:
                        pe.wait_ge(taken, (2 * i + (s - 2)) * n + (base + j + 1))
                    for k in range(q * KQ, (q + 1) * KQ):
                        ins = pe.matmul(bank(3 * s + j), aT[:, k, j * P:(j + 1) * P], weights.W[:, k, :],
                                        start=(k == 0), stop=(k == KT - 1))
                    if q == WQ - 1:
                        ins.then_inc(mm, 1)
                if q < WQ - 1:
                    ins.then_inc(weights.used, 1)
            pe.wait_ge(mm, (2 * i + (s + 1)) * n + base)
            pe.sem_inc(weights.used, 1)
            if after:
                after(i, s, first)
    pair(0, True)
    with pe.Fori(1, groups // 2) as i:
        pair(i, False)


class Project:

    def __init__(self, m, weights):
        self.m, self.weights = m, weights
        sem = lambda name: m.nc.alloc_semaphore("p_" + name)
        self.mm, self.taken, self.gate_mm, self.gate_taken = sem("mm"), sem("taken"), sem("gate_mm"), sem("gate_taken")
        self.stored = [sem(f"stored{j}") for j in range(MAXB)]
        self.small_in = sem("gate_weights_in")

    def at(self, grp):
        self.grp, self.n = grp, len(GROUPS[grp])
        self.base = grp * ZG * len(GROUPS[0])
        self.bias = self.m.stat[0:MH, 74:76]
        self.wg = self.m.xn[:, 1, 0:KT * 2 * MH].rearrange("p (k g) -> p k g", k=KT)

    def sync(self, sp):
        m = self.m
        sp.dma_start(self.wg, m.a["w_in"][0].rearrange("(k p) c -> p k c", p=P)[:, :, ZC:ZC + 2 * MH]
                     ).then_inc(self.small_in, 16)
        with m.nc.allow_non_contiguous_dma(reason="eight biases"):
            sp.dma_start(self.bias, m.a["b_gates"][0].rearrange("(g h) -> h g", h=MH)).then_inc(self.small_in, 16)
        self.weights.load(sp, m.a["w_in"][0], ZG)

    def tensor(self, pe):
        m, n = self.m, self.n
        pe.wait_ge(self.small_in, 32 * (self.grp + 1))
        for g in range(2):
            for k in range(KT):
                ins = pe.matmul(m.bank(6 + g)[0:MH, 0:n * P], self.wg[:, k, g * MH:(g + 1) * MH],
                                m.aT[:, k, 0:n * P], start=(k == 0), stop=(k == KT - 1))
            ins.then_inc(self.gate_mm, 1)
        product_groups(pe, m.aT, self.weights, m.bank, n, ZG, self.mm, self.taken, self.base)

    def take_gates(self, act):
        m, n = self.m, self.n
        for g in range(2):
            act.wait_ge(self.gate_mm, 2 * self.grp + g + 1)
            act.activation(m.stage[0:MH, MAXB * CG + g * TG:MAXB * CG + g * TG + n * P], m.bank(6 + g)[0:MH, 0:n * P],
                           ACT.Identity, bias=self.bias[:, g:g + 1]).then_inc(self.gate_taken, 1)

    def take(self, act, g, s, first):
        m, n = self.m, self.n
        g_before = 0 if self.grp == 0 else ZG
        for j in range(n):
            act.wait_ge(self.mm, g * n + (self.base + j + 1))
            if not first:
                act.wait_ge(self.stored[j], 16 * g + 16 * (g_before if j < len(GROUPS[0]) else 0))
            act.copy(m.stage[:, j * CG:(j + 1) * CG], m.bank(3 * s + j)).then_inc(self.taken, 1)
            act.wait_ge(self.taken, g * n + (self.base + j + 1))
            act.dma_start(m.zd[GROUPS[self.grp][j], :, bass.ds(g * CG, CG)], m.stage[:, j * CG:(j + 1) * CG]
                          ).then_inc(self.stored[j], 16)

    def stored_all(self, act):
        for j in range(self.n):
            act.wait_ge(self.stored[j], 16 * ZG * (2 if self.grp and j < len(GROUPS[0]) else 1))

    def alone(self, grp):
        self.at(grp)
        with self.m.nc.Block() as block:
            block.sync(self.sync)
            block.tensor(self.tensor)

            @block.scalar
            def _(act):
                self.take_gates(act)
                self.take(act, 0, 0, True)
                self.take(act, 1, 1, False)
                with act.Fori(1, ZG // 2) as i:
                    for s in range(2):
                        self.take(act, 2 * i + s, s, False)
                self.stored_all(act)
        self.weights.done(ZG)

    def beside(self, grp):
        self.at(grp)
        return self

    hooked_pairs = ZG // 2

    def act_slot(self, act, i, r):
        if isinstance(i, int):
            g = 2 * i + r - 1
            if g < 0:
                self.take_gates(act)
            elif g < ZG:
                self.take(act, g, g % 2, g == 0)
                if g == ZG - 1:
                    self.stored_all(act)
        else:
            self.take(act, 2 * i + (r - 1), (r + 1) % 2, False)

    def dve_slot(self, dve, i, r):
        pass

    def open(self, dve):
        pass

    def end(self):
        self.weights.done(ZG)


def make_rows(m):
    nc, a, out, bank, cols, cdbc = m.nc, m.a, m.out, m.bank, m.cols, m.cdbc
    sem = lambda name: nc.alloc_semaphore("s_" + name)
    dve_row, act_row, mm, chain, m_io = sem("dve_row"), sem("act_row"), sem("mm"), sem("dve"), sem("m_io")
    used = {"chain": 0, "io": 0}

    def run(grp):
        blks = GROUPS[grp]
        n = len(blks)
        T = n * P
        xrow = m.xn[0:MH, :, :].rearrange("p a d -> p (a d)")
        bs, am, tmp = (xrow[:, i * TG:i * TG + T] for i in range(3))
        ig, fg = (m.stage[0:MH, MAXB * CG + g * TG:MAXB * CG + g * TG + T] for g in range(2))
        mx = m.mrows[:, 0:T]
        grow = m.gain[0:MH, :]
        ex = grow[:, 0:3 * TG]
        exs = [ex[:, i * T:(i + 1) * T] for i in range(3)]
        mprev = m.stat[0:MH, 76:76 + n]
        kept = m.stat[0:MH, 72:74]
        cde = grow[:, 3 * TG:3 * TG + n]
        cdd = grow[:, 3 * TG + 16:3 * TG + 16 + n * MH].rearrange("p (b h) -> p b h", b=n)
        onesrow = grow[:, 3 * TG + 40:3 * TG + 40 + P]
        v3 = lambda ap: ap.rearrange("p (b l) -> p b l", b=n)
        io0 = used["io"]
        with nc.Block() as block:
            @block.sync
            def _(sp):
                if grp:
                    with nc.allow_non_contiguous_dma(reason="four numbers"):
                        sp.dma_start(mprev[:, n - 1:n], a["state_mlstm_m"][0].rearrange("o h -> h o")).then_inc(m_io, 16)
                        sp.wait_ge(dve_row, 3 * grp + 3)
                        sp.dma_start(out["m_prompt"][0].rearrange("o h -> h o"), kept[:, 0:1]).then_inc(m_io, 16)
                        sp.dma_start(out["m_sample"][0].rearrange("o h -> h o"), kept[:, 1:2]).then_inc(m_io, 16)
                        sp.wait_ge(m_io, 48)

            @block.tensor
            def _(pe):
                pe.wait_ge(dve_row, 3 * grp + 3)
                for j in range(n):
                    for q, src in enumerate([am] + exs):
                        c = (j * 4 + q) * MH
                        pe.transpose(bank(5)[:, c:c + MH], src[:, j * P:(j + 1) * P], m.ident[0:MH, 0:MH])
                pe.matmul(bank(6)[:, 0:n * MH], onesrow, cdd, start=True, stop=True).then_inc(mm, 1)

            @block.scalar
            def _(act):
                act.wait_ge(dve_row, 3 * grp + 1)
                act.activation(tmp, tmp, ACT.Exp).then_inc(act_row, 1)
                act.wait_ge(act_row, 4 * grp + 1)
                act.activation(tmp, tmp, ACT.Ln, bias=1.0).then_inc(act_row, 1)
                act.wait_ge(dve_row, 3 * grp + 2)
                act.activation(ex[:, 0:3 * T], ex[:, 0:3 * T], ACT.Exp).then_inc(act_row, 1)
                act.activation(cde, cde, ACT.Exp).then_inc(act_row, 1)

            @block.vector
            def _(dve):
                ch = Chain(dve, chain)
                ch.n = used["chain"]
                do = ch.then_wait
                do(dve.memset(onesrow, 1.0))
                if grp == 0:
                    do(dve.memset(mprev[:, 0:1], 0.0))
                else:
                    do(dve.tensor_copy(mprev[:, 0:1], kept[:, 0:1]))
                    dve.wait_ge(m_io, 16)
                dve.scalar_tensor_tensor(out=tmp, in0=fg, scalar=-1.0, in1=fg, op0=ALU.mult, op1=ALU.min).then_inc(dve_row, 1)
                do(dve.tensor_scalar(fg, fg, 0.0, None, ALU.min))
                dve.wait_ge(act_row, 4 * grp + 2)
                do(dve.tensor_tensor(fg, fg, tmp, ALU.subtract))
                if grp:
                    do(dve.memset(fg[:, T - SAMPLE:T], 0.0))
                for j in range(n):
                    do(dve.tensor_tensor_scan(bs[:, j * P:(j + 1) * P], fg[:, j * P:(j + 1) * P],
                                              fg[:, j * P:(j + 1) * P], 0.0, ALU.add, ALU.bypass))
                do(dve.tensor_tensor(am, ig, bs, ALU.subtract))
                if grp:
                    do(dve.memset(am[:, T - SAMPLE:T], -FAR))
                for j in range(n):
                    am_b, mx_b = am[:, j * P:(j + 1) * P], mx[:, j * P:(j + 1) * P]
                    do(dve.tensor_tensor_scan(mx_b, am_b, am_b, mprev[:, j:j + 1], ALU.max, ALU.bypass))
                    to = [kept[:, 1:2]] if blks[j] == SB else [kept[:, 0:1]]
                    if blks[j] != SB and j + 1 < n and blks[j + 1] != SB:
                        to.append(mprev[:, j + 1:j + 2])
                    for dst in to:
                        do(dve.tensor_tensor(dst, bs[:, (j + 1) * P - 1:(j + 1) * P], mx[:, (j + 1) * P - 1:(j + 1) * P], ALU.add))
                last = v3(mx)[:, :, P - 1:P]
                prev = mprev.rearrange("p (b o) -> p b o", o=1)
                do(dve.tensor_tensor(v3(exs[0]), prev.to_broadcast([MH, n, P]), v3(mx), ALU.subtract))
                do(dve.scalar_tensor_tensor(out=exs[1], in0=bs, scalar=-1.0, in1=mx, op0=ALU.mult, op1=ALU.subtract))
                do(dve.tensor_tensor(v3(exs[2]), v3(am), last.to_broadcast([MH, n, P]), ALU.subtract))
                do(dve.tensor_tensor(cde.rearrange("p (b o) -> p b o", o=1), prev, last, ALU.subtract))
                dve.sem_inc(dve_row, 1)
                dve.wait_ge(act_row, 4 * grp + 4)
                for hh in range(MH):
                    do(dve.tensor_scalar(cdd[:, :, hh], cde, m.ident[0:MH, hh:hh + 1], None, ALU.mult))
                dve.sem_inc(dve_row, 1)
                dve.wait_ge(mm, grp + 1)
                do(dve.tensor_copy(cols[:, 0:n, :, :].rearrange("p b q h -> p (b q h)"), bank(5)[:, 0:n * 4 * MH]))
                do(dve.tensor_scalar(cols[:, 0:n, 3, :], cols[:, 0:n, 3, :], MK ** -0.5, None, ALU.mult))
                do(dve.tensor_copy(cdbc[:, 0:n, :].rearrange("p b h -> p (b h)"), bank(6)[:, 0:n * MH]))
                used["chain"] = ch.n
    return run


def make_mixers(m):
    nc, a, out, bank, zd = m.nc, m.a, m.out, m.bank, m.zd
    aT, far, ident, cols, cdbc, mrows, gain, xn, stage, stat = (
        m.aT, m.far, m.ident, m.cols, m.cdbc, m.mrows, m.gain, m.xn, m.stage, m.stat)
    with ExitStack() as s:
        sem = lambda name: nc.alloc_semaphore("m_" + name)
        room = {"h": (m.h[1][:, :, :].rearrange("p b d -> p (b d)"), 0), "w": (m.W[:, :, :].rearrange("p k c -> p (k c)"), 0)}

        def carve(of, n, *dims):
            v, at = room[of]
            room[of] = (v, at + n)
            assert at + n <= v.shape[1]
            v = v[:, at:at + n]
            return v.rearrange("p (a b) -> p a b", a=dims[0]) if dims else v
        zb = [m.ring[:, i * ZC:(i + 1) * ZC] for i in range(2)]
        qkT = carve("h", 24 * P, 24, P)
        rk = carve("h", 2 * RW)
        tv = carve("w", 2 * RW)
        sT = carve("h", RW, RH, P)
        kdec = xn[:, 0, 0:RW].rearrange("p (h d) -> p h d", h=RH)
        dw = xn[:, 0, RW:RW + 512]
        smT = xn[:, 0, RW + 512:2 * RW].rearrange("p (h l) -> p h l", h=MH)
        obuf = xn[:, 1, :]
        gateb = stage[:, 0:2 * RW]
        wk = stage[:, 2 * RW:2 * RW + 512].rearrange("p (h d) -> p h d", h=MH)
        tv2 = m.ring[:, 2 * ZC:2 * ZC + 2 * RW]
        vext = carve("w", MH * (MV + 1), MH, MV + 1)
        S = carve("w", RW, RH, RD)
        Sd = carve("w", RW, RH, RD)
        Cx = m.Cx
        Cd = carve("w", MH * (MV + 1), MH, MV + 1)
        dec = carve("w", RH * P + 3 * RH)
        rope = carve("w", MAXB * RD, MAXB, RD)
        st = stat
        half = RD // 2

        const_in, st_in, z_in = sem("const"), sem("state_in"), [sem("z0"), sem("z1")]
        rot_v, rot_p, tq, te = sem("rot_v"), sem("rot_p"), sem("turned"), sem("turned_copied")
        qd_done, kd_done, wk_done, vx_done = sem("qdec"), sem("kdec"), sem("wkey"), sem("vext")
        pmb, mb_read, dwx, dwe = sem("maxima"), sem("maxima_read"), sem("dw_exponents"), sem("dw")
        ps_r, ps_m, s_r, s_m = sem("ps_ret"), sem("ps_ml"), sem("scores_ret"), sem("scores_ml")
        pu_r, pu_m, sd, cd = sem("upd_ret"), sem("upd_ml"), sem("s_decayed"), sem("c_decayed")
        su, cu = sem("s_updated"), sem("c_updated")
        po_r, po_m, po_i = sem("out_ret"), sem("out_ml"), sem("out_inter")
        ne, nr, ni = sem("inter_scaled"), sem("ret_read"), sem("num_read")
        sg, gg = sem("gates_sig"), sem("gates_gain")
        sq, rts, msr, mixd = sem("squares"), sem("roots"), sem("means"), sem("mixed")
        pt, ptc = sem("mix_turned"), sem("mix_copied")
        st_out, reset = sem("state_out"), sem("state_reset")
        ch_v, ch_p = sem("dve"), sem("pool")
        dec_in = sem("dec_in")
        qk16 = lambda z: z[:, 0:2 * RW].rearrange("p (h t e) -> p h t e", h=2 * RH, t=2)

        n_pool, n_dve = 7, 26

        def cs(j, q):
            return rope[:, j:j + 1, q * half:(q + 1) * half].to_broadcast([P, 2 * RH, half])

        vx_one, ptv, qi, iq = sem("vext_one"), sem("mix_copied_v"), sem("ret_inter"), sem("ret_inter_scaled")

        def mix_copy(copy, q, j, sample, done):
            src = bank(2 + q).rearrange("p (k l) -> p k l", k=4)
            to = aT[:, 4 * q:4 * q + 4, j * P:(j + 1) * P]
            if sample:
                copy(to[:, :, 0:SAMPLE], src[:, :, 0:SAMPLE])
                copy(to[:, :, SAMPLE:P], src[:, :, 0:SAMPLE]).then_inc(done, 1)
            else:
                copy(to, src).then_inc(done, 1)

        def z_wait(eng, t):
            eng.wait_ge(z_in[t % 2], 16 * (t // 2 + 1))

        def run(grp):
            blks = [(sum(map(len, GROUPS[:grp])) + j, j, b, b == SB) for j, b in enumerate(GROUPS[grp])]

            def blocks(eng, body):
                for t, j, b, sample in blks:
                    body(t, j, t % 2, sample)
            with nc.Block() as block:
                stage_of(block, grp, blks, blocks)

        def stage_of(block, grp, blks, blocks):
            @block.sync
            def _(sp):
                t0 = blks[0][0]
                for t, j, b, sample in blks[:2]:
                    sp.dma_start(zb[t % 2], zd[b]).then_inc(z_in[t % 2], 16)
                sp.dma_start(rope[:, 0:len(blks), :].rearrange("p b r -> p (b r)"),
                             a["c_rope"][:, t0 * RD:(t0 + len(blks)) * RD]).then_inc(const_in, 16)
                sp.dma_start(gain[:, 0:RW], a["g_ret"][0:1, :].to_broadcast([P, RW])).then_inc(const_in, 16)
                sp.dma_start(gain[:, RW:], a["g_mlstm"][0:1, :].to_broadcast([P, MW])).then_inc(const_in, 16)
                sp.dma_start(dec, a["c_decay"][0]).then_inc(dec_in, 16)
                cx_all = Cx[:, :, :].rearrange("p h v -> p (h v)")
                s_all = S.rearrange("p h v -> p (h v)")
                if grp == 0:
                    sp.wait_ge(su, 2)
                    sp.wait_ge(cu, 2)
                    sp.dma_start(m.s_keep, s_all).then_inc(st_out, 16)
                    sp.dma_start(m.c_keep, cx_all).then_inc(st_out, 16)
                    sp.wait_ge(st_out, 32)
                    return
                sp.dma_start(s_all, m.s_keep).then_inc(st_in, 16)
                sp.dma_start(cx_all, m.c_keep).then_inc(st_in, 16)
                sp.wait_ge(pt, 4 * 3)
                sp.dma_start(zb[0], zd[SB]).then_inc(z_in[0], 16)

                def states(tag):
                    sp.dma_start(out["ret_" + tag][0, 0].rearrange("h k v -> k h v"), S).then_inc(st_out, 16)
                    sp.dma_start(out["C_" + tag][0, 0].rearrange("h k v -> k h v"), Cx[:, :, 0:MV]).then_inc(st_out, 16)
                    with nc.allow_non_contiguous_dma(reason="one normaliser column"):
                        sp.dma_start(out["n_" + tag][0, 0].rearrange("h k -> k h"), Cx[:, :, MV]).then_inc(st_out, 16)
                sp.wait_ge(su, 4)
                sp.wait_ge(cu, 4)
                states("prompt")
                sp.wait_ge(s_r, 4)
                sp.wait_ge(kd_done, 4)
                sp.wait_ge(sd, 4)
                sp.wait_ge(iq, 4)
                sp.dma_start(dec, a["c_decay"][1]).then_inc(dec_in, 16)
                sp.wait_ge(st_out, 32 + 48)
                sp.wait_ge(po_i, 4)
                sp.dma_start(S, a["state_ret"][0, 0].rearrange("h k v -> k h v")).then_inc(st_in, 16)
                sp.dma_start(Cx[:, :, 0:MV], a["state_mlstm_C"][0, 0].rearrange("h k v -> k h v")).then_inc(st_in, 16)
                with nc.allow_non_contiguous_dma(reason="one normaliser column"):
                    sp.dma_start(Cx[:, :, MV], a["state_mlstm_n"][0, 0].rearrange("h k -> k h")).then_inc(st_in, 16)
                sp.wait_ge(su, NB)
                sp.wait_ge(cu, NB)
                states("sample")
                sp.wait_ge(st_out, 32 + 96)

            def state_wait(eng, t):
                if t == 0:
                    eng.wait_ge(reset, 2)
                elif t == 2:
                    eng.wait_ge(st_in, 32)
                elif t == 4:
                    eng.wait_ge(st_in, 32 + 48)
                else:
                    eng.wait_ge(su, t)
                    eng.wait_ge(cu, t)

            def dec_wait(eng, t):
                eng.wait_ge(dec_in, 16 * (1 if t < 2 else 2 if t < 4 else 3))

            @block.gpsimd
            def _(pool):
                ch = Chain(pool, ch_p)
                pool.wait_ge(const_in, 48 * (grp + 1))

                def body(t, j, r, sample):
                    ch.n, ch.off = 0, t * n_pool
                    do = ch.then_wait
                    z_wait(pool, t)
                    x = qk16(zb[r])
                    if t:
                        pool.wait_ge(tq, 6 * t)
                        pool.wait_ge(msr, t)
                        pool.wait_ge(kd_done, t)
                    t1 = tv2[:, 0:RW].rearrange("p (h e) -> p h e", e=half)
                    t2 = tv2[:, RW:].rearrange("p (h e) -> p h e", e=half)
                    do(pool.tensor_tensor(t1, x[:, :, 0, :], cs(j, 1), ALU.mult))
                    do(pool.tensor_tensor(t2, x[:, :, 1, :], cs(j, 0), ALU.mult))
                    pool.tensor_tensor(qk16(rk)[:, :, 1, :], t1, t2, ALU.add).then_inc(rot_p, 1)
                    pool.wait_ge(rot_p, t + 1)
                    pool.wait_ge(rot_v, t + 1)
                    dec_wait(pool, t)
                    if t:
                        pool.wait_ge(pu_r, t)
                        pool.wait_ge(pu_m, t)
                    kd = dec[:, RH * P:RH * P + RH].rearrange("p (h o) -> p h o", o=1)
                    pool.tensor_tensor(kdec, rk[:, RW:].rearrange("p (h d) -> p h d", h=RH),
                                       kd.to_broadcast([P, RH, RD]), ALU.mult).then_inc(kd_done, 1)
                    wc = cols[:, j, 3, :].rearrange("p (h o) -> p h o", o=1)
                    pool.tensor_tensor(wk, zb[r][:, Z_MK:Z_MV].rearrange("p (h d) -> p h d", h=MH),
                                       wc.to_broadcast([P, MH, MK]), ALU.mult).then_inc(wk_done, 1)
                    state_wait(pool, t)
                    gl = dec[:, RH * P + RH:RH * P + 2 * RH].rearrange("p (h o) -> p h o", o=1)
                    pool.tensor_tensor(Sd, S, gl.to_broadcast([P, RH, RD]), ALU.mult).then_inc(sd, 1)
                    cb = cdbc[:, j, :].rearrange("p (h o) -> p h o", o=1)
                    pool.tensor_tensor(Cd, Cx[:, :, :], cb.to_broadcast([P, MH, MV + 1]), ALU.mult).then_inc(cd, 1)
                    pool.wait_ge(sg, t + 1)
                    do(pool.tensor_tensor(gateb[:, 0:RW], gateb[:, 0:RW], zb[r][:, Z_RG:Z_RG + RW], ALU.mult))
                    pool.tensor_tensor(gateb, gateb, gain[:, :], ALU.mult).then_inc(gg, 1)
                    assert ch.n <= n_pool
                    pool.sem_inc(ch_p, n_pool - ch.n)
                blocks(pool, body)

            @block.scalar
            def _(act):
                def body(t, j, r, sample):
                    z_wait(act, t)
                    if t:
                        act.wait_ge(mixd, 2 * t)
                    act.activation(gateb[:, 0:RW], zb[r][:, Z_RG:Z_RG + RW], ACT.Sigmoid)
                    act.activation(gateb[:, RW:], zb[r][:, Z_MO:Z_MO + MW], ACT.Sigmoid).then_inc(sg, 1)
                    if t:
                        act.wait_ge(po_m, t)
                        act.wait_ge(pu_m, t)
                    act.copy(vext[:, :, 0:MV], zb[r][:, Z_MV:Z_MO].rearrange("p (h v) -> p h v", h=MH)).then_inc(vx_done, 1)
                    if t:
                        act.wait_ge(po_i, t)
                    for q in range(6):
                        act.wait_ge(tq, 6 * t + q + 1)
                        act.copy(qkT[:, 4 * q:4 * q + 4, :], bank(q).rearrange("p (k l) -> p k l", k=4)).then_inc(te, 1)
                    act.wait_ge(dwx, t + 1)
                    act.activation(dw, dw, ACT.Exp, scale=-1.0).then_inc(dwe, 1)
                    act.wait_ge(po_i, t + 1)
                    for hh in range(MH):
                        ins = act.activation(tv[:, hh * MV:(hh + 1) * MV], bank(0, 1024, 2)[:, hh * MV:(hh + 1) * MV],
                                           ACT.Identity, scale=cols[:, j, 1, hh:hh + 1])
                    ins.then_inc(ne, 1)
                    act.wait_ge(rot_p, t + 1)
                    for q in range(2):
                        act.wait_ge(nr if q == 0 else ni, t + 1)
                        act.activation(tv2[:, q * RW:(q + 1) * RW], obuf[:, q * RW:(q + 1) * RW], ACT.Square).then_inc(sq, 1)
                    act.wait_ge(msr, t + 1)
                    act.activation(st[:, 12:24], st[:, 0:12], ACT.Sqrt).then_inc(rts, 1)
                    for q in range(2):
                        act.wait_ge(pt, 4 * t + (q + 1))
                        mix_copy(act.copy, q, j, sample, ptc)
                blocks(act, body)

            @block.tensor
            def _(pe):
                def body(t, j, r, sample):
                    z = zb[r]
                    z_wait(pe, t)
                    pe.wait_ge(rot_v, t + 1)
                    pe.wait_ge(rot_p, t + 1)
                    if t:
                        pe.wait_ge(ptc, 2 * t)
                        pe.wait_ge(ptv, 2 * t)
                    for q in range(6):
                        for i in range(4):
                            n = 4 * q + i
                            src = (rk[:, n * P:(n + 1) * P] if n < 2 * RH else
                                   z[:, Z_MQ + (n - 2 * RH) * P:Z_MQ + (n - 2 * RH + 1) * P])
                            ins = pe.transpose(bank(q)[:, i * P:(i + 1) * P], src, ident)
                        ins.then_inc(tq, 1)
                    if t:
                        pe.wait_ge(cu, t)
                        pe.wait_ge(ni, t)
                    for hh in range(MH):
                        ins = pe.matmul(bank(6)[:, hh * P:(hh + 1) * P], ident[0:MH, hh:hh + 1].to_broadcast([MH, P]),
                                        mrows[:, j * P:(j + 1) * P], start=True, stop=True)
                    ins.then_inc(pmb, 1)
                    pe.wait_ge(te, 6 * t + 4)
                    for hh in range(RH):
                        ins = pe.matmul(bank(0, 1024, 2)[:, hh * P:(hh + 1) * P], qkT[:, RH + hh, :], qkT[:, hh, :],
                                        start=True, stop=True)
                    ins.then_inc(ps_r, 1)
                    pe.wait_ge(te, 6 * t + 6)
                    for hh in range(MH):
                        ins = pe.matmul(bank(2)[:, hh * P:(hh + 1) * P], qkT[:, 20 + hh, :], qkT[:, 16 + hh, :],
                                        start=True, stop=True)
                    ins.then_inc(ps_m, 1)
                    state_wait(pe, t)
                    for hh in range(RH):
                        ins = pe.matmul(bank(3, 1024, 2)[:, hh * RD:(hh + 1) * RD], qkT[:, hh, :], S[:, hh, :],
                                        start=True, stop=True)
                    ins.then_inc(qi, 1)
                    pe.wait_ge(kd_done, t + 1)
                    pe.wait_ge(iq, t + 1)
                    for hh in range(RH):
                        ins = pe.matmul(bank(3, 1024, 2)[:, hh * RD:(hh + 1) * RD], kdec[:, hh, :],
                                      z[:, Z_RV + hh * RD:Z_RV + (hh + 1) * RD], start=True, stop=True)
                    ins.then_inc(pu_r, 1)
                    pe.wait_ge(wk_done, t + 1)
                    pe.wait_ge(vx_done, t + 1)
                    pe.wait_ge(vx_one, grp + 1)
                    pe.wait_ge(mb_read, t + 1)
                    for hh in range(MH):
                        pe.matmul(bank(5, 1024, 2)[:, hh * MV:(hh + 1) * MV], wk[:, hh, :], vext[:, hh, 0:MV],
                                  start=True, stop=True)
                        ins = pe.matmul(bank(7)[:, 8 + hh:9 + hh], wk[:, hh, :], vext[:, hh, MV:MV + 1],
                                      start=True, stop=True)
                    ins.then_inc(pu_m, 1)
                    pe.wait_ge(s_r, t + 1)
                    for hh in range(RH):
                        ins = pe.matmul(bank(0, 1024, 2)[:, hh * RD:(hh + 1) * RD], sT[:, hh, :],
                                        z[:, Z_RV + hh * RD:Z_RV + (hh + 1) * RD], start=True, stop=True)
                    ins.then_inc(po_r, 1)
                    pe.wait_ge(s_m, t + 1)
                    pe.wait_ge(su, t + 1)
                    for hh in range(MH):
                        pe.matmul(bank(2, 1024, 2)[:, hh * MV:(hh + 1) * MV], smT[:, hh, :], vext[:, hh, 0:MV],
                                  start=True, stop=True)
                        ins = pe.matmul(bank(7)[:, hh:hh + 1], smT[:, hh, :], vext[:, hh, MV:MV + 1], start=True, stop=True)
                    ins.then_inc(po_m, 1)
                    pe.wait_ge(nr, t + 1)
                    for hh in range(MH):
                        pe.matmul(bank(0, 1024, 2)[:, hh * MV:(hh + 1) * MV], qkT[:, 16 + hh, :], Cx[:, hh, 0:MV],
                                  start=True, stop=True)
                        ins = pe.matmul(bank(7)[:, 4 + hh:5 + hh], qkT[:, 16 + hh, :], Cx[:, hh, MV:MV + 1],
                                      start=True, stop=True)
                    ins.then_inc(po_i, 1)
                    pe.wait_ge(ni, t + 1)
                    pe.wait_ge(cu, t + 1)
                    for q in range(4):
                        pe.wait_ge(mixd, 2 * t + (1 if q < 2 else 2))
                        for i in range(4):
                            n = 4 * q + i
                            ins = pe.transpose(bank(2 + q)[:, i * P:(i + 1) * P], obuf[:, n * P:(n + 1) * P], ident)
                        ins.then_inc(pt, 1)
                blocks(pe, body)

            @block.vector
            def _(dve):
                ch = Chain(dve, ch_v)
                if grp == 0:
                    dve.memset(S, 0.0).then_inc(reset, 1)
                    dve.memset(Cx[:, :, :], 0.0).then_inc(reset, 1)
                dve.memset(vext[:, :, MV:MV + 1], 1.0).then_inc(vx_one, 1)
                dve.wait_ge(const_in, 48 * (grp + 1))

                def body(t, j, r, sample):
                    ch.n, ch.off = 0, t * n_dve
                    do = ch.then_wait
                    z_wait(dve, t)
                    x = qk16(zb[r])
                    t1 = tv[:, 0:RW].rearrange("p (h e) -> p h e", e=half)
                    t2 = tv[:, RW:].rearrange("p (h e) -> p h e", e=half)
                    do(dve.tensor_tensor(t1, x[:, :, 0, :], cs(j, 0), ALU.mult))
                    do(dve.tensor_tensor(t2, x[:, :, 1, :], cs(j, 1), ALU.mult))
                    if t:
                        dve.wait_ge(tq, 6 * t)
                        dve.wait_ge(kd_done, t)
                    dve.tensor_tensor(qk16(rk)[:, :, 0, :], t1, t2, ALU.subtract).then_inc(rot_v, 1)
                    dve.wait_ge(pmb, t + 1)
                    if t:
                        dve.wait_ge(s_m, t)
                    for hh in range(MH):
                        ins = dve.scalar_tensor_tensor(out=dw[:, hh * P:(hh + 1) * P], in0=bank(6)[:, hh * P:(hh + 1) * P],
                                                     scalar=cols[:, j, 0, hh:hh + 1], in1=far,
                                                     op0=ALU.subtract, op1=ALU.max)
                        if hh < MH - 1:
                            do(ins)
                    ins.then_inc(dwx, 1)
                    dve.wait_ge(dwx, t + 1)
                    dve.sem_inc(mb_read, 1)
                    dve.wait_ge(ps_r, t + 1)
                    dec_wait(dve, t)
                    dve.tensor_tensor(sT.rearrange("p h l -> p (h l)"), bank(0, 1024, 2), dec[:, 0:RH * P], ALU.mult).then_inc(s_r, 1)
                    dve.wait_ge(qi, t + 1)
                    qd = dec[:, RH * P + 2 * RH:].rearrange("p (h o) -> p h o", o=1)
                    dve.tensor_tensor(tv[:, 0:RW].rearrange("p (h v) -> p h v", h=RH),
                                      bank(3, 1024, 2).rearrange("p (h v) -> p h v", h=RH),
                                      qd.to_broadcast([P, RH, RD]), ALU.mult).then_inc(iq, 1)
                    dve.wait_ge(ps_m, t + 1)
                    dve.wait_ge(dwe, t + 1)
                    dve.scalar_tensor_tensor(out=smT.rearrange("p h l -> p (h l)"), in0=bank(2), scalar=MK ** -0.5, in1=dw,
                                             op0=ALU.mult, op1=ALU.mult).then_inc(s_m, 1)
                    dve.wait_ge(po_r, t + 1)
                    dve.wait_ge(sd, t + 1)
                    dve.wait_ge(pu_r, t + 1)
                    dve.tensor_tensor(S.rearrange("p h v -> p (h v)"), Sd.rearrange("p h v -> p (h v)"),
                                      bank(3, 1024, 2), ALU.add).then_inc(su, 1)
                    dve.wait_ge(iq, t + 1)
                    if t:
                        dve.wait_ge(pt, 4 * t)
                    dve.tensor_tensor(obuf[:, 0:RW], bank(0, 1024, 2), tv[:, 0:RW], ALU.add).then_inc(nr, 1)
                    dve.wait_ge(po_i, t + 1)
                    dve.wait_ge(po_m, t + 1)
                    do(dve.tensor_tensor(st[:, 24:28], bank(7)[:, 4:8], cols[:, j, 1, :], ALU.mult))
                    do(dve.tensor_tensor(st[:, 28:32], bank(7)[:, 0:4], st[:, 24:28], ALU.add))
                    do(dve.scalar_tensor_tensor(out=st[:, 32:36], in0=st[:, 28:32], scalar=-1.0, in1=st[:, 28:32],
                                                op0=ALU.mult, op1=ALU.max))
                    do(dve.tensor_tensor(st[:, 36:40], st[:, 32:36], cols[:, j, 2, :], ALU.max))
                    do(dve.reciprocal(st[:, 40:44], st[:, 36:40]))
                    dve.wait_ge(ne, t + 1)
                    do(dve.tensor_tensor(tv[:, RW:], bank(2, 1024, 2), tv[:, 0:RW], ALU.add))
                    rd = st[:, 40:44].rearrange("p (h o) -> p h o", o=1)
                    dve.tensor_tensor(obuf[:, RW:].rearrange("p (h v) -> p h v", h=MH),
                                      tv[:, RW:].rearrange("p (h v) -> p h v", h=MH),
                                      rd.to_broadcast([P, MH, MV]), ALU.mult).then_inc(ni, 1)
                    dve.wait_ge(cd, t + 1)
                    do(dve.tensor_tensor(Cx[:, :, 0:MV], Cd[:, :, 0:MV],
                                         bank(5, 1024, 2).rearrange("p (h v) -> p h v", h=MH), ALU.add))
                    dve.tensor_tensor(Cx[:, :, MV], Cd[:, :, MV], bank(7)[:, 8:12], ALU.add).then_inc(cu, 1)
                    dve.wait_ge(sq, 2 * t + 2)
                    do(dve.tensor_reduce(st[:, 44:52], tv2[:, 0:RW].rearrange("p (h v) -> p h v", h=RH), AX_X, ALU.add))
                    do(dve.tensor_reduce(st[:, 52:56], tv2[:, RW:].rearrange("p (h v) -> p h v", h=MH), AX_X, ALU.add))
                    do(dve.tensor_scalar(st[:, 0:8], st[:, 44:52], 1.0 / RD, EPS, ALU.mult, ALU.add))
                    dve.tensor_scalar(st[:, 8:12], st[:, 52:56], 1.0 / MV, EPS, ALU.mult, ALU.add).then_inc(msr, 1)
                    dve.wait_ge(rts, t + 1)
                    do(dve.reciprocal(st[:, 56:68], st[:, 12:24]))
                    dve.wait_ge(gg, t + 1)
                    do(dve.tensor_tensor(obuf[:, 0:RW].rearrange("p (h v) -> p h v", h=RH),
                                         obuf[:, 0:RW].rearrange("p (h v) -> p h v", h=RH),
                                         st[:, 56:64].rearrange("p (h o) -> p h o", o=1).to_broadcast([P, RH, RD]), ALU.mult))
                    dve.tensor_tensor(obuf[:, 0:RW], obuf[:, 0:RW], gateb[:, 0:RW], ALU.mult).then_inc(mixd, 1)
                    do(dve.tensor_tensor(obuf[:, RW:].rearrange("p (h v) -> p h v", h=MH),
                                         obuf[:, RW:].rearrange("p (h v) -> p h v", h=MH),
                                         st[:, 64:68].rearrange("p (h o) -> p h o", o=1).to_broadcast([P, MH, MV]), ALU.mult))
                    dve.tensor_tensor(obuf[:, RW:], obuf[:, RW:], gateb[:, RW:], ALU.mult).then_inc(mixd, 1)
                    for q in range(2, 4):
                        dve.wait_ge(pt, 4 * t + (q + 1))
                        mix_copy(dve.tensor_copy, q, j, sample, ptv)
                    assert ch.n < n_dve, ch.n
                    dve.sem_inc(ch_v, n_dve - ch.n)
                blocks(dve, body)
    return run



def make_route(m, weights):
    nc, a, bank, aT = m.nc, m.a, m.bank, m.aT
    sem = lambda name: nc.alloc_semaphore("r_" + name)
    at = [0]

    def carve(n):
        v = m.ring[:, at[0]:at[0] + n]
        at[0] += n
        return v
    hot = carve(NPICK * NC).rearrange("p (k c) -> p k c", c=NC)
    keys = carve(2 * NKEY)
    keysT = carve(2 * NKEY)
    qT = carve(4 * TG).rearrange("p (r t) -> p r t", r=4)
    sc = carve(TG)
    sc2 = carve(NKEY)
    top = carve(MAXB * HH * TOPK).rearrange("p (b x k) -> p b x k", b=MAXB, x=HH)
    topi = carve(MAXB * HH * TOPK).rearrange("p (b x k) -> p b x k", b=MAXB, x=HH)
    cand, cidx, cand2 = (carve(EH * NC).rearrange("p (h c) -> p h c", h=EH) for _ in range(3))
    best, bestf, sm, ef = (carve(NPICK).rearrange("p (h k) -> p h k", h=EH) for _ in range(4))
    ti = carve(HH * TOPK).rearrange("p (x k) -> p x k", x=HH)
    sums = carve(2 * EH)
    tv, tx, besti, eidx, gate = m.tv, m.tx, m.besti, m.eidx, m.gate
    k_in, k_t, k_c = sem("keys"), sem("keys_turned"), sem("keys_copied")
    qmm, qcp, smm, scp = sem("q_mm"), sem("q_copied"), sem("s_mm"), sem("s_copied")
    chain, exd, exq, copied = sem("dve"), sem("exp_done"), sem("exp_ready"), sem("picks_copied")
    gate_dve = []
    used = {"chain": 0, "blocks": 0}

    def run(grp):
        n = len(GROUPS[grp])
        xb, b0 = HH * grp, used["blocks"]
        used["blocks"] += n
        tail = SB in GROUPS[grp]
        fresh = n * P - (SAMPLE if tail else 0)
        with nc.Block() as block:
            @block.sync
            def _(sp):
                sp.dma_start(keys[:, 0:NKEY], a["peer_keys1"][0]).then_inc(k_in, 16)
                sp.dma_start(keys[:, NKEY:], a["peer_keys2"][0]).then_inc(k_in, 16)
                weights.load(sp, a["w_peer_q"][0], DG)

            @block.tensor
            def _(pe):
                pe.wait_ge(k_in, 32 * (grp + 1))
                for i in range(2):
                    ins = pe.transpose(bank(4)[:, i * P:(i + 1) * P], keys[:, i * P:(i + 1) * P], m.ident)
                ins.then_inc(k_t, 1)
                pe.wait_ge(k_c, grp + 1)

                def four(g, first):
                    for q in range(WQ):
                        weights.wait(pe, g, q)
                        for c in range(4):
                            for k in range(q * KQ, (q + 1) * KQ):
                                ins = pe.matmul(bank(c)[:, 0:fresh], weights.W[:, k, c * P:(c + 1) * P],
                                                aT[:, k, 0:fresh], start=(k == 0), stop=(k == KT - 1))
                            if q == WQ - 1:
                                ins.then_inc(qmm, 1)
                        if q < WQ - 1:
                            ins.then_inc(weights.used, 1)
                    pe.wait_ge(qmm, 4 * g + (xb + 4))
                    pe.sem_inc(weights.used, 1)
                    for c in range(4):
                        pe.wait_ge(qcp, 4 * g + (xb + c + 1))
                        if not first:
                            pe.wait_ge(scp, 4 * g + (xb + c - 3))
                        for j in range(n):
                            ins = pe.matmul(bank(4 + c)[:, j * P:(j + 1) * P], qT[:, c, j * P:(j + 1) * P],
                                            keysT[:, (c % 2) * P:(c % 2 + 1) * P], start=True, stop=True)
                        ins.then_inc(smm, 1)
                four(0, grp == 0)
                with pe.Fori(1, DG) as g:
                    four(g, False)

            @block.scalar
            def _(act):
                act.wait_ge(k_t, grp + 1)
                act.copy(keysT, bank(4)[:, 0:2 * P]).then_inc(k_c, 1)

                def four(g, first):
                    for c in range(4):
                        act.wait_ge(qmm, 4 * g + (xb + c + 1))
                        if not first:
                            act.wait_ge(smm, 4 * g + (xb + c - 3))
                        if tail:
                            act.copy(qT[:, c, fresh:n * P], bank(c)[:, fresh - SAMPLE:fresh])
                        act.copy(qT[:, c, 0:fresh], bank(c)[:, 0:fresh]).then_inc(qcp, 1)
                four(0, grp == 0)
                with act.Fori(1, DG) as g:
                    four(g, False)
                for j in range(n):
                    act.wait_ge(exq, b0 + j + 1)
                    act.activation(sm, sm, ACT.Exp).then_inc(exd, 1)

            @block.vector
            def _(dve):
                ch = Chain(dve, chain)
                if not gate_dve:
                    gate_dve.append(Gate(nc, dve, "r_passed"))
                passed = gate_dve[0]

                def sixteen(vals, idx, src, spare):
                    def do(ins):
                        ch.then_wait(ins)
                        passed.close()
                    do(dve.max(vals[:, 0:8], src))
                    do(dve.max_index(idx[:, 0:8], vals[:, 0:8], src))
                    do(dve.match_replace(spare, vals[:, 0:8], src, LOWEST))
                    do(dve.max(vals[:, 8:16], spare))
                    do(dve.max_index(idx[:, 8:16], vals[:, 8:16], spare))

                steps = 4 * (5 * n + 2)
                base = used["chain"]
                with dve.Fori(0, DG) as g:
                    ch.n, ch.off = 0, g * steps + base
                    for c in range(4):
                        dve.wait_ge(smm, 4 * g + (xb + c + 1))
                        dve.tensor_copy(sc[:, 0:n * P], bank(4 + c)[:, 0:n * P]).then_inc(scp, 1)
                        dve.wait_ge(scp, 4 * g + (xb + c + 1))
                        passed.close()
                        for j in range(n):
                            sixteen(tv[:, j, :], tx[:, j, :], sc[:, j * P:(j + 1) * P], sc2)
                        x = bass.ds(4 * g + c, 1)
                        ch.then_wait(dve.tensor_copy(top[:, 0:n, x, :].rearrange("p b o k -> p b (o k)"), tv[:, 0:n, :]))
                        ch.then_wait(dve.tensor_copy(topi[:, 0:n, x, :].rearrange("p b o k -> p b (o k)"), tx[:, 0:n, :]))
                    assert ch.n == steps
                base += DG * steps
                n_blk = 150
                with dve.Fori(0, n) as b:
                    ch.n, ch.off = 0, b * n_blk + base
                    do = ch.then_wait
                    tb = top[:, bass.ds(b, 1), :, :].rearrange("p o h k -> p (o h) k").rearrange("p (h t) k -> p h t k", t=2)
                    do(dve.tensor_copy(ti, topi[:, bass.ds(b, 1), :, :].rearrange("p o h k -> p (o h) k")))
                    ib = ti.rearrange("p (h t) k -> p h t k", t=2)
                    do(dve.tensor_scalar(ib[:, :, 0, :], ib[:, :, 0, :], float(NKEY), None, ALU.mult))
                    c0 = 0
                    for j, rows_, w in PAIR_ROWS:
                        for src, dst in ((tb, cand), (ib, cidx)):
                            if rows_ == 1:
                                o = dst[:, :, c0:c0 + w]
                                x1 = src[:, :, 0, j:j + 1].to_broadcast([P, EH, w])
                                x2 = src[:, :, 1, 0:w]
                            else:
                                o = dst[:, :, c0:c0 + rows_ * w].rearrange("p h (n w) -> p h n w", n=rows_)
                                x1 = src[:, :, 0, j:j + rows_].rearrange("p h (n o) -> p h n o", o=1).to_broadcast([P, EH, rows_, w])
                                x2 = src[:, :, 1, 0:w].rearrange("p h (o w) -> p h o w", o=1).to_broadcast([P, EH, rows_, w])
                            do(dve.tensor_tensor(o, x1, x2, ALU.add))
                        c0 += rows_ * w
                    passed.close()
                    for e in range(EH):
                        sixteen(best[:, e, :], besti[:, e, :], cand[:, e, :], cand2[:, e, :])
                    do(dve.tensor_tensor(sm, best, best[:, :, 0:1].to_broadcast([P, EH, TOPK]), ALU.subtract))
                    dve.sem_inc(exq, 1)
                    do(dve.tensor_copy(bestf, besti[:, :, :]))
                    bf = bestf.rearrange("p h (k o) -> p (h k) o", o=1)
                    io = m.iota.rearrange("p (o c) -> p o c", o=1)
                    do(dve.tensor_tensor(hot, bf.to_broadcast([P, NPICK, NC]), io.to_broadcast([P, NPICK, NC]), ALU.is_equal))
                    for e in range(EH):
                        he = hot[:, e * TOPK:(e + 1) * TOPK, :]
                        do(dve.tensor_tensor(he, he, cidx[:, e:e + 1, :].to_broadcast([P, TOPK, NC]), ALU.mult))
                    do(dve.tensor_reduce(ef.rearrange("p h k -> p (h k)"), hot, AX_X, ALU.add))
                    do(dve.tensor_copy(eidx[:, bass.ds(b, 1), :].rearrange("p o k -> p (o k)"),
                                       ef.rearrange("p h k -> p (h k)")))
                    dve.wait_ge(exd, b + (b0 + 1))
                    do(dve.tensor_reduce(sums[:, 0:EH], sm, AX_X, ALU.add))
                    do(dve.reciprocal(sums[:, EH:], sums[:, 0:EH]))
                    do(dve.tensor_tensor(gate[:, bass.ds(b, 1), :].rearrange("p o (h k) -> p (o h) k", k=TOPK), sm,
                                         sums[:, EH:].rearrange("p (h o) -> p h o", o=1).to_broadcast([P, EH, TOPK]), ALU.mult))
                    assert ch.n <= n_blk, ch.n
                    dve.sem_inc(chain, n_blk - ch.n)
                used["chain"] = base + n * n_blk
                if tail:
                    for v in (eidx, gate):
                        dve.tensor_copy(v[SAMPLE:P, n - 1, 0:NPICK // 2], v[SAMPLE:P, n - 1, NPICK // 2:]).then_inc(copied, 1)
        weights.done(DG)
    return run


def make_gather(m):
    nc, a, bank, gain, stat, eidx, gate = m.nc, m.a, m.bank, m.gain, m.stat, m.eidx, m.gate
    sem = lambda name: nc.alloc_semaphore("g_" + name)
    ring = m.ring[:, :].rearrange("p (s d) -> p s d", s=8)
    u_in = [sem(f"u{i}") for i in range(4)]
    v_in = [sem(f"v{i}") for i in range(4)]
    uix, vix, dots, gel, wts = m.uix, m.vix, m.dots, m.gel, m.wts
    cx = m.xn[:, 0, :]
    u_idx, v_idx, u_used, v_used = sem("u_idx"), sem("v_idx"), sem("u_used"), sem("v_used")
    gelud, weighted, c_ready, zeroed, folded = sem("gelu"), sem("weights"), sem("c"), sem("zeroed"), sem("folded")
    squared, rooted, mean, inverted, fmm, g_in = (
        sem("squared"), sem("rooted"), sem("mean"), sem("inverted"), sem("fold_mm"), sem("gain"))
    NG = NPICK // GRP
    u_tab, v_tab = a["peer_u"][0], a["peer_v"][0]
    off = bass.IndirectOffsetOnAxis
    pool_gate = []
    uses = [0]

    def run(block, grp, js, side=None):
        h = m.h[grp]
        t0 = sum(map(len, GROUPS[:grp]))
        todo = [(t0 + j, j, NG // 2 if GROUPS[grp][j] == SB else NG, side if x == 0 else None) for x, j in enumerate(js)]
        uses[0] += 1
        use = uses[0]

        def pairs(eng, groups, sd, body):
            last = 0
            if sd:
                with eng.Fori(1, sd.hooked_pairs) as i:
                    body(i, sd)
                last = sd.hooked_pairs
                body(last, sd)
            if last + 1 < groups // 2:
                with eng.Fori(last + 1, groups // 2) as i:
                    body(i, None)

        @block.sync
        def _(sp):
            sp.dma_start(gain[:, :], m.row_bcast(a["g_ffn"][0])).then_inc(g_in, 16)
            if side:
                side.sync(sp)

        @block.gpsimd
        def _(pool):
            if not pool_gate:
                pool_gate.append(Gate(nc, pool, "g_passed"))
            passed = pool_gate[0]

            def group(n, r, j, g, first, ix, landed, ready):
                if not first:
                    for i in range(4):
                        pool.wait_ge(landed[i], 32 * n - 32)
                passed.close()
                pool.tensor_copy(ix[:, r, :], eidx[:, j, bass.ds(g * GRP, GRP)]).then_inc(ready, 1)
                pool.wait_ge(ready, n + 1)
                passed.close()

            def row(n, r, x, first, ix, slot, tab, used, landed):
                if not (first and x < 4):
                    pool.wait_ge(used, GRP * n + (x - 3))
                passed.close()
                pool.indirect_dma_start(ring[:, slot + x % 4, :], None, tab, off(ix[:, r, x:x + 1], 0)
                                        ).then_inc(landed[x % 4], 16)

            def u_group(n, r, j, g, first):
                group(n, r, j, g, first, uix, u_in, u_idx)

            def v_group(n, r, j, g, first):
                group(n, r, j, g, first, vix, v_in, v_idx)

            def u_row(n, r, x, first):
                row(n, r, x, first, uix, 0, u_tab, u_used, u_in)

            def v_row(n, r, x, first):
                row(n, r, x, first, vix, 4, v_tab, v_used, v_in)

            for t, j, groups, sd in todo:
                n0, start = t * NG, t == 0
                u_group(n0, 0, j, 0, start)
                for x in range(GRP):
                    u_row(n0, 0, x, start)

                def both(g, ru, rv, first):
                    u_group(n0 + g, ru, j, g, first)
                    v_group(n0 + g - 1, rv, j, g - 1, first)
                    for x in range(GRP):
                        u_row(n0 + g, ru, x, False)
                        v_row(n0 + g - 1, rv, x, first)
                both(1, 1, 0, start)
                with pool.Fori(1, groups // 2) as i:
                    both(2 * i, 0, 1, False)
                    both(2 * i + 1, 1, 0, False)
                v_group(n0 + groups - 1, 1, j, groups - 1, False)
                for x in range(GRP):
                    v_row(n0 + groups - 1, 1, x, False)

        @block.scalar
        def _(act):
            for t, j, groups, sd in todo:
                n0 = t * NG
                if t:
                    act.wait_ge(u_used, NG * GRP * t)
                act.activation(cx, h[:, j, :], ACT.Square, accum_out=stat[:, 0:1]).then_inc(squared, 1)
                act.wait_ge(mean, t + 1)
                act.activation(stat[:, 2:3], stat[:, 1:2], ACT.Sqrt).then_inc(rooted, 1)

                def gelus(n, r, first):
                    act.wait_ge(u_used, GRP * n + GRP)
                    if not first:
                        act.wait_ge(weighted, n - 1)
                    act.activation(gel[:, r, :], dots[:, r, :], ACT.Gelu).then_inc(gelud, 1)

                def pair(i, slots, first=False):
                    for r in range(2):
                        gelus(n0 + 2 * i + r, r, first)
                        if slots:
                            slots.act_slot(act, i, r)
                pair(0, sd, t == 0)
                pairs(act, groups, sd, pair)

        @block.vector
        def _(dve):
            dve.wait_ge(g_in, 16 * use)
            if side:
                side.open(dve)
            for t, j, groups, sd in todo:
                n0, hb = t * NG, h[:, j, :]
                dve.wait_ge(squared, t + 1)
                dve.tensor_scalar(stat[:, 1:2], stat[:, 0:1], 1.0 / D, EPS, ALU.mult, ALU.add).then_inc(mean, 1)
                dve.wait_ge(rooted, t + 1)
                dve.reciprocal(stat[:, 3:4], stat[:, 2:3]).then_inc(inverted, 1)
                dve.wait_ge(inverted, t + 1)
                dve.scalar_tensor_tensor(out=cx, in0=hb, scalar=stat[:, 3:4], in1=gain[:, :],
                                         op0=ALU.mult, op1=ALU.mult).then_inc(c_ready, 1)
                dve.wait_ge(c_ready, t + 1)
                if groups < NG:
                    dve.memset(h[SAMPLE:P, j, :], 0.0).then_inc(zeroed, 1)
                    dve.wait_ge(zeroed, 1)

                def dot(n, r, x):
                    dve.wait_ge(u_in[x % 4], 32 * n + (16 if x < 4 else 32))
                    row = ring[:, x % 4, :]
                    dve.tensor_tensor_reduce(row, row, cx, 1.0, 0.0, ALU.mult, ALU.add,
                                             dots[:, r, x:x + 1]).then_inc(u_used, 1)

                def weigh(n, r, g):
                    dve.wait_ge(gelud, n + 1)
                    dve.tensor_tensor(wts[:, r, :], gel[:, r, :], gate[:, j, bass.ds(g * GRP, GRP)],
                                      ALU.mult).then_inc(weighted, 1)
                    dve.wait_ge(weighted, n + 1)

                def add(n, r, x):
                    dve.wait_ge(v_in[x % 4], 32 * n + (16 if x < 4 else 32))
                    if not (isinstance(n, int) and n == 0 and x == 0):
                        dve.wait_ge(v_used, GRP * n + x)
                    dve.scalar_tensor_tensor(out=hb, in0=ring[:, 4 + x % 4, :], scalar=wts[:, r, x:x + 1],
                                             in1=hb, op0=ALU.mult, op1=ALU.add).then_inc(v_used, 1)

                def both(g, ru, rv):
                    dot(n0 + g, ru, 0)
                    weigh(n0 + g - 1, rv, g - 1)
                    for x in range(GRP):
                        if x:
                            dot(n0 + g, ru, x)
                        add(n0 + g - 1, rv, x)

                def pair(i, slots):
                    for r in range(2):
                        both(2 * i + r, r, 1 - r)
                        if slots:
                            slots.dve_slot(dve, i, r)
                for x in range(GRP):
                    dot(n0, 0, x)
                both(1, 1, 0)
                pairs(dve, groups, sd, pair)
                weigh(n0 + groups - 1, 1, groups - 1)
                for x in range(GRP):
                    add(n0 + groups - 1, 1, x)
            if groups < NG:
                dve.wait_ge(fmm, 1)
                dve.tensor_copy(h[:, j, :], bank(0, D, 4)).then_inc(folded, 1)

        @block.tensor
        def _(pe):
            if side:
                side.tensor(pe)
            t, j, groups, _ = todo[-1]
            if groups < NG:
                if side:
                    side.emptied(pe)
                pe.wait_ge(v_used, GRP * (NG * t + groups))
                for q in range(4):
                    ins = pe.matmul(bank(q), m.fold, h[:, j, q * 512:(q + 1) * 512], start=True, stop=True)
                ins.then_inc(fmm, 1)
        if side:
            side.end()
    return run


class Embeddings:
    PK = PLE // P
    hooked_pairs = DG // 2 + 1

    def __init__(self, m, weights):
        self.m, self.weights = m, weights
        sem = lambda name: m.nc.alloc_semaphore("x_" + name)
        self.p_in, self.wp_in, self.pt, self.ptc = sem("p_in"), sem("wp_in"), sem("p_turned"), sem("p_copied")
        self.mm, self.taken, self.pj, self.scaled, self.free = (
            sem("mm"), sem("sigmoid"), sem("proj"), sem("scaled"), sem("free"))
        self.p = m.stage[:, 0:MAXB * PLE].rearrange("p (b c) -> p b c", b=MAXB)
        self.pT = m.stage[:, MAXB * PLE:2 * MAXB * PLE].rearrange("p (k t) -> p k t", k=self.PK)
        self.sig = m.stage[:, 2 * MAXB * PLE:2 * MAXB * PLE + 2 * CG].rearrange("p (r c) -> p r c", r=2)
        self.p_loads = 0

    def at(self, grp):
        m = self.m
        self.grp, self.n, self.h = grp, len(GROUPS[grp]), m.h[grp]
        self.base = grp * DG * len(GROUPS[0])
        if grp == 0:
            self.wp = [m.xn[:, 1, :].rearrange("p (a b) -> p a b", b=P), m.aT[:, :, 2 * P:3 * P]]
        else:
            self.wp = [m.ring[:, k * D:(k + 1) * D].rearrange("p (a b) -> p a b", b=P) for k in range(self.PK)]

    def sync(self, sp):
        m = self.m
        for j, b in enumerate(GROUPS[self.grp]):
            if b < SB:
                sp.dma_start(self.p[:, j, :], m.a["p_prompt"][0, 0, b * P:(b + 1) * P, :]).then_inc(self.p_in, 16)
                self.p_loads += 1
            else:
                for c in range(2):
                    sp.dma_start(self.p[c * SAMPLE:(c + 1) * SAMPLE, j, :], m.a["p_sample"][0, 0]).then_inc(self.p_in, 16)
                    self.p_loads += 1
        for k in range(self.PK):
            sp.dma_start(self.wp[k], m.a["w_ple_proj"][0, k * P:(k + 1) * P, :].rearrange("p (a b) -> p a b", b=P)
                         ).then_inc(self.wp_in, 16)
        self.weights.load(sp, m.a["w_ple_gate"][0], DG)

    def tensor(self, pe):
        m, n = self.m, self.n
        pe.wait_ge(self.p_in, 16 * self.p_loads)
        for j in range(n):
            for k in range(self.PK):
                ins = pe.transpose(m.bank(6 + k)[:, j * P:(j + 1) * P], self.p[:, j, k * P:(k + 1) * P], m.ident)
        ins.then_inc(self.pt, 1)
        pe.wait_ge(self.ptc, self.grp + 1)
        pe.wait_ge(self.wp_in, 32 * (self.grp + 1))

        def projection(i, s, first):
            for j in range(n):
                x = s * n + j
                pe.wait_ge(self.free, 2 * n * i + (self.base + x + 1))
                for k in range(self.PK):
                    ins = pe.matmul(m.bank(6 + x % 2), self.pT[:, k, j * P:(j + 1) * P],
                                    self.wp[k][:, bass.ds((2 * i + s) * (CG // P), CG // P), :],
                                    start=(k == 0), stop=(k == self.PK - 1))
                ins.then_inc(self.pj, 1)
        product_groups(pe, m.aT, self.weights, m.bank, n, DG, self.mm, self.taken, self.base, projection)

    def emptied(self, eng):
        eng.wait_ge(self.taken, self.base + DG * self.n)

    def take_p(self, act):
        act.wait_ge(self.pt, self.grp + 1)
        act.copy(self.pT[:, :, 0:self.n * P], self.m.bank(6, 1024, 2).rearrange("p (k c) -> p k c", k=2)[:, :, 0:self.n * P]
                 ).then_inc(self.ptc, 1)

    def sigmoids(self, act, i, s):
        for j in range(self.n):
            x = s * self.n + j
            N = 2 * self.n * i + (self.base + x)
            act.wait_ge(self.mm, N + 1)
            act.wait_ge(self.free, N + 1)
            act.activation(self.sig[:, x % 2, :], self.m.bank(3 * s + j), ACT.Sigmoid).then_inc(self.taken, 1)

    def open(self, dve):
        if self.grp == 0:
            dve.sem_inc(self.free, 2)

    def add(self, dve, i, s):
        for j in range(self.n):
            x = s * self.n + j
            N = 2 * self.n * i + (self.base + x)
            sig = self.sig[:, x % 2, :]
            dve.wait_ge(self.taken, N + 1)
            dve.wait_ge(self.pj, N + 1)
            dve.tensor_tensor(sig, self.m.bank(6 + x % 2), sig, ALU.mult).then_inc(self.scaled, 1)
            dve.wait_ge(self.scaled, N + 1)
            hc = self.h[:, j, bass.ds((2 * i + s) * CG, CG)]
            dve.tensor_tensor(hc, hc, sig, ALU.add).then_inc(self.free, 1)

    def beside(self, grp):
        self.at(grp)
        return self

    def act_slot(self, act, i, r):
        if isinstance(i, int):
            if i == 0 and r == 0:
                self.take_p(act)
        else:
            self.sigmoids(act, i - 1, r)

    def dve_slot(self, dve, i, r):
        if not isinstance(i, int):
            self.add(dve, i - 1, r)

    def end(self):
        self.weights.done(DG)

    def alone(self, grp):
        self.at(grp)
        m, out, xn, gain, stat = self.m, self.m.out, self.m.xn, self.m.gain, self.m.stat
        sem = lambda name: m.nc.alloc_semaphore("y_" + name)
        g_in, squared, mean, rooted, inverted, y_ready = (
            sem("gain"), sem("squared"), sem("mean"), sem("rooted"), sem("inverted"), sem("ready"))
        y_out = [sem("out0"), sem("out1")]
        junk = m.ring[:, 2 * D:3 * D]
        blks = [(t, m.h[g][:, j, :], b, g) for t, (g, j, b) in
                enumerate((g, j, b) for g, blks in enumerate(GROUPS) for j, b in enumerate(blks))]
        with m.nc.Block() as block:
            @block.sync
            def _(sp):
                sp.dma_start(gain[:, :], m.row_bcast(m.a["g_final"])).then_inc(g_in, 16)
                self.sync(sp)
                for t, hb, b, g in blks:
                    sp.wait_ge(y_ready, t + 1)
                    if b < SB:
                        sp.dma_start(out["y_prompt"][0, b * P:(b + 1) * P, :], xn[:, t % 2, :]).then_inc(y_out[t % 2], 16)
                    else:
                        sp.dma_start(out["y_sample"][0], xn[0:SAMPLE, t % 2, :]).then_inc(y_out[t % 2], 16)
                sp.wait_ge(y_out[0], 48)
                sp.wait_ge(y_out[1], 32)

            block.tensor(self.tensor)

            def act_final(act, t, hb):
                if t:
                    act.wait_ge(mean, t)
                act.activation(junk, hb, ACT.Square, accum_out=stat[:, 0:1]).then_inc(squared, 1)
                act.wait_ge(mean, t + 1)
                if t:
                    act.wait_ge(inverted, t)
                act.activation(stat[:, 2:3], stat[:, 1:2], ACT.Sqrt).then_inc(rooted, 1)

            @block.scalar
            def _(act):
                self.take_p(act)
                for t, hb, b, g in blks:
                    if g == 0:
                        act_final(act, t, hb)
                with act.Fori(0, DG // 2) as i:
                    for s in range(2):
                        self.sigmoids(act, i, s)
                act.wait_ge(self.free, 2 + self.base + DG * self.n)
                for t, hb, b, g in blks:
                    if g:
                        act_final(act, t, hb)

            def dve_final(dve, t, hb):
                dve.wait_ge(squared, t + 1)
                dve.tensor_scalar(stat[:, 1:2], stat[:, 0:1], 1.0 / D, EPS, ALU.mult, ALU.add).then_inc(mean, 1)
                dve.wait_ge(rooted, t + 1)
                dve.reciprocal(stat[:, 3:4], stat[:, 2:3]).then_inc(inverted, 1)
                dve.wait_ge(inverted, t + 1)
                if t >= 2:
                    dve.wait_ge(y_out[t % 2], 16 * (t // 2))
                dve.scalar_tensor_tensor(out=xn[:, t % 2, :], in0=hb, scalar=stat[:, 3:4],
                                         in1=gain[:, :], op0=ALU.mult, op1=ALU.mult).then_inc(y_ready, 1)

            @block.vector
            def _(dve):
                dve.wait_ge(g_in, 16)
                for t, hb, b, g in blks:
                    if g == 0:
                        dve_final(dve, t, hb)
                with dve.Fori(0, DG // 2) as i:
                    for s in range(2):
                        self.add(dve, i, s)
                dve.wait_ge(self.free, 2 + self.base + DG * self.n)
                for t, hb, b, g in blks:
                    if g:
                        dve_final(dve, t, hb)
        self.weights.done(DG)


_INS = ["x_prompt", "x_sample", "p_prompt", "p_sample", "state_ret", "state_mlstm_C", "state_mlstm_n", "state_mlstm_m",
        "g_mix", "w_in", "b_gates", "g_ret", "g_mlstm", "w_out", "g_ffn", "w_peer_q", "peer_keys1", "peer_keys2",
        "peer_u", "peer_v", "g_ple", "w_ple_gate", "w_ple_proj", "g_final"]
_OUTS = [("y_prompt", (1, PROMPT, D)), ("y_sample", (1, SAMPLE, D)),
         ("ret_prompt", (1, 1, RH, RD, RD)), ("C_prompt", (1, 1, MH, MK, MV)), ("n_prompt", (1, 1, MH, MK)), ("m_prompt", (1, 1, MH)),
         ("ret_sample", (1, 1, RH, RD, RD)), ("C_sample", (1, 1, MH, MK, MV)), ("n_sample", (1, 1, MH, MK)), ("m_sample", (1, 1, MH))]


def kernel(**inputs):
    import concourse.bacc as bacc
    from concourse.bass_utils import run_bass_kernel_spmd

    nc = bacc.Bacc("TRN2", target_bir_lowering=False, num_devices=1)
    arrays, a, out = {}, {}, {}
    for name, value in [(n, inputs[n]) for n in _INS] + list(constants().items()):
        v = np.ascontiguousarray(value)
        arrays[f"in_{name}"] = v
        a[name] = nc.dram_tensor(f"in_{name}", v.shape, mybir.dt.from_np(v.dtype), kind="ExternalInput").ap()
    for name, shape in _OUTS:
        out[name] = nc.dram_tensor(f"out_{name}", shape, F32, kind="ExternalOutput").ap()
    build(nc, a, out)
    r = run_bass_kernel_spmd(nc, [arrays], core_ids=[0])
    return tuple(r.results[0][f"out_{name}"] for name, _ in _OUTS)
```

```python
from contextlib import ExitStack

import numpy as np

import concourse.bass as bass
from concourse import mybir

F32 = mybir.dt.float32
U32 = mybir.dt.uint32
ALU = mybir.AluOpType
ACT = mybir.ActivationFunctionType
AX_X = mybir.AxisListType.X

P = 128
D = 2048
KT = D // P
PROMPT, SAMPLE = 512, 64
NB = PROMPT // P + 1
SB = NB - 1
T = NB * P
PAST = 256
EPS = 1e-6
RH, RD = 8, 128
MH, MK, MV = 4, 128, 256
RW, MW = RH * RD, MH * MV
ZC = 4 * RW + 2 * MH * MK + 2 * MW
Z_RQ, Z_RK, Z_RV, Z_RG = 0, RW, 2 * RW, 3 * RW
Z_MQ = 4 * RW
Z_MK = Z_MQ + MH * MK
Z_MV = Z_MK + MH * MK
Z_MO = Z_MV + MW
GROUPS = [[0, 1], [2, 3, SB]]
MAXB = 3
TG = MAXB * P
WQ = 4
KQ = KT // WQ
CG = 512
ZG = ZC // CG
DG = D // CG
EH, EQ, NKEY, TOPK = 8, 256, 128, 16
HH = 2 * EH
NE = NKEY * NKEY
NPICK = EH * TOPK
PLE = 256
GRP = 8
PAIR_ROWS = [(0, 1, 16), (1, 1, 8), (2, 1, 5), (3, 1, 4), (4, 1, 3), (5, 3, 2), (8, 8, 1)]
NC = sum(n * w for _, n, w in PAIR_ROWS)
LOWEST = -3.0e38
FAR = 1.0e30


def constants():
    half = RD // 2
    inv = np.float32(10000.0) ** (-np.arange(half, dtype=np.float32) / np.float32(half))
    pos = np.concatenate([np.arange(PROMPT), PAST + np.arange(SAMPLE), PAST + np.arange(SAMPLE)]).astype(np.float32)
    ang = (pos[:, None] * inv[None, :]).astype(np.float32)
    rope = np.stack([np.cos(ang), np.sin(ang)], 1).astype(np.float32)
    rope = rope.reshape(NB, P, 2 * half).transpose(1, 0, 2).reshape(P, NB * 2 * half)
    lg = np.log(1.0 - 2.0 ** (-5.0 - np.arange(RH)))
    scale = RD ** -0.5
    i = np.arange(P)
    tabs = []
    for n in (P, SAMPLE):
        diff = i[None, :] - i[:, None]
        keep = (diff >= 0) & (i[:, None] < n)
        dec = np.where(keep[:, None, :], np.exp(np.where(keep, diff, 0)[:, None, :] * lg[None, :, None]), 0) * scale
        kd = np.where(i[:, None] < n, np.exp((n - 1.0 - np.minimum(i, n - 1))[:, None] * lg[None, :]), 0) * scale
        gl = np.broadcast_to(np.exp(n * lg)[None, :], (P, RH))
        qd = np.exp((i[:, None] + 1.0) * lg[None, :])
        tabs.append(np.concatenate([dec.reshape(P, RH * P), kd, gl, qd], 1))
    far = np.where(i[:, None] <= i[None, :], 0.0, FAR)
    ident = np.eye(P)
    fold = (i[:, None] % SAMPLE == i[None, :] % SAMPLE)
    row = np.concatenate([far, ident, fold.astype(float), np.broadcast_to(np.arange(NC), (P, NC))], 1)
    return {
        "c_rope": rope,
        "c_decay": np.stack(tabs).astype(np.float32),
        "c_misc": row.astype(np.float32),
    }


class Machine:
    pass


class Gate:

    def __init__(self, nc, eng, name):
        self.eng, self.sem = eng, nc.alloc_semaphore(name)

    def close(self):
        self.eng.sem_inc(self.sem, 1)


class Chain:

    def __init__(self, eng, sem):
        self.eng, self.sem, self.n, self.off = eng, sem, 0, 0

    def then_wait(self, ins):
        self.n += 1
        ins.then_inc(self.sem, 1)
        self.eng.wait_ge(self.sem, self.off + self.n)


def build(nc, a, out):
    with ExitStack() as ctx:
        def sb(name, shape, dt=F32):
            return ctx.enter_context(nc.sbuf_tensor(name, shape, dt))

        actT = sb("actT", [P, KT * TG])
        h1 = sb("h1", [P, len(GROUPS[0]), D])
        h2 = sb("h2", [P, MAXB, D])
        ring = sb("ring", [P, 8 * D])
        W = sb("W", [P, KT, CG])
        gain = sb("gain", [P, D])
        xn = sb("xn", [P, 2, D])
        stage = sb("stage", [P, NB * CG])
        misc = sb("misc", [P, 3 * P + NC])
        stat = sb("stat", [P, 80])
        eidx = sb("eidx", [P, MAXB, NPICK], U32)
        gate = sb("gate", [P, MAXB, NPICK])
        cols = sb("cols", [P, MAXB, 4, MH])
        cdbc = sb("cdbc", [P, MAXB, MH])
        mrows = sb("mrows", [MH, TG])
        Cx = sb("Cx", [P, MH, MV + 1])
        tv = sb("tv", [P, MAXB, TOPK])
        tx = sb("tx", [P, MAXB, TOPK], U32)
        besti = sb("besti", [P, EH, TOPK], U32)
        uix = sb("uix", [P, 2, GRP], U32)
        vix = sb("vix", [P, 2, GRP], U32)
        dots = sb("dots", [P, 2, GRP])
        gel = sb("gel", [P, 2, GRP])
        wts = sb("wts", [P, 2, GRP])
        psum = ctx.enter_context(nc.psum_tensor("psum", [P, 8, 512], F32))

        far = misc[:, 0:P]
        ident = misc[:, P:2 * P]
        fold = misc[:, 2 * P:3 * P]
        iota = misc[:, 3 * P:]
        aT = actT[:, :].rearrange("p (k t) -> p k t", k=KT)
        zd = nc.dram_tensor("z_scratch", (NB, P, ZC), F32, kind="Internal").ap()
        s_keep = nc.dram_tensor("s_scratch", (P, RW), F32, kind="Internal").ap()
        c_keep = nc.dram_tensor("c_scratch", (P, MH * (MV + 1)), F32, kind="Internal").ap()

        def bank(n, width=512, banks=1):
            v = psum[:, n:n + banks, :].rearrange("p b c -> p (b c)")
            return v[:, 0:width]

        def row_bcast(ap1d):
            return ap1d.rearrange("(o d) -> o d", o=1).to_broadcast([P, ap1d.shape[0]])

        hs = (h1, h2)
        x_in, misc_in = nc.alloc_semaphore("x_in"), nc.alloc_semaphore("misc_in")
        x_loads = [0]

        def load_x(eng, grp):
            for j, b in enumerate(GROUPS[grp]):
                if b < SB:
                    eng.dma_start(hs[grp][:, j, :], a["x_prompt"][0, b * P:(b + 1) * P, :]).then_inc(x_in, 16)
                    x_loads[0] += 1
                else:
                    for c in range(2):
                        eng.dma_start(hs[grp][c * SAMPLE:(c + 1) * SAMPLE, j, :], a["x_sample"][0]).then_inc(x_in, 16)
                        x_loads[0] += 1
            return 16 * x_loads[0]

        m = Machine()
        m.nc, m.a, m.out, m.aT, m.h, m.ring = nc, a, out, aT, hs, ring
        m.W, m.gain, m.xn, m.stage, m.stat, m.eidx = W, gain, xn, stage, stat, eidx
        m.gate, m.cols, m.cdbc, m.mrows, m.far, m.ident = gate, cols, cdbc, mrows, far, ident
        m.fold, m.iota, m.zd, m.s_keep, m.c_keep, m.bank = fold, iota, zd, s_keep, c_keep, bank
        m.row_bcast, m.Cx, m.tv, m.tx, m.besti, m.uix = row_bcast, Cx, tv, tx, besti, uix
        m.load_x, m.x_in = load_x, x_in
        m.vix, m.dots, m.gel, m.wts = vix, dots, gel, wts
        norm = make_norm_transpose(m)
        weights = Weights(nc, W)
        project = Project(m, weights)
        rows = make_rows(m)
        mixers = make_mixers(m)
        project_out = ProjectOut(m, weights)
        scores = Scores(m, weights)
        picks = make_picks(m)
        gather = make_gather(m)
        embed = Embeddings(m, weights)

        def norm_stage(grp, g, from_x=False):
            with nc.Block() as block:
                def loads(sp, gin):
                    if from_x and grp == 0:
                        sp.dma_start(misc[:, :], a["c_misc"]).then_inc(misc_in, 16)
                    sp.dma_start(gain[:, :], row_bcast(a[g][0])).then_inc(gin, 16)
                    if from_x:
                        load_x(sp, grp)
                norm(block, grp, loads, (lambda eng: eng.wait_ge(x_in, 16 * x_loads[0])) if from_x else None, misc_in)

        norm_stage(0, "g_mix", True)
        project.alone(0)
        rows(0)
        mixers(0)
        project_out.alone(0)
        norm_stage(0, "g_ffn")
        scores.alone(0)
        picks(0)
        norm_stage(1, "g_mix", True)
        with nc.Block() as block:
            gather(block, 0, [0], project.beside(1))
        rows(1)
        mixers(1)
        with nc.Block() as block:
            gather(block, 0, [1], OutToScores(m, weights, project_out, scores, 1))
        picks(1)
        norm_stage(0, "g_ple")
        with nc.Block() as block:
            gather(block, 1, [0, 1, 2], embed.beside(0))
        norm_stage(1, "g_ple")
        embed.alone(1)


def make_norm_transpose(m):
    nc, xn, gain, stat, bank, aT = m.nc, m.xn, m.gain, m.stat, m.bank, m.aT
    squared, mean, rooted, normed, turned, copied_a, copied_v, chain, gin = (
        nc.alloc_semaphore("n_" + x) for x in
        ("squared", "mean", "rooted", "normed", "turned", "copied_a", "copied_v", "dve", "gain"))
    ssq, ms, rt, rs = (stat[:, 2 * i:2 * i + 2] for i in range(4))
    junk = m.stage[:, 0:D]
    used = {"uses": 0, "blocks": 0}

    def run(block, grp, loads, inputs, misc_in):
        h, t0, use = m.h[grp], used["blocks"], used["uses"]
        todo = [(j, t0 + j, (t0 + j) % 2) for j in range(len(GROUPS[grp]))]
        used["blocks"] += len(todo)
        used["uses"] += 1

        @block.sync
        def _(sp):
            loads(sp, gin)

        @block.scalar
        def _(act):
            if inputs is not None:
                inputs(act)
            for j, t, r in todo:
                if t:
                    act.wait_ge(squared, t)
                    act.wait_ge(mean, t)
                act.activation(junk, h[:, j, :], ACT.Square, accum_out=ssq[:, r:r + 1]).then_inc(squared, 1)
                act.wait_ge(mean, t + 1)
                act.activation(rt[:, r:r + 1], ms[:, r:r + 1], ACT.Sqrt).then_inc(rooted, 1)
                for q in range(2):
                    act.wait_ge(turned, 4 * t + q + 1)
                    act.copy(aT[:, 4 * q:4 * q + 4, j * P:(j + 1) * P],
                             bank(4 * r + q).rearrange("p (k l) -> p k l", k=4)).then_inc(copied_a, 1)

        @block.vector
        def _(dve):
            dve.wait_ge(gin, 16 * (use + 1))
            for j, t, r in todo:
                dve.wait_ge(squared, t + 1)
                dve.tensor_scalar(ms[:, r:r + 1], ssq[:, r:r + 1], 1.0 / D, EPS, ALU.mult, ALU.add).then_inc(mean, 1)
                dve.wait_ge(rooted, t + 1)
                dve.reciprocal(rs[:, r:r + 1], rt[:, r:r + 1]).then_inc(chain, 1)
                dve.wait_ge(chain, t + 1)
                if t >= 2:
                    dve.wait_ge(turned, 4 * (t - 1))
                dve.scalar_tensor_tensor(out=xn[:, r, :], in0=h[:, j, :], scalar=rs[:, r:r + 1],
                                         in1=gain[:, :], op0=ALU.mult, op1=ALU.mult).then_inc(normed, 1)
                for q in range(2, 4):
                    dve.wait_ge(turned, 4 * t + q + 1)
                    dve.tensor_copy(aT[:, 4 * q:4 * q + 4, j * P:(j + 1) * P],
                                    bank(4 * r + q).rearrange("p (k l) -> p k l", k=4)).then_inc(copied_v, 1)

        @block.tensor
        def _(pe):
            pe.wait_ge(misc_in, 16)
            for j, t, r in todo:
                pe.wait_ge(normed, t + 1)
                if t >= 2:
                    pe.wait_ge(copied_a, 2 * (t - 1))
                    pe.wait_ge(copied_v, 2 * (t - 1))
                for q in range(4):
                    for i in range(4):
                        k = 4 * q + i
                        ins = pe.transpose(bank(4 * r + q)[:, i * P:(i + 1) * P], xn[:, r, k * P:(k + 1) * P], m.ident)
                    ins.then_inc(turned, 1)
    return run


class Weights:

    def __init__(self, nc, W):
        self.W, self.g0 = W, 0
        self.landed = [nc.alloc_semaphore(f"w_landed{q}") for q in range(WQ)]
        self.used = nc.alloc_semaphore("w_used")

    def load(self, eng, w, groups, before=0):
        wv = w.rearrange("(k p) c -> p k c", p=P)

        def part(g, q):
            ks = slice(q * KQ, (q + 1) * KQ)
            eng.dma_start(self.W[:, ks, :], wv[:, ks, bass.ds(g * CG, CG)]).then_inc(self.landed[q], 16)
        if not before:
            for q in range(WQ):
                part(0, q)
        with eng.Fori(0 if before else 1, groups) as g:
            for q in range(WQ):
                eng.wait_ge(self.used, WQ * g + (WQ * (self.g0 + before - 1) + q + 1))
                part(g, q)

    def wait(self, pe, g, q):
        pe.wait_ge(self.landed[q], 16 * g + 16 * (self.g0 + 1))

    def done(self, groups):
        self.g0 += groups


def product_groups(pe, aT, weights, bank, n, groups, mm, taken, base, after=None):
    def pair(i, first):
        for s in range(2):
            for q in range(WQ):
                weights.wait(pe, 2 * i + s, q)
                for j in range(n):
                    if q == 0 and not first:
                        pe.wait_ge(taken, (2 * i + (s - 2)) * n + (base + j + 1))
                    for k in range(q * KQ, (q + 1) * KQ):
                        ins = pe.matmul(bank(3 * s + j), aT[:, k, j * P:(j + 1) * P], weights.W[:, k, :],
                                        start=(k == 0), stop=(k == KT - 1))
                    if q == WQ - 1:
                        ins.then_inc(mm, 1)
                if q < WQ - 1:
                    ins.then_inc(weights.used, 1)
            pe.wait_ge(mm, (2 * i + (s + 1)) * n + base)
            pe.sem_inc(weights.used, 1)
            if after:
                after(i, s, first)
    pair(0, True)
    with pe.Fori(1, groups // 2) as i:
        pair(i, False)


class Project:

    def __init__(self, m, weights):
        self.m, self.weights = m, weights
        sem = lambda name: m.nc.alloc_semaphore("p_" + name)
        self.mm, self.taken, self.gate_mm, self.gate_taken = sem("mm"), sem("taken"), sem("gate_mm"), sem("gate_taken")
        self.stored = [sem(f"stored{j}") for j in range(MAXB)]
        self.small_in = sem("gate_weights_in")

    def at(self, grp):
        self.grp, self.n = grp, len(GROUPS[grp])
        self.base = grp * ZG * len(GROUPS[0])
        self.bias = self.m.stat[0:MH, 74:76]
        self.wg = self.m.xn[:, 1, 0:KT * 2 * MH].rearrange("p (k g) -> p k g", k=KT)

    def sync(self, sp):
        m = self.m
        sp.dma_start(self.wg, m.a["w_in"][0].rearrange("(k p) c -> p k c", p=P)[:, :, ZC:ZC + 2 * MH]
                     ).then_inc(self.small_in, 16)
        with m.nc.allow_non_contiguous_dma(reason="eight biases"):
            sp.dma_start(self.bias, m.a["b_gates"][0].rearrange("(g h) -> h g", h=MH)).then_inc(self.small_in, 16)
        self.weights.load(sp, m.a["w_in"][0], ZG)

    def tensor(self, pe):
        m, n = self.m, self.n
        pe.wait_ge(self.small_in, 32 * (self.grp + 1))
        for g in range(2):
            for k in range(KT):
                ins = pe.matmul(m.bank(6 + g)[0:MH, 0:n * P], self.wg[:, k, g * MH:(g + 1) * MH],
                                m.aT[:, k, 0:n * P], start=(k == 0), stop=(k == KT - 1))
            ins.then_inc(self.gate_mm, 1)
        product_groups(pe, m.aT, self.weights, m.bank, n, ZG, self.mm, self.taken, self.base)

    def take_gates(self, act):
        m, n = self.m, self.n
        for g in range(2):
            act.wait_ge(self.gate_mm, 2 * self.grp + g + 1)
            act.activation(m.stage[0:MH, MAXB * CG + g * TG:MAXB * CG + g * TG + n * P], m.bank(6 + g)[0:MH, 0:n * P],
                           ACT.Identity, bias=self.bias[:, g:g + 1]).then_inc(self.gate_taken, 1)

    def take(self, act, g, s, first):
        m, n = self.m, self.n
        g_before = 0 if self.grp == 0 else ZG
        for j in range(n):
            act.wait_ge(self.mm, g * n + (self.base + j + 1))
            if not first:
                act.wait_ge(self.stored[j], 16 * g + 16 * (g_before if j < len(GROUPS[0]) else 0))
            act.copy(m.stage[:, j * CG:(j + 1) * CG], m.bank(3 * s + j)).then_inc(self.taken, 1)
            act.wait_ge(self.taken, g * n + (self.base + j + 1))
            act.dma_start(m.zd[GROUPS[self.grp][j], :, bass.ds(g * CG, CG)], m.stage[:, j * CG:(j + 1) * CG]
                          ).then_inc(self.stored[j], 16)

    def stored_all(self, act):
        for j in range(self.n):
            act.wait_ge(self.stored[j], 16 * ZG * (2 if self.grp and j < len(GROUPS[0]) else 1))

    def alone(self, grp):
        self.at(grp)
        with self.m.nc.Block() as block:
            block.sync(self.sync)
            block.tensor(self.tensor)

            @block.scalar
            def _(act):
                self.take_gates(act)
                self.take(act, 0, 0, True)
                self.take(act, 1, 1, False)
                with act.Fori(1, ZG // 2) as i:
                    for s in range(2):
                        self.take(act, 2 * i + s, s, False)
                self.stored_all(act)
        self.weights.done(ZG)

    def beside(self, grp):
        self.at(grp)
        return self

    plan = [(1, ZG // 2, "middle"), (ZG // 2, ZG // 2 + 1, "last")]

    def act_slot(self, act, i, r, part):
        if part == "first" and r == 0:
            self.take_gates(act)
        elif part == "first":
            self.take(act, 0, 0, True)
        elif part == "middle":
            self.take(act, 2 * i + (r - 1), (r + 1) % 2, False)
        elif r == 0:
            self.take(act, ZG - 1, 1, False)
            self.stored_all(act)

    def dve_slot(self, dve, i, r, part):
        pass

    def open(self, dve):
        pass

    def end(self):
        self.weights.done(ZG)


def make_rows(m):
    nc, a, out, bank, cols, cdbc = m.nc, m.a, m.out, m.bank, m.cols, m.cdbc
    sem = lambda name: nc.alloc_semaphore("s_" + name)
    dve_row, act_row, mm, chain, m_io = sem("dve_row"), sem("act_row"), sem("mm"), sem("dve"), sem("m_io")
    used = {"chain": 0, "io": 0}

    def run(grp):
        blks = GROUPS[grp]
        n = len(blks)
        T = n * P
        xrow = m.xn[0:MH, :, :].rearrange("p a d -> p (a d)")
        bs, am, tmp = (xrow[:, i * TG:i * TG + T] for i in range(3))
        ig, fg = (m.stage[0:MH, MAXB * CG + g * TG:MAXB * CG + g * TG + T] for g in range(2))
        mx = m.mrows[:, 0:T]
        grow = m.gain[0:MH, :]
        ex = grow[:, 0:3 * TG]
        exs = [ex[:, i * T:(i + 1) * T] for i in range(3)]
        mprev = m.stat[0:MH, 76:76 + n]
        kept = m.stat[0:MH, 72:74]
        cde = grow[:, 3 * TG:3 * TG + n]
        cdd = grow[:, 3 * TG + 16:3 * TG + 16 + n * MH].rearrange("p (b h) -> p b h", b=n)
        onesrow = grow[:, 3 * TG + 40:3 * TG + 40 + P]
        v3 = lambda ap: ap.rearrange("p (b l) -> p b l", b=n)
        io0 = used["io"]
        with nc.Block() as block:
            @block.sync
            def _(sp):
                if grp:
                    with nc.allow_non_contiguous_dma(reason="four numbers"):
                        sp.dma_start(mprev[:, n - 1:n], a["state_mlstm_m"][0].rearrange("o h -> h o")).then_inc(m_io, 16)
                        sp.wait_ge(dve_row, 3 * grp + 3)
                        sp.dma_start(out["m_prompt"][0].rearrange("o h -> h o"), kept[:, 0:1]).then_inc(m_io, 16)
                        sp.dma_start(out["m_sample"][0].rearrange("o h -> h o"), kept[:, 1:2]).then_inc(m_io, 16)
                        sp.wait_ge(m_io, 48)

            @block.tensor
            def _(pe):
                pe.wait_ge(dve_row, 3 * grp + 3)
                for j in range(n):
                    for q, src in enumerate([am] + exs):
                        c = (j * 4 + q) * MH
                        pe.transpose(bank(5)[:, c:c + MH], src[:, j * P:(j + 1) * P], m.ident[0:MH, 0:MH])
                pe.matmul(bank(6)[:, 0:n * MH], onesrow, cdd, start=True, stop=True).then_inc(mm, 1)

            @block.scalar
            def _(act):
                act.wait_ge(dve_row, 3 * grp + 1)
                act.activation(tmp, tmp, ACT.Exp).then_inc(act_row, 1)
                act.wait_ge(act_row, 4 * grp + 1)
                act.activation(tmp, tmp, ACT.Ln, bias=1.0).then_inc(act_row, 1)
                act.wait_ge(dve_row, 3 * grp + 2)
                act.activation(ex[:, 0:3 * T], ex[:, 0:3 * T], ACT.Exp).then_inc(act_row, 1)
                act.activation(cde, cde, ACT.Exp).then_inc(act_row, 1)

            @block.vector
            def _(dve):
                ch = Chain(dve, chain)
                ch.n = used["chain"]
                do = ch.then_wait
                do(dve.memset(onesrow, 1.0))
                if grp == 0:
                    do(dve.memset(mprev[:, 0:1], 0.0))
                else:
                    do(dve.tensor_copy(mprev[:, 0:1], kept[:, 0:1]))
                    dve.wait_ge(m_io, 16)
                dve.scalar_tensor_tensor(out=tmp, in0=fg, scalar=-1.0, in1=fg, op0=ALU.mult, op1=ALU.min).then_inc(dve_row, 1)
                do(dve.tensor_scalar(fg, fg, 0.0, None, ALU.min))
                dve.wait_ge(act_row, 4 * grp + 2)
                do(dve.tensor_tensor(fg, fg, tmp, ALU.subtract))
                if grp:
                    do(dve.memset(fg[:, T - SAMPLE:T], 0.0))
                for j in range(n):
                    do(dve.tensor_tensor_scan(bs[:, j * P:(j + 1) * P], fg[:, j * P:(j + 1) * P],
                                              fg[:, j * P:(j + 1) * P], 0.0, ALU.add, ALU.bypass))
                do(dve.tensor_tensor(am, ig, bs, ALU.subtract))
                if grp:
                    do(dve.memset(am[:, T - SAMPLE:T], -FAR))
                for j in range(n):
                    am_b, mx_b = am[:, j * P:(j + 1) * P], mx[:, j * P:(j + 1) * P]
                    do(dve.tensor_tensor_scan(mx_b, am_b, am_b, mprev[:, j:j + 1], ALU.max, ALU.bypass))
                    to = [kept[:, 1:2]] if blks[j] == SB else [kept[:, 0:1]]
                    if blks[j] != SB and j + 1 < n and blks[j + 1] != SB:
                        to.append(mprev[:, j + 1:j + 2])
                    for dst in to:
                        do(dve.tensor_tensor(dst, bs[:, (j + 1) * P - 1:(j + 1) * P], mx[:, (j + 1) * P - 1:(j + 1) * P], ALU.add))
                last = v3(mx)[:, :, P - 1:P]
                prev = mprev.rearrange("p (b o) -> p b o", o=1)
                do(dve.tensor_tensor(v3(exs[0]), prev.to_broadcast([MH, n, P]), v3(mx), ALU.subtract))
                do(dve.scalar_tensor_tensor(out=exs[1], in0=bs, scalar=-1.0, in1=mx, op0=ALU.mult, op1=ALU.subtract))
                do(dve.tensor_tensor(v3(exs[2]), v3(am), last.to_broadcast([MH, n, P]), ALU.subtract))
                do(dve.tensor_tensor(cde.rearrange("p (b o) -> p b o", o=1), prev, last, ALU.subtract))
                dve.sem_inc(dve_row, 1)
                dve.wait_ge(act_row, 4 * grp + 4)
                for hh in range(MH):
                    do(dve.tensor_scalar(cdd[:, :, hh], cde, m.ident[0:MH, hh:hh + 1], None, ALU.mult))
                dve.sem_inc(dve_row, 1)
                dve.wait_ge(mm, grp + 1)
                do(dve.tensor_copy(cols[:, 0:n, :, :].rearrange("p b q h -> p (b q h)"), bank(5)[:, 0:n * 4 * MH]))
                do(dve.tensor_scalar(cols[:, 0:n, 3, :], cols[:, 0:n, 3, :], MK ** -0.5, None, ALU.mult))
                do(dve.tensor_copy(cdbc[:, 0:n, :].rearrange("p b h -> p (b h)"), bank(6)[:, 0:n * MH]))
                used["chain"] = ch.n
    return run


def make_mixers(m):
    nc, a, out, bank, zd = m.nc, m.a, m.out, m.bank, m.zd
    aT, far, ident, cols, cdbc, mrows, gain, xn, stage, stat = (
        m.aT, m.far, m.ident, m.cols, m.cdbc, m.mrows, m.gain, m.xn, m.stage, m.stat)
    with ExitStack() as s:
        sem = lambda name: nc.alloc_semaphore("m_" + name)
        room = {"h": (m.h[1][:, :, :].rearrange("p b d -> p (b d)"), 0), "w": (m.W[:, :, :].rearrange("p k c -> p (k c)"), 0)}

        def carve(of, n, *dims):
            v, at = room[of]
            room[of] = (v, at + n)
            assert at + n <= v.shape[1]
            v = v[:, at:at + n]
            return v.rearrange("p (a b) -> p a b", a=dims[0]) if dims else v
        zb = [m.ring[:, i * ZC:(i + 1) * ZC] for i in range(2)]
        qkT = carve("h", 24 * P, 24, P)
        rk = carve("h", 2 * RW)
        tv = carve("w", 2 * RW)
        sT = carve("h", RW, RH, P)
        kdec = xn[:, 0, 0:RW].rearrange("p (h d) -> p h d", h=RH)
        dw = xn[:, 0, RW:RW + 512]
        smT = xn[:, 0, RW + 512:2 * RW].rearrange("p (h l) -> p h l", h=MH)
        obuf = xn[:, 1, :]
        gateb = stage[:, 0:2 * RW]
        wk = stage[:, 2 * RW:2 * RW + 512].rearrange("p (h d) -> p h d", h=MH)
        tv2 = m.ring[:, 2 * ZC:2 * ZC + 2 * RW]
        vext = carve("w", MH * (MV + 1), MH, MV + 1)
        S = carve("w", RW, RH, RD)
        Sd = carve("w", RW, RH, RD)
        Cx = m.Cx
        Cd = carve("w", MH * (MV + 1), MH, MV + 1)
        dec = carve("w", RH * P + 3 * RH)
        rope = carve("w", MAXB * RD, MAXB, RD)
        st = stat
        half = RD // 2

        const_in, st_in, z_in = sem("const"), sem("state_in"), [sem("z0"), sem("z1")]
        rot_v, rot_p, tq, te = sem("rot_v"), sem("rot_p"), sem("turned"), sem("turned_copied")
        qd_done, kd_done, wk_done, vx_done = sem("qdec"), sem("kdec"), sem("wkey"), sem("vext")
        pmb, mb_read, dwx, dwe = sem("maxima"), sem("maxima_read"), sem("dw_exponents"), sem("dw")
        ps_r, ps_m, s_r, s_m = sem("ps_ret"), sem("ps_ml"), sem("scores_ret"), sem("scores_ml")
        pu_r, pu_m, sd, cd = sem("upd_ret"), sem("upd_ml"), sem("s_decayed"), sem("c_decayed")
        su, cu = sem("s_updated"), sem("c_updated")
        po_r, po_m, po_i = sem("out_ret"), sem("out_ml"), sem("out_inter")
        ne, nr, ni = sem("inter_scaled"), sem("ret_read"), sem("num_read")
        sg, gg = sem("gates_sig"), sem("gates_gain")
        sq, rts, msr, mixd = sem("squares"), sem("roots"), sem("means"), sem("mixed")
        pt, ptc = sem("mix_turned"), sem("mix_copied")
        st_out, reset = sem("state_out"), sem("state_reset")
        ch_v, ch_p = sem("dve"), sem("pool")
        dec_in = sem("dec_in")
        qk16 = lambda z: z[:, 0:2 * RW].rearrange("p (h t e) -> p h t e", h=2 * RH, t=2)

        n_pool, n_dve = 7, 26

        def cs(j, q):
            return rope[:, j:j + 1, q * half:(q + 1) * half].to_broadcast([P, 2 * RH, half])

        vx_one, ptv, qi, iq = sem("vext_one"), sem("mix_copied_v"), sem("ret_inter"), sem("ret_inter_scaled")

        def mix_copy(copy, q, j, sample, done):
            src = bank(2 + q).rearrange("p (k l) -> p k l", k=4)
            to = aT[:, 4 * q:4 * q + 4, j * P:(j + 1) * P]
            if sample:
                copy(to[:, :, 0:SAMPLE], src[:, :, 0:SAMPLE])
                copy(to[:, :, SAMPLE:P], src[:, :, 0:SAMPLE]).then_inc(done, 1)
            else:
                copy(to, src).then_inc(done, 1)

        def z_wait(eng, t):
            eng.wait_ge(z_in[t % 2], 16 * (t // 2 + 1))

        def run(grp):
            blks = [(sum(map(len, GROUPS[:grp])) + j, j, b, b == SB) for j, b in enumerate(GROUPS[grp])]

            def blocks(eng, body):
                for t, j, b, sample in blks:
                    body(t, j, t % 2, sample)
            with nc.Block() as block:
                stage_of(block, grp, blks, blocks)

        def stage_of(block, grp, blks, blocks):
            @block.sync
            def _(sp):
                t0 = blks[0][0]
                for t, j, b, sample in blks[:2]:
                    sp.dma_start(zb[t % 2], zd[b]).then_inc(z_in[t % 2], 16)
                sp.dma_start(rope[:, 0:len(blks), :].rearrange("p b r -> p (b r)"),
                             a["c_rope"][:, t0 * RD:(t0 + len(blks)) * RD]).then_inc(const_in, 16)
                sp.dma_start(gain[:, 0:RW], a["g_ret"][0:1, :].to_broadcast([P, RW])).then_inc(const_in, 16)
                sp.dma_start(gain[:, RW:], a["g_mlstm"][0:1, :].to_broadcast([P, MW])).then_inc(const_in, 16)
                sp.dma_start(dec, a["c_decay"][0]).then_inc(dec_in, 16)
                cx_all = Cx[:, :, :].rearrange("p h v -> p (h v)")
                s_all = S.rearrange("p h v -> p (h v)")
                if grp == 0:
                    sp.wait_ge(su, 2)
                    sp.wait_ge(cu, 2)
                    sp.dma_start(m.s_keep, s_all).then_inc(st_out, 16)
                    sp.dma_start(m.c_keep, cx_all).then_inc(st_out, 16)
                    sp.wait_ge(st_out, 32)
                    return
                sp.dma_start(s_all, m.s_keep).then_inc(st_in, 16)
                sp.dma_start(cx_all, m.c_keep).then_inc(st_in, 16)
                sp.wait_ge(pt, 4 * 3)
                sp.dma_start(zb[0], zd[SB]).then_inc(z_in[0], 16)

                def states(tag):
                    sp.dma_start(out["ret_" + tag][0, 0].rearrange("h k v -> k h v"), S).then_inc(st_out, 16)
                    sp.dma_start(out["C_" + tag][0, 0].rearrange("h k v -> k h v"), Cx[:, :, 0:MV]).then_inc(st_out, 16)
                    with nc.allow_non_contiguous_dma(reason="one normaliser column"):
                        sp.dma_start(out["n_" + tag][0, 0].rearrange("h k -> k h"), Cx[:, :, MV]).then_inc(st_out, 16)
                sp.wait_ge(su, 4)
                sp.wait_ge(cu, 4)
                states("prompt")
                sp.wait_ge(s_r, 4)
                sp.wait_ge(kd_done, 4)
                sp.wait_ge(sd, 4)
                sp.wait_ge(iq, 4)
                sp.dma_start(dec, a["c_decay"][1]).then_inc(dec_in, 16)
                sp.wait_ge(st_out, 32 + 48)
                sp.wait_ge(po_i, 4)
                sp.dma_start(S, a["state_ret"][0, 0].rearrange("h k v -> k h v")).then_inc(st_in, 16)
                sp.dma_start(Cx[:, :, 0:MV], a["state_mlstm_C"][0, 0].rearrange("h k v -> k h v")).then_inc(st_in, 16)
                with nc.allow_non_contiguous_dma(reason="one normaliser column"):
                    sp.dma_start(Cx[:, :, MV], a["state_mlstm_n"][0, 0].rearrange("h k -> k h")).then_inc(st_in, 16)
                sp.wait_ge(su, NB)
                sp.wait_ge(cu, NB)
                states("sample")
                sp.wait_ge(st_out, 32 + 96)

            def state_wait(eng, t):
                if t == 0:
                    eng.wait_ge(reset, 2)
                elif t == 2:
                    eng.wait_ge(st_in, 32)
                elif t == 4:
                    eng.wait_ge(st_in, 32 + 48)
                else:
                    eng.wait_ge(su, t)
                    eng.wait_ge(cu, t)

            def dec_wait(eng, t):
                eng.wait_ge(dec_in, 16 * (1 if t < 2 else 2 if t < 4 else 3))

            @block.gpsimd
            def _(pool):
                ch = Chain(pool, ch_p)
                pool.wait_ge(const_in, 48 * (grp + 1))

                def body(t, j, r, sample):
                    ch.n, ch.off = 0, t * n_pool
                    do = ch.then_wait
                    z_wait(pool, t)
                    x = qk16(zb[r])
                    if t:
                        pool.wait_ge(tq, 6 * t)
                        pool.wait_ge(msr, t)
                        pool.wait_ge(kd_done, t)
                    t1 = tv2[:, 0:RW].rearrange("p (h e) -> p h e", e=half)
                    t2 = tv2[:, RW:].rearrange("p (h e) -> p h e", e=half)
                    do(pool.tensor_tensor(t1, x[:, :, 0, :], cs(j, 1), ALU.mult))
                    do(pool.tensor_tensor(t2, x[:, :, 1, :], cs(j, 0), ALU.mult))
                    pool.tensor_tensor(qk16(rk)[:, :, 1, :], t1, t2, ALU.add).then_inc(rot_p, 1)
                    pool.wait_ge(rot_p, t + 1)
                    pool.wait_ge(rot_v, t + 1)
                    dec_wait(pool, t)
                    if t:
                        pool.wait_ge(pu_r, t)
                        pool.wait_ge(pu_m, t)
                    kd = dec[:, RH * P:RH * P + RH].rearrange("p (h o) -> p h o", o=1)
                    pool.tensor_tensor(kdec, rk[:, RW:].rearrange("p (h d) -> p h d", h=RH),
                                       kd.to_broadcast([P, RH, RD]), ALU.mult).then_inc(kd_done, 1)
                    wc = cols[:, j, 3, :].rearrange("p (h o) -> p h o", o=1)
                    pool.tensor_tensor(wk, zb[r][:, Z_MK:Z_MV].rearrange("p (h d) -> p h d", h=MH),
                                       wc.to_broadcast([P, MH, MK]), ALU.mult).then_inc(wk_done, 1)
                    state_wait(pool, t)
                    gl = dec[:, RH * P + RH:RH * P + 2 * RH].rearrange("p (h o) -> p h o", o=1)
                    pool.tensor_tensor(Sd, S, gl.to_broadcast([P, RH, RD]), ALU.mult).then_inc(sd, 1)
                    cb = cdbc[:, j, :].rearrange("p (h o) -> p h o", o=1)
                    pool.tensor_tensor(Cd, Cx[:, :, :], cb.to_broadcast([P, MH, MV + 1]), ALU.mult).then_inc(cd, 1)
                    pool.wait_ge(sg, t + 1)
                    do(pool.tensor_tensor(gateb[:, 0:RW], gateb[:, 0:RW], zb[r][:, Z_RG:Z_RG + RW], ALU.mult))
                    pool.tensor_tensor(gateb, gateb, gain[:, :], ALU.mult).then_inc(gg, 1)
                    assert ch.n <= n_pool
                    pool.sem_inc(ch_p, n_pool - ch.n)
                blocks(pool, body)

            @block.scalar
            def _(act):
                def body(t, j, r, sample):
                    z_wait(act, t)
                    if t:
                        act.wait_ge(mixd, 2 * t)
                    act.activation(gateb[:, 0:RW], zb[r][:, Z_RG:Z_RG + RW], ACT.Sigmoid)
                    act.activation(gateb[:, RW:], zb[r][:, Z_MO:Z_MO + MW], ACT.Sigmoid).then_inc(sg, 1)
                    if t:
                        act.wait_ge(po_m, t)
                        act.wait_ge(pu_m, t)
                    act.copy(vext[:, :, 0:MV], zb[r][:, Z_MV:Z_MO].rearrange("p (h v) -> p h v", h=MH)).then_inc(vx_done, 1)
                    if t:
                        act.wait_ge(po_i, t)
                    for q in range(6):
                        act.wait_ge(tq, 6 * t + q + 1)
                        act.copy(qkT[:, 4 * q:4 * q + 4, :], bank(q).rearrange("p (k l) -> p k l", k=4)).then_inc(te, 1)
                    act.wait_ge(dwx, t + 1)
                    act.activation(dw, dw, ACT.Exp, scale=-1.0).then_inc(dwe, 1)
                    act.wait_ge(po_i, t + 1)
                    for hh in range(MH):
                        ins = act.activation(tv[:, hh * MV:(hh + 1) * MV], bank(0, 1024, 2)[:, hh * MV:(hh + 1) * MV],
                                           ACT.Identity, scale=cols[:, j, 1, hh:hh + 1])
                    ins.then_inc(ne, 1)
                    act.wait_ge(rot_p, t + 1)
                    for q in range(2):
                        act.wait_ge(nr if q == 0 else ni, t + 1)
                        act.activation(tv2[:, q * RW:(q + 1) * RW], obuf[:, q * RW:(q + 1) * RW], ACT.Square).then_inc(sq, 1)
                    act.wait_ge(msr, t + 1)
                    act.activation(st[:, 12:24], st[:, 0:12], ACT.Sqrt).then_inc(rts, 1)
                    for q in range(2):
                        act.wait_ge(pt, 4 * t + (q + 1))
                        mix_copy(act.copy, q, j, sample, ptc)
                blocks(act, body)

            @block.tensor
            def _(pe):
                def body(t, j, r, sample):
                    z = zb[r]
                    z_wait(pe, t)
                    pe.wait_ge(rot_v, t + 1)
                    pe.wait_ge(rot_p, t + 1)
                    if t:
                        pe.wait_ge(ptc, 2 * t)
                        pe.wait_ge(ptv, 2 * t)
                    for q in range(6):
                        for i in range(4):
                            n = 4 * q + i
                            src = (rk[:, n * P:(n + 1) * P] if n < 2 * RH else
                                   z[:, Z_MQ + (n - 2 * RH) * P:Z_MQ + (n - 2 * RH + 1) * P])
                            ins = pe.transpose(bank(q)[:, i * P:(i + 1) * P], src, ident)
                        ins.then_inc(tq, 1)
                    if t:
                        pe.wait_ge(cu, t)
                        pe.wait_ge(ni, t)
                    for hh in range(MH):
                        ins = pe.matmul(bank(6)[:, hh * P:(hh + 1) * P], ident[0:MH, hh:hh + 1].to_broadcast([MH, P]),
                                        mrows[:, j * P:(j + 1) * P], start=True, stop=True)
                    ins.then_inc(pmb, 1)
                    pe.wait_ge(te, 6 * t + 4)
                    for hh in range(RH):
                        ins = pe.matmul(bank(0, 1024, 2)[:, hh * P:(hh + 1) * P], qkT[:, RH + hh, :], qkT[:, hh, :],
                                        start=True, stop=True)
                    ins.then_inc(ps_r, 1)
                    pe.wait_ge(te, 6 * t + 6)
                    for hh in range(MH):
                        ins = pe.matmul(bank(2)[:, hh * P:(hh + 1) * P], qkT[:, 20 + hh, :], qkT[:, 16 + hh, :],
                                        start=True, stop=True)
                    ins.then_inc(ps_m, 1)
                    state_wait(pe, t)
                    for hh in range(RH):
                        ins = pe.matmul(bank(3, 1024, 2)[:, hh * RD:(hh + 1) * RD], qkT[:, hh, :], S[:, hh, :],
                                        start=True, stop=True)
                    ins.then_inc(qi, 1)
                    pe.wait_ge(kd_done, t + 1)
                    pe.wait_ge(iq, t + 1)
                    for hh in range(RH):
                        ins = pe.matmul(bank(3, 1024, 2)[:, hh * RD:(hh + 1) * RD], kdec[:, hh, :],
                                      z[:, Z_RV + hh * RD:Z_RV + (hh + 1) * RD], start=True, stop=True)
                    ins.then_inc(pu_r, 1)
                    pe.wait_ge(wk_done, t + 1)
                    pe.wait_ge(vx_done, t + 1)
                    pe.wait_ge(vx_one, grp + 1)
                    pe.wait_ge(mb_read, t + 1)
                    for hh in range(MH):
                        pe.matmul(bank(5, 1024, 2)[:, hh * MV:(hh + 1) * MV], wk[:, hh, :], vext[:, hh, 0:MV],
                                  start=True, stop=True)
                        ins = pe.matmul(bank(7)[:, 8 + hh:9 + hh], wk[:, hh, :], vext[:, hh, MV:MV + 1],
                                      start=True, stop=True)
                    ins.then_inc(pu_m, 1)
                    pe.wait_ge(s_r, t + 1)
                    for hh in range(RH):
                        ins = pe.matmul(bank(0, 1024, 2)[:, hh * RD:(hh + 1) * RD], sT[:, hh, :],
                                        z[:, Z_RV + hh * RD:Z_RV + (hh + 1) * RD], start=True, stop=True)
                    ins.then_inc(po_r, 1)
                    pe.wait_ge(s_m, t + 1)
                    pe.wait_ge(su, t + 1)
                    for hh in range(MH):
                        pe.matmul(bank(2, 1024, 2)[:, hh * MV:(hh + 1) * MV], smT[:, hh, :], vext[:, hh, 0:MV],
                                  start=True, stop=True)
                        ins = pe.matmul(bank(7)[:, hh:hh + 1], smT[:, hh, :], vext[:, hh, MV:MV + 1], start=True, stop=True)
                    ins.then_inc(po_m, 1)
                    pe.wait_ge(nr, t + 1)
                    for hh in range(MH):
                        pe.matmul(bank(0, 1024, 2)[:, hh * MV:(hh + 1) * MV], qkT[:, 16 + hh, :], Cx[:, hh, 0:MV],
                                  start=True, stop=True)
                        ins = pe.matmul(bank(7)[:, 4 + hh:5 + hh], qkT[:, 16 + hh, :], Cx[:, hh, MV:MV + 1],
                                      start=True, stop=True)
                    ins.then_inc(po_i, 1)
                    pe.wait_ge(ni, t + 1)
                    pe.wait_ge(cu, t + 1)
                    for q in range(4):
                        pe.wait_ge(mixd, 2 * t + (1 if q < 2 else 2))
                        for i in range(4):
                            n = 4 * q + i
                            ins = pe.transpose(bank(2 + q)[:, i * P:(i + 1) * P], obuf[:, n * P:(n + 1) * P], ident)
                        ins.then_inc(pt, 1)
                blocks(pe, body)

            @block.vector
            def _(dve):
                ch = Chain(dve, ch_v)
                if grp == 0:
                    dve.memset(S, 0.0).then_inc(reset, 1)
                    dve.memset(Cx[:, :, :], 0.0).then_inc(reset, 1)
                dve.memset(vext[:, :, MV:MV + 1], 1.0).then_inc(vx_one, 1)
                dve.wait_ge(const_in, 48 * (grp + 1))

                def body(t, j, r, sample):
                    ch.n, ch.off = 0, t * n_dve
                    do = ch.then_wait
                    z_wait(dve, t)
                    x = qk16(zb[r])
                    t1 = tv[:, 0:RW].rearrange("p (h e) -> p h e", e=half)
                    t2 = tv[:, RW:].rearrange("p (h e) -> p h e", e=half)
                    do(dve.tensor_tensor(t1, x[:, :, 0, :], cs(j, 0), ALU.mult))
                    do(dve.tensor_tensor(t2, x[:, :, 1, :], cs(j, 1), ALU.mult))
                    if t:
                        dve.wait_ge(tq, 6 * t)
                        dve.wait_ge(kd_done, t)
                    dve.tensor_tensor(qk16(rk)[:, :, 0, :], t1, t2, ALU.subtract).then_inc(rot_v, 1)
                    dve.wait_ge(pmb, t + 1)
                    if t:
                        dve.wait_ge(s_m, t)
                    for hh in range(MH):
                        ins = dve.scalar_tensor_tensor(out=dw[:, hh * P:(hh + 1) * P], in0=bank(6)[:, hh * P:(hh + 1) * P],
                                                     scalar=cols[:, j, 0, hh:hh + 1], in1=far,
                                                     op0=ALU.subtract, op1=ALU.max)
                        if hh < MH - 1:
                            do(ins)
                    ins.then_inc(dwx, 1)
                    dve.wait_ge(dwx, t + 1)
                    dve.sem_inc(mb_read, 1)
                    dve.wait_ge(ps_r, t + 1)
                    dec_wait(dve, t)
                    dve.tensor_tensor(sT.rearrange("p h l -> p (h l)"), bank(0, 1024, 2), dec[:, 0:RH * P], ALU.mult).then_inc(s_r, 1)
                    dve.wait_ge(qi, t + 1)
                    qd = dec[:, RH * P + 2 * RH:].rearrange("p (h o) -> p h o", o=1)
                    dve.tensor_tensor(tv[:, 0:RW].rearrange("p (h v) -> p h v", h=RH),
                                      bank(3, 1024, 2).rearrange("p (h v) -> p h v", h=RH),
                                      qd.to_broadcast([P, RH, RD]), ALU.mult).then_inc(iq, 1)
                    dve.wait_ge(ps_m, t + 1)
                    dve.wait_ge(dwe, t + 1)
                    dve.scalar_tensor_tensor(out=smT.rearrange("p h l -> p (h l)"), in0=bank(2), scalar=MK ** -0.5, in1=dw,
                                             op0=ALU.mult, op1=ALU.mult).then_inc(s_m, 1)
                    dve.wait_ge(po_r, t + 1)
                    dve.wait_ge(sd, t + 1)
                    dve.wait_ge(pu_r, t + 1)
                    dve.tensor_tensor(S.rearrange("p h v -> p (h v)"), Sd.rearrange("p h v -> p (h v)"),
                                      bank(3, 1024, 2), ALU.add).then_inc(su, 1)
                    dve.wait_ge(iq, t + 1)
                    if t:
                        dve.wait_ge(pt, 4 * t)
                    dve.tensor_tensor(obuf[:, 0:RW], bank(0, 1024, 2), tv[:, 0:RW], ALU.add).then_inc(nr, 1)
                    dve.wait_ge(po_i, t + 1)
                    dve.wait_ge(po_m, t + 1)
                    do(dve.tensor_tensor(st[:, 24:28], bank(7)[:, 4:8], cols[:, j, 1, :], ALU.mult))
                    do(dve.tensor_tensor(st[:, 28:32], bank(7)[:, 0:4], st[:, 24:28], ALU.add))
                    do(dve.scalar_tensor_tensor(out=st[:, 32:36], in0=st[:, 28:32], scalar=-1.0, in1=st[:, 28:32],
                                                op0=ALU.mult, op1=ALU.max))
                    do(dve.tensor_tensor(st[:, 36:40], st[:, 32:36], cols[:, j, 2, :], ALU.max))
                    do(dve.reciprocal(st[:, 40:44], st[:, 36:40]))
                    dve.wait_ge(ne, t + 1)
                    do(dve.tensor_tensor(tv[:, RW:], bank(2, 1024, 2), tv[:, 0:RW], ALU.add))
                    rd = st[:, 40:44].rearrange("p (h o) -> p h o", o=1)
                    dve.tensor_tensor(obuf[:, RW:].rearrange("p (h v) -> p h v", h=MH),
                                      tv[:, RW:].rearrange("p (h v) -> p h v", h=MH),
                                      rd.to_broadcast([P, MH, MV]), ALU.mult).then_inc(ni, 1)
                    dve.wait_ge(cd, t + 1)
                    do(dve.tensor_tensor(Cx[:, :, 0:MV], Cd[:, :, 0:MV],
                                         bank(5, 1024, 2).rearrange("p (h v) -> p h v", h=MH), ALU.add))
                    dve.tensor_tensor(Cx[:, :, MV], Cd[:, :, MV], bank(7)[:, 8:12], ALU.add).then_inc(cu, 1)
                    dve.wait_ge(sq, 2 * t + 2)
                    do(dve.tensor_reduce(st[:, 44:52], tv2[:, 0:RW].rearrange("p (h v) -> p h v", h=RH), AX_X, ALU.add))
                    do(dve.tensor_reduce(st[:, 52:56], tv2[:, RW:].rearrange("p (h v) -> p h v", h=MH), AX_X, ALU.add))
                    do(dve.tensor_scalar(st[:, 0:8], st[:, 44:52], 1.0 / RD, EPS, ALU.mult, ALU.add))
                    dve.tensor_scalar(st[:, 8:12], st[:, 52:56], 1.0 / MV, EPS, ALU.mult, ALU.add).then_inc(msr, 1)
                    dve.wait_ge(rts, t + 1)
                    do(dve.reciprocal(st[:, 56:68], st[:, 12:24]))
                    dve.wait_ge(gg, t + 1)
                    do(dve.tensor_tensor(obuf[:, 0:RW].rearrange("p (h v) -> p h v", h=RH),
                                         obuf[:, 0:RW].rearrange("p (h v) -> p h v", h=RH),
                                         st[:, 56:64].rearrange("p (h o) -> p h o", o=1).to_broadcast([P, RH, RD]), ALU.mult))
                    dve.tensor_tensor(obuf[:, 0:RW], obuf[:, 0:RW], gateb[:, 0:RW], ALU.mult).then_inc(mixd, 1)
                    do(dve.tensor_tensor(obuf[:, RW:].rearrange("p (h v) -> p h v", h=MH),
                                         obuf[:, RW:].rearrange("p (h v) -> p h v", h=MH),
                                         st[:, 64:68].rearrange("p (h o) -> p h o", o=1).to_broadcast([P, MH, MV]), ALU.mult))
                    dve.tensor_tensor(obuf[:, RW:], obuf[:, RW:], gateb[:, RW:], ALU.mult).then_inc(mixd, 1)
                    for q in range(2, 4):
                        dve.wait_ge(pt, 4 * t + (q + 1))
                        mix_copy(dve.tensor_copy, q, j, sample, ptv)
                    assert ch.n < n_dve, ch.n
                    dve.sem_inc(ch_v, n_dve - ch.n)
                blocks(dve, body)
    return run



class ProjectOut:

    def __init__(self, m, weights):
        self.m, self.weights = m, weights
        self.mm, self.added = m.nc.alloc_semaphore("o_mm"), m.nc.alloc_semaphore("o_added")

    def at(self, grp):
        self.grp, self.n = grp, len(GROUPS[grp])
        self.base = grp * DG * len(GROUPS[0])

    def sync(self, sp):
        self.x_count = self.m.load_x(sp, self.grp)
        self.weights.load(sp, self.m.a["w_out"][0], DG)

    def tensor(self, pe):
        product_groups(pe, self.m.aT, self.weights, self.m.bank, self.n, DG, self.mm, self.added, self.base)

    def add(self, dve, i, s):
        m, n = self.m, self.n
        for j in range(n):
            k = (2 * i + s) * n + (self.base + j + 1)
            dve.wait_ge(self.mm, k)
            hc = m.h[self.grp][:, j, bass.ds((2 * i + s) * CG, CG)]
            dve.tensor_tensor(hc, m.bank(3 * s + j), hc, ALU.add).then_inc(self.added, 1)

    def alone(self, grp):
        self.at(grp)
        with self.m.nc.Block() as block:
            block.sync(self.sync)
            block.tensor(self.tensor)

            @block.vector
            def _(dve):
                dve.wait_ge(self.m.x_in, self.x_count)
                with dve.Fori(0, DG // 2) as i:
                    for s in range(2):
                        self.add(dve, i, s)
        self.weights.done(DG)


class Scores:

    def __init__(self, m, weights):
        self.m, self.weights = m, weights
        sem = lambda name: m.nc.alloc_semaphore("r_" + name)
        spare = m.xn[:, 1, :]
        self.qT = spare[:, 0:4 * TG].rearrange("p (r t) -> p r t", r=4)
        self.sc, self.sc2 = spare[:, 4 * TG:5 * TG], spare[:, 5 * TG:5 * TG + NKEY]
        n = MAXB * HH * TOPK
        m.top, m.topi = (m.stage[:, i * n:(i + 1) * n].rearrange("p (b x k) -> p b x k", b=MAXB, x=HH) for i in range(2))
        self.keys, self.keysT = (m.stage[:, 2 * n + i * 2 * NKEY:2 * n + (i + 1) * 2 * NKEY] for i in range(2))
        self.k_in, self.k_t, self.k_c = sem("keys"), sem("keys_turned"), sem("keys_copied")
        self.qmm, self.qcp, self.smm, self.scp = sem("q_mm"), sem("q_copied"), sem("s_mm"), sem("s_copied")
        self.chain, self.passed = sem("scores_dve"), Gate(m.nc, m.nc.vector, "r_scores_passed")
        self.chain_base = 0

    def at(self, grp):
        self.grp, self.n, self.xb = grp, len(GROUPS[grp]), HH * grp
        self.tail = SB in GROUPS[grp]
        self.fresh = self.n * P - (SAMPLE if self.tail else 0)

    def load_keys(self, sp):
        for i in range(2):
            sp.dma_start(self.keys[:, i * P:(i + 1) * P], self.m.a[f"peer_keys{i + 1}"][0]).then_inc(self.k_in, 16)

    def turn_keys(self, pe):
        pe.wait_ge(self.k_in, 32 * (self.grp + 1))
        for i in range(2):
            ins = pe.transpose(self.m.bank(4)[:, i * P:(i + 1) * P], self.keys[:, i * P:(i + 1) * P], self.m.ident)
        ins.then_inc(self.k_t, 1)
        pe.wait_ge(self.k_c, self.grp + 1)

    def copy_keys(self, act):
        act.wait_ge(self.k_t, self.grp + 1)
        act.copy(self.keysT, self.m.bank(4)[:, 0:2 * P]).then_inc(self.k_c, 1)

    def four(self, pe, g, first, before=0):
        m, xb, fresh = self.m, self.xb, self.fresh
        for q in range(WQ):
            self.weights.wait(pe, g + before, q)
            for c in range(4):
                for k in range(q * KQ, (q + 1) * KQ):
                    ins = pe.matmul(m.bank(c)[:, 0:fresh], self.weights.W[:, k, c * P:(c + 1) * P],
                                    m.aT[:, k, 0:fresh], start=(k == 0), stop=(k == KT - 1))
                if q == WQ - 1:
                    ins.then_inc(self.qmm, 1)
            if q < WQ - 1:
                ins.then_inc(self.weights.used, 1)
        pe.wait_ge(self.qmm, 4 * g + (xb + 4))
        pe.sem_inc(self.weights.used, 1)
        for c in range(4):
            pe.wait_ge(self.qcp, 4 * g + (xb + c + 1))
            if not first:
                pe.wait_ge(self.scp, 4 * g + (xb + c - 3))
            for j in range(self.n):
                ins = pe.matmul(m.bank(4 + c)[:, j * P:(j + 1) * P], self.qT[:, c, j * P:(j + 1) * P],
                                self.keysT[:, (c % 2) * P:(c % 2 + 1) * P], start=True, stop=True)
            ins.then_inc(self.smm, 1)

    def copy_queries(self, act, g, first):
        m, xb, fresh = self.m, self.xb, self.fresh
        for c in range(4):
            act.wait_ge(self.qmm, 4 * g + (xb + c + 1))
            if not first:
                act.wait_ge(self.smm, 4 * g + (xb + c - 3))
            if self.tail:
                act.copy(self.qT[:, c, fresh:self.n * P], m.bank(c)[:, fresh - SAMPLE:fresh])
            act.copy(self.qT[:, c, 0:fresh], m.bank(c)[:, 0:fresh]).then_inc(self.qcp, 1)

    def best_keys(self, dve, g):
        m, n, xb = self.m, self.n, self.xb
        ch = Chain(dve, self.chain)
        steps = 4 * (5 * n + 2)
        ch.off = g * steps + self.chain_base
        for c in range(4):
            dve.wait_ge(self.smm, 4 * g + (xb + c + 1))
            dve.tensor_copy(self.sc[:, 0:n * P], m.bank(4 + c)[:, 0:n * P]).then_inc(self.scp, 1)
            dve.wait_ge(self.scp, 4 * g + (xb + c + 1))
            self.passed.close()
            for j in range(n):
                sixteen(dve, ch, self.passed, m.tv[:, j, :], m.tx[:, j, :], self.sc[:, j * P:(j + 1) * P], self.sc2)
            x = bass.ds(4 * g + c, 1)
            ch.then_wait(dve.tensor_copy(m.top[:, 0:n, x, :].rearrange("p b o k -> p b (o k)"), m.tv[:, 0:n, :]))
            ch.then_wait(dve.tensor_copy(m.topi[:, 0:n, x, :].rearrange("p b o k -> p b (o k)"), m.tx[:, 0:n, :]))
        assert ch.n == steps

    def end(self):
        self.chain_base += DG * 4 * (5 * self.n + 2)

    def alone(self, grp):
        self.at(grp)
        with self.m.nc.Block() as block:
            @block.sync
            def _(sp):
                self.load_keys(sp)
                self.weights.load(sp, self.m.a["w_peer_q"][0], DG)

            @block.tensor
            def _(pe):
                self.turn_keys(pe)
                self.four(pe, 0, grp == 0)
                with pe.Fori(1, DG) as g:
                    self.four(pe, g, False)

            @block.scalar
            def _(act):
                self.copy_keys(act)
                self.copy_queries(act, 0, grp == 0)
                with act.Fori(1, DG) as g:
                    self.copy_queries(act, g, False)

            @block.vector
            def _(dve):
                with dve.Fori(0, DG) as g:
                    self.best_keys(dve, g)
        self.end()
        self.weights.done(DG)


def sixteen(dve, ch, passed, vals, idx, src, spare):
    def do(ins):
        ch.then_wait(ins)
        passed.close()
    do(dve.max(vals[:, 0:8], src))
    do(dve.max_index(idx[:, 0:8], vals[:, 0:8], src))
    do(dve.match_replace(spare, vals[:, 0:8], src, LOWEST))
    do(dve.max(vals[:, 8:16], spare))
    do(dve.max_index(idx[:, 8:16], vals[:, 8:16], spare))


class OutToScores:
    plan = [(1, 3, "out"), (3, 4, "norms"), (4, 5, "norms"), (5, 7, "scores")]

    def __init__(self, m, weights, project_out, scores, grp):
        self.m, self.weights, self.out, self.scores = m, weights, project_out, scores
        self.h, self.n = m.h[grp], len(GROUPS[grp])
        self.spare, self.st = m.xn[:, 1, :], [m.stat[:, 8 + i:9 + i] for i in range(4)]
        (self.squared, self.mean, self.rooted, self.inverted, self.normed, self.turned, self.copied) = (
            m.nc.alloc_semaphore("b_" + x) for x in
            ("squared", "mean", "rooted", "inverted", "normed", "turned", "copied"))
        self.out.at(grp)
        self.scores.at(grp)
        self.adds = self.out.base + DG * self.n

    def sync(self, sp):
        self.scores.load_keys(sp)
        self.out.sync(sp)
        self.weights.load(sp, self.m.a["w_peer_q"][0], DG, DG)

    def tensor(self, pe):
        m = self.m
        self.out.tensor(pe)
        pe.wait_ge(self.out.added, self.adds)
        for j in range(self.n):
            pe.wait_ge(self.normed, j + 1)
            if j:
                pe.wait_ge(self.copied, 4 * j)
            for q in range(4):
                for i in range(4):
                    k = 4 * q + i
                    ins = pe.transpose(m.bank(q)[:, i * P:(i + 1) * P], self.spare[:, k * P:(k + 1) * P], m.ident)
                ins.then_inc(self.turned, 1)
        self.scores.turn_keys(pe)
        pe.wait_ge(self.copied, 4 * self.n)
        with pe.Fori(0, DG) as g:
            self.scores.four(pe, g, False, DG)

    def open(self, dve):
        dve.wait_ge(self.m.x_in, self.out.x_count)

    def act_slot(self, act, i, r, part):
        m = self.m
        j = 2 * (i - 3) + r
        if part == "norms" and j < self.n:
            if j == 0:
                act.wait_ge(self.out.added, self.adds)
            else:
                act.wait_ge(self.turned, 4 * j)
                act.wait_ge(self.mean, j)
                act.wait_ge(self.inverted, j)
            act.activation(self.spare, self.h[:, j, :], ACT.Square, accum_out=self.st[0]).then_inc(self.squared, 1)
            act.wait_ge(self.mean, j + 1)
            act.activation(self.st[2], self.st[1], ACT.Sqrt).then_inc(self.rooted, 1)
            for q in range(4):
                act.wait_ge(self.turned, 4 * j + q + 1)
                act.copy(m.aT[:, 4 * q:4 * q + 4, j * P:(j + 1) * P],
                         m.bank(q).rearrange("p (k l) -> p k l", k=4)).then_inc(self.copied, 1)
        elif part == "norms":
            self.scores.copy_keys(act)
        elif part == "scores":
            self.scores.copy_queries(act, 2 * i + (r - 10), False)

    def dve_slot(self, dve, i, r, part):
        j = 2 * (i - 3) + r
        if part == "out":
            self.out.add(dve, i - 1, r)
        elif part == "norms" and j < self.n:
            dve.wait_ge(self.squared, j + 1)
            dve.tensor_scalar(self.st[1], self.st[0], 1.0 / D, EPS, ALU.mult, ALU.add).then_inc(self.mean, 1)
            dve.wait_ge(self.rooted, j + 1)
            dve.reciprocal(self.st[3], self.st[2]).then_inc(self.inverted, 1)
            dve.wait_ge(self.inverted, j + 1)
            dve.scalar_tensor_tensor(out=self.spare, in0=self.h[:, j, :], scalar=self.st[3], in1=self.m.gain[:, :],
                                     op0=ALU.mult, op1=ALU.mult).then_inc(self.normed, 1)
        elif part == "scores":
            self.scores.best_keys(dve, 2 * i + (r - 10))

    def end(self):
        self.scores.end()
        self.weights.done(2 * DG)


def make_picks(m):
    nc, top, topi, besti, eidx, gate = m.nc, m.top, m.topi, m.besti, m.eidx, m.gate
    sem = lambda name: nc.alloc_semaphore("r_" + name)
    at = [0]

    def carve(n):
        v = m.ring[:, at[0]:at[0] + n]
        at[0] += n
        return v
    hot = carve(NPICK * NC).rearrange("p (k c) -> p k c", c=NC)
    cand, cidx, cand2 = (carve(EH * NC).rearrange("p (h c) -> p h c", h=EH) for _ in range(3))
    best, bestf, sm, ef = (carve(NPICK).rearrange("p (h k) -> p h k", h=EH) for _ in range(4))
    ti = carve(HH * TOPK).rearrange("p (x k) -> p x k", x=HH)
    sums = carve(2 * EH)
    chain, exd, exq, copied = sem("dve"), sem("exp_done"), sem("exp_ready"), sem("picks_copied")
    passed = Gate(nc, nc.vector, "r_passed")
    used = {"chain": 0, "blocks": 0}

    def run(grp):
        n = len(GROUPS[grp])
        b0 = used["blocks"]
        used["blocks"] += n
        with nc.Block() as block:
            @block.scalar
            def _(act):
                for j in range(n):
                    act.wait_ge(exq, b0 + j + 1)
                    act.activation(sm, sm, ACT.Exp).then_inc(exd, 1)

            @block.vector
            def _(dve):
                ch = Chain(dve, chain)
                base = used["chain"]
                n_blk = 150
                with dve.Fori(0, n) as b:
                    ch.n, ch.off = 0, b * n_blk + base
                    do = ch.then_wait
                    tb = top[:, bass.ds(b, 1), :, :].rearrange("p o h k -> p (o h) k").rearrange("p (h t) k -> p h t k", t=2)
                    do(dve.tensor_copy(ti, topi[:, bass.ds(b, 1), :, :].rearrange("p o h k -> p (o h) k")))
                    ib = ti.rearrange("p (h t) k -> p h t k", t=2)
                    do(dve.tensor_scalar(ib[:, :, 0, :], ib[:, :, 0, :], float(NKEY), None, ALU.mult))
                    c0 = 0
                    for j, rows_, w in PAIR_ROWS:
                        for src, dst in ((tb, cand), (ib, cidx)):
                            if rows_ == 1:
                                o = dst[:, :, c0:c0 + w]
                                x1 = src[:, :, 0, j:j + 1].to_broadcast([P, EH, w])
                                x2 = src[:, :, 1, 0:w]
                            else:
                                o = dst[:, :, c0:c0 + rows_ * w].rearrange("p h (n w) -> p h n w", n=rows_)
                                x1 = src[:, :, 0, j:j + rows_].rearrange("p h (n o) -> p h n o", o=1).to_broadcast([P, EH, rows_, w])
                                x2 = src[:, :, 1, 0:w].rearrange("p h (o w) -> p h o w", o=1).to_broadcast([P, EH, rows_, w])
                            do(dve.tensor_tensor(o, x1, x2, ALU.add))
                        c0 += rows_ * w
                    passed.close()
                    for e in range(EH):
                        sixteen(dve, ch, passed, best[:, e, :], besti[:, e, :], cand[:, e, :], cand2[:, e, :])
                    do(dve.tensor_tensor(sm, best, best[:, :, 0:1].to_broadcast([P, EH, TOPK]), ALU.subtract))
                    dve.sem_inc(exq, 1)
                    do(dve.tensor_copy(bestf, besti[:, :, :]))
                    bf = bestf.rearrange("p h (k o) -> p (h k) o", o=1)
                    io = m.iota.rearrange("p (o c) -> p o c", o=1)
                    do(dve.tensor_tensor(hot, bf.to_broadcast([P, NPICK, NC]), io.to_broadcast([P, NPICK, NC]), ALU.is_equal))
                    for e in range(EH):
                        he = hot[:, e * TOPK:(e + 1) * TOPK, :]
                        do(dve.tensor_tensor(he, he, cidx[:, e:e + 1, :].to_broadcast([P, TOPK, NC]), ALU.mult))
                    do(dve.tensor_reduce(ef.rearrange("p h k -> p (h k)"), hot, AX_X, ALU.add))
                    do(dve.tensor_copy(eidx[:, bass.ds(b, 1), :].rearrange("p o k -> p (o k)"),
                                       ef.rearrange("p h k -> p (h k)")))
                    dve.wait_ge(exd, b + (b0 + 1))
                    do(dve.tensor_reduce(sums[:, 0:EH], sm, AX_X, ALU.add))
                    do(dve.reciprocal(sums[:, EH:], sums[:, 0:EH]))
                    do(dve.tensor_tensor(gate[:, bass.ds(b, 1), :].rearrange("p o (h k) -> p (o h) k", k=TOPK), sm,
                                         sums[:, EH:].rearrange("p (h o) -> p h o", o=1).to_broadcast([P, EH, TOPK]), ALU.mult))
                    assert ch.n <= n_blk, ch.n
                    dve.sem_inc(chain, n_blk - ch.n)
                used["chain"] = base + n * n_blk
                if SB in GROUPS[grp]:
                    for v in (eidx, gate):
                        dve.tensor_copy(v[SAMPLE:P, n - 1, 0:NPICK // 2], v[SAMPLE:P, n - 1, NPICK // 2:]).then_inc(copied, 1)
    return run


def make_gather(m):
    nc, a, bank, gain, stat, eidx, gate = m.nc, m.a, m.bank, m.gain, m.stat, m.eidx, m.gate
    sem = lambda name: nc.alloc_semaphore("g_" + name)
    ring = m.ring[:, :].rearrange("p (s d) -> p s d", s=8)
    u_in = [sem(f"u{i}") for i in range(4)]
    v_in = [sem(f"v{i}") for i in range(4)]
    uix, vix, dots, gel, wts = m.uix, m.vix, m.dots, m.gel, m.wts
    cx = m.xn[:, 0, :]
    u_idx, v_idx, u_used, v_used = sem("u_idx"), sem("v_idx"), sem("u_used"), sem("v_used")
    gelud, weighted, c_ready, zeroed, folded = sem("gelu"), sem("weights"), sem("c"), sem("zeroed"), sem("folded")
    squared, rooted, mean, inverted, fmm, g_in = (
        sem("squared"), sem("rooted"), sem("mean"), sem("inverted"), sem("fold_mm"), sem("gain"))
    NG = NPICK // GRP
    u_tab, v_tab = a["peer_u"][0], a["peer_v"][0]
    off = bass.IndirectOffsetOnAxis
    pool_gate = []
    uses = [0]

    def run(block, grp, js, side=None):
        h = m.h[grp]
        t0 = sum(map(len, GROUPS[:grp]))
        todo = [(t0 + j, j, NG // 2 if GROUPS[grp][j] == SB else NG, side if x == 0 else None) for x, j in enumerate(js)]
        uses[0] += 1
        use = uses[0]

        def pairs(eng, groups, sd, body):
            plan = sd.plan if sd else []
            end = plan[-1][1] if plan else 1
            for start, stop, part in plan:
                if stop == start + 1:
                    body(start, sd, part)
                else:
                    with eng.Fori(start, stop) as i:
                        body(i, sd, part)
            if end < groups // 2:
                with eng.Fori(end, groups // 2) as i:
                    body(i, None, "")

        @block.sync
        def _(sp):
            sp.dma_start(gain[:, :], m.row_bcast(a["g_ffn"][0])).then_inc(g_in, 16)
            if side:
                side.sync(sp)

        @block.gpsimd
        def _(pool):
            if not pool_gate:
                pool_gate.append(Gate(nc, pool, "g_passed"))
            passed = pool_gate[0]

            def group(n, r, j, g, first, ix, landed, ready):
                if not first:
                    for i in range(4):
                        pool.wait_ge(landed[i], 32 * n - 32)
                passed.close()
                pool.tensor_copy(ix[:, r, :], eidx[:, j, bass.ds(g * GRP, GRP)]).then_inc(ready, 1)
                pool.wait_ge(ready, n + 1)
                passed.close()

            def row(n, r, x, first, ix, slot, tab, used, landed):
                if not (first and x < 4):
                    pool.wait_ge(used, GRP * n + (x - 3))
                passed.close()
                pool.indirect_dma_start(ring[:, slot + x % 4, :], None, tab, off(ix[:, r, x:x + 1], 0)
                                        ).then_inc(landed[x % 4], 16)

            def u_group(n, r, j, g, first):
                group(n, r, j, g, first, uix, u_in, u_idx)

            def v_group(n, r, j, g, first):
                group(n, r, j, g, first, vix, v_in, v_idx)

            def u_row(n, r, x, first):
                row(n, r, x, first, uix, 0, u_tab, u_used, u_in)

            def v_row(n, r, x, first):
                row(n, r, x, first, vix, 4, v_tab, v_used, v_in)

            for t, j, groups, sd in todo:
                n0, start = t * NG, t == 0
                u_group(n0, 0, j, 0, start)
                for x in range(GRP):
                    u_row(n0, 0, x, start)

                def both(g, ru, rv, first):
                    u_group(n0 + g, ru, j, g, first)
                    v_group(n0 + g - 1, rv, j, g - 1, first)
                    for x in range(GRP):
                        u_row(n0 + g, ru, x, False)
                        v_row(n0 + g - 1, rv, x, first)
                both(1, 1, 0, start)
                with pool.Fori(1, groups // 2) as i:
                    both(2 * i, 0, 1, False)
                    both(2 * i + 1, 1, 0, False)
                v_group(n0 + groups - 1, 1, j, groups - 1, False)
                for x in range(GRP):
                    v_row(n0 + groups - 1, 1, x, False)

        @block.scalar
        def _(act):
            for t, j, groups, sd in todo:
                n0 = t * NG
                if t:
                    act.wait_ge(u_used, NG * GRP * t)
                act.activation(cx, h[:, j, :], ACT.Square, accum_out=stat[:, 0:1]).then_inc(squared, 1)
                act.wait_ge(mean, t + 1)
                act.activation(stat[:, 2:3], stat[:, 1:2], ACT.Sqrt).then_inc(rooted, 1)

                def gelus(n, r, first):
                    act.wait_ge(u_used, GRP * n + GRP)
                    if not first:
                        act.wait_ge(weighted, n - 1)
                    act.activation(gel[:, r, :], dots[:, r, :], ACT.Gelu).then_inc(gelud, 1)

                def pair(i, slots, part, first=False):
                    for r in range(2):
                        gelus(n0 + 2 * i + r, r, first)
                        if slots:
                            slots.act_slot(act, i, r, part)
                pair(0, sd, "first", t == 0)
                pairs(act, groups, sd, pair)

        @block.vector
        def _(dve):
            dve.wait_ge(g_in, 16 * use)
            if side:
                side.open(dve)
            for t, j, groups, sd in todo:
                n0, hb = t * NG, h[:, j, :]
                dve.wait_ge(squared, t + 1)
                dve.tensor_scalar(stat[:, 1:2], stat[:, 0:1], 1.0 / D, EPS, ALU.mult, ALU.add).then_inc(mean, 1)
                dve.wait_ge(rooted, t + 1)
                dve.reciprocal(stat[:, 3:4], stat[:, 2:3]).then_inc(inverted, 1)
                dve.wait_ge(inverted, t + 1)
                dve.scalar_tensor_tensor(out=cx, in0=hb, scalar=stat[:, 3:4], in1=gain[:, :],
                                         op0=ALU.mult, op1=ALU.mult).then_inc(c_ready, 1)
                dve.wait_ge(c_ready, t + 1)
                if groups < NG:
                    dve.memset(h[SAMPLE:P, j, :], 0.0).then_inc(zeroed, 1)
                    dve.wait_ge(zeroed, 1)

                def dot(n, r, x):
                    dve.wait_ge(u_in[x % 4], 32 * n + (16 if x < 4 else 32))
                    row = ring[:, x % 4, :]
                    dve.tensor_tensor_reduce(row, row, cx, 1.0, 0.0, ALU.mult, ALU.add,
                                             dots[:, r, x:x + 1]).then_inc(u_used, 1)

                def weigh(n, r, g):
                    dve.wait_ge(gelud, n + 1)
                    dve.tensor_tensor(wts[:, r, :], gel[:, r, :], gate[:, j, bass.ds(g * GRP, GRP)],
                                      ALU.mult).then_inc(weighted, 1)
                    dve.wait_ge(weighted, n + 1)

                def add(n, r, x):
                    dve.wait_ge(v_in[x % 4], 32 * n + (16 if x < 4 else 32))
                    if not (isinstance(n, int) and n == 0 and x == 0):
                        dve.wait_ge(v_used, GRP * n + x)
                    dve.scalar_tensor_tensor(out=hb, in0=ring[:, 4 + x % 4, :], scalar=wts[:, r, x:x + 1],
                                             in1=hb, op0=ALU.mult, op1=ALU.add).then_inc(v_used, 1)

                def both(g, ru, rv):
                    dot(n0 + g, ru, 0)
                    weigh(n0 + g - 1, rv, g - 1)
                    for x in range(GRP):
                        if x:
                            dot(n0 + g, ru, x)
                        add(n0 + g - 1, rv, x)

                def pair(i, slots, part):
                    for r in range(2):
                        both(2 * i + r, r, 1 - r)
                        if slots:
                            slots.dve_slot(dve, i, r, part)
                for x in range(GRP):
                    dot(n0, 0, x)
                both(1, 1, 0)
                pairs(dve, groups, sd, pair)
                weigh(n0 + groups - 1, 1, groups - 1)
                for x in range(GRP):
                    add(n0 + groups - 1, 1, x)
            if groups < NG:
                dve.wait_ge(fmm, 1)
                dve.tensor_copy(h[:, j, :], bank(0, D, 4)).then_inc(folded, 1)

        @block.tensor
        def _(pe):
            if side:
                side.tensor(pe)
            t, j, groups, _ = todo[-1]
            if groups < NG:
                if side:
                    side.emptied(pe)
                pe.wait_ge(v_used, GRP * (NG * t + groups))
                for q in range(4):
                    ins = pe.matmul(bank(q), m.fold, h[:, j, q * 512:(q + 1) * 512], start=True, stop=True)
                ins.then_inc(fmm, 1)
        if side:
            side.end()
    return run


class Embeddings:
    PK = PLE // P
    plan = [(1, DG // 2 + 1, "groups")]

    def __init__(self, m, weights):
        self.m, self.weights = m, weights
        sem = lambda name: m.nc.alloc_semaphore("x_" + name)
        self.p_in, self.wp_in, self.pt, self.ptc = sem("p_in"), sem("wp_in"), sem("p_turned"), sem("p_copied")
        self.mm, self.taken, self.pj, self.scaled, self.free = (
            sem("mm"), sem("sigmoid"), sem("proj"), sem("scaled"), sem("free"))
        self.p = m.stage[:, 0:MAXB * PLE].rearrange("p (b c) -> p b c", b=MAXB)
        self.pT = m.stage[:, MAXB * PLE:2 * MAXB * PLE].rearrange("p (k t) -> p k t", k=self.PK)
        self.sig = m.stage[:, 2 * MAXB * PLE:2 * MAXB * PLE + 2 * CG].rearrange("p (r c) -> p r c", r=2)
        self.p_loads = 0

    def at(self, grp):
        m = self.m
        self.grp, self.n, self.h = grp, len(GROUPS[grp]), m.h[grp]
        self.base = grp * DG * len(GROUPS[0])
        if grp == 0:
            self.wp = [m.xn[:, 1, :].rearrange("p (a b) -> p a b", b=P), m.aT[:, :, 2 * P:3 * P]]
        else:
            self.wp = [m.ring[:, k * D:(k + 1) * D].rearrange("p (a b) -> p a b", b=P) for k in range(self.PK)]

    def sync(self, sp):
        m = self.m
        for j, b in enumerate(GROUPS[self.grp]):
            if b < SB:
                sp.dma_start(self.p[:, j, :], m.a["p_prompt"][0, 0, b * P:(b + 1) * P, :]).then_inc(self.p_in, 16)
                self.p_loads += 1
            else:
                for c in range(2):
                    sp.dma_start(self.p[c * SAMPLE:(c + 1) * SAMPLE, j, :], m.a["p_sample"][0, 0]).then_inc(self.p_in, 16)
                    self.p_loads += 1
        for k in range(self.PK):
            sp.dma_start(self.wp[k], m.a["w_ple_proj"][0, k * P:(k + 1) * P, :].rearrange("p (a b) -> p a b", b=P)
                         ).then_inc(self.wp_in, 16)
        self.weights.load(sp, m.a["w_ple_gate"][0], DG)

    def tensor(self, pe):
        m, n = self.m, self.n
        pe.wait_ge(self.p_in, 16 * self.p_loads)
        for j in range(n):
            for k in range(self.PK):
                ins = pe.transpose(m.bank(6 + k)[:, j * P:(j + 1) * P], self.p[:, j, k * P:(k + 1) * P], m.ident)
        ins.then_inc(self.pt, 1)
        pe.wait_ge(self.ptc, self.grp + 1)
        pe.wait_ge(self.wp_in, 32 * (self.grp + 1))

        def projection(i, s, first):
            for j in range(n):
                x = s * n + j
                pe.wait_ge(self.free, 2 * n * i + (self.base + x + 1))
                for k in range(self.PK):
                    ins = pe.matmul(m.bank(6 + x % 2), self.pT[:, k, j * P:(j + 1) * P],
                                    self.wp[k][:, bass.ds((2 * i + s) * (CG // P), CG // P), :],
                                    start=(k == 0), stop=(k == self.PK - 1))
                ins.then_inc(self.pj, 1)
        product_groups(pe, m.aT, self.weights, m.bank, n, DG, self.mm, self.taken, self.base, projection)

    def emptied(self, eng):
        eng.wait_ge(self.taken, self.base + DG * self.n)

    def take_p(self, act):
        act.wait_ge(self.pt, self.grp + 1)
        act.copy(self.pT[:, :, 0:self.n * P], self.m.bank(6, 1024, 2).rearrange("p (k c) -> p k c", k=2)[:, :, 0:self.n * P]
                 ).then_inc(self.ptc, 1)

    def sigmoids(self, act, i, s):
        for j in range(self.n):
            x = s * self.n + j
            N = 2 * self.n * i + (self.base + x)
            act.wait_ge(self.mm, N + 1)
            act.wait_ge(self.free, N + 1)
            act.activation(self.sig[:, x % 2, :], self.m.bank(3 * s + j), ACT.Sigmoid).then_inc(self.taken, 1)

    def open(self, dve):
        if self.grp == 0:
            dve.sem_inc(self.free, 2)

    def add(self, dve, i, s):
        for j in range(self.n):
            x = s * self.n + j
            N = 2 * self.n * i + (self.base + x)
            sig = self.sig[:, x % 2, :]
            dve.wait_ge(self.taken, N + 1)
            dve.wait_ge(self.pj, N + 1)
            dve.tensor_tensor(sig, self.m.bank(6 + x % 2), sig, ALU.mult).then_inc(self.scaled, 1)
            dve.wait_ge(self.scaled, N + 1)
            hc = self.h[:, j, bass.ds((2 * i + s) * CG, CG)]
            dve.tensor_tensor(hc, hc, sig, ALU.add).then_inc(self.free, 1)

    def beside(self, grp):
        self.at(grp)
        return self

    def act_slot(self, act, i, r, part):
        if part == "groups":
            self.sigmoids(act, i - 1, r)
        elif r == 0:
            self.take_p(act)

    def dve_slot(self, dve, i, r, part):
        self.add(dve, i - 1, r)

    def end(self):
        self.weights.done(DG)

    def alone(self, grp):
        self.at(grp)
        m, out, xn, gain, stat = self.m, self.m.out, self.m.xn, self.m.gain, self.m.stat
        sem = lambda name: m.nc.alloc_semaphore("y_" + name)
        g_in, squared, mean, rooted, inverted, y_ready = (
            sem("gain"), sem("squared"), sem("mean"), sem("rooted"), sem("inverted"), sem("ready"))
        y_out = [sem("out0"), sem("out1")]
        junk = m.ring[:, 2 * D:3 * D]
        blks = [(t, m.h[g][:, j, :], b, g) for t, (g, j, b) in
                enumerate((g, j, b) for g, blks in enumerate(GROUPS) for j, b in enumerate(blks))]
        with m.nc.Block() as block:
            @block.sync
            def _(sp):
                sp.dma_start(gain[:, :], m.row_bcast(m.a["g_final"])).then_inc(g_in, 16)
                self.sync(sp)
                for t, hb, b, g in blks:
                    sp.wait_ge(y_ready, t + 1)
                    if b < SB:
                        sp.dma_start(out["y_prompt"][0, b * P:(b + 1) * P, :], xn[:, t % 2, :]).then_inc(y_out[t % 2], 16)
                    else:
                        sp.dma_start(out["y_sample"][0], xn[0:SAMPLE, t % 2, :]).then_inc(y_out[t % 2], 16)
                sp.wait_ge(y_out[0], 48)
                sp.wait_ge(y_out[1], 32)

            block.tensor(self.tensor)

            def act_final(act, t, hb):
                if t:
                    act.wait_ge(mean, t)
                act.activation(junk, hb, ACT.Square, accum_out=stat[:, 0:1]).then_inc(squared, 1)
                act.wait_ge(mean, t + 1)
                if t:
                    act.wait_ge(inverted, t)
                act.activation(stat[:, 2:3], stat[:, 1:2], ACT.Sqrt).then_inc(rooted, 1)

            @block.scalar
            def _(act):
                self.take_p(act)
                for t, hb, b, g in blks:
                    if g == 0:
                        act_final(act, t, hb)
                with act.Fori(0, DG // 2) as i:
                    for s in range(2):
                        self.sigmoids(act, i, s)
                act.wait_ge(self.free, 2 + self.base + DG * self.n)
                for t, hb, b, g in blks:
                    if g:
                        act_final(act, t, hb)

            def dve_final(dve, t, hb):
                dve.wait_ge(squared, t + 1)
                dve.tensor_scalar(stat[:, 1:2], stat[:, 0:1], 1.0 / D, EPS, ALU.mult, ALU.add).then_inc(mean, 1)
                dve.wait_ge(rooted, t + 1)
                dve.reciprocal(stat[:, 3:4], stat[:, 2:3]).then_inc(inverted, 1)
                dve.wait_ge(inverted, t + 1)
                if t >= 2:
                    dve.wait_ge(y_out[t % 2], 16 * (t // 2))
                dve.scalar_tensor_tensor(out=xn[:, t % 2, :], in0=hb, scalar=stat[:, 3:4],
                                         in1=gain[:, :], op0=ALU.mult, op1=ALU.mult).then_inc(y_ready, 1)

            @block.vector
            def _(dve):
                dve.wait_ge(g_in, 16)
                for t, hb, b, g in blks:
                    if g == 0:
                        dve_final(dve, t, hb)
                with dve.Fori(0, DG // 2) as i:
                    for s in range(2):
                        self.add(dve, i, s)
                dve.wait_ge(self.free, 2 + self.base + DG * self.n)
                for t, hb, b, g in blks:
                    if g:
                        dve_final(dve, t, hb)
        self.weights.done(DG)


_INS = ["x_prompt", "x_sample", "p_prompt", "p_sample", "state_ret", "state_mlstm_C", "state_mlstm_n", "state_mlstm_m",
        "g_mix", "w_in", "b_gates", "g_ret", "g_mlstm", "w_out", "g_ffn", "w_peer_q", "peer_keys1", "peer_keys2",
        "peer_u", "peer_v", "g_ple", "w_ple_gate", "w_ple_proj", "g_final"]
_OUTS = [("y_prompt", (1, PROMPT, D)), ("y_sample", (1, SAMPLE, D)),
         ("ret_prompt", (1, 1, RH, RD, RD)), ("C_prompt", (1, 1, MH, MK, MV)), ("n_prompt", (1, 1, MH, MK)), ("m_prompt", (1, 1, MH)),
         ("ret_sample", (1, 1, RH, RD, RD)), ("C_sample", (1, 1, MH, MK, MV)), ("n_sample", (1, 1, MH, MK)), ("m_sample", (1, 1, MH))]


def kernel(**inputs):
    import concourse.bacc as bacc
    from concourse.bass_utils import run_bass_kernel_spmd

    nc = bacc.Bacc("TRN2", target_bir_lowering=False, num_devices=1)
    arrays, a, out = {}, {}, {}
    for name, value in [(n, inputs[n]) for n in _INS] + list(constants().items()):
        v = np.ascontiguousarray(value)
        arrays[f"in_{name}"] = v
        a[name] = nc.dram_tensor(f"in_{name}", v.shape, mybir.dt.from_np(v.dtype), kind="ExternalInput").ap()
    for name, shape in _OUTS:
        out[name] = nc.dram_tensor(f"out_{name}", shape, F32, kind="ExternalOutput").ap()
    build(nc, a, out)
    r = run_bass_kernel_spmd(nc, [arrays], core_ids=[0])
    return tuple(r.results[0][f"out_{name}"] for name, _ in _OUTS)
```
